# Optimizing a Trainium2 kernel written in Bass

```python
import math
import jax, jax.numpy as jnp
from jax import lax
import numpy as np

D_MODEL = 2048
BATCH = 1
SEQ = 256
DEPTH = 2

N_A = DEPTH // 2
N_B = DEPTH - N_A
CONV_K = 31
FFN_CONV_K = 3
D_FF = 5632
GROUPS = ((128, 1), (512, 4), (2048, 16))
N_GROUPS = len(GROUPS)
HEADS_PER_GROUP = 8
HEAD_DIM = 128
Q_WIDTH = N_GROUPS * HEADS_PER_GROUP * HEAD_DIM
O_WIDTH = HEADS_PER_GROUP * HEAD_DIM
ROT_DIM = HEAD_DIM // 4
ROPE_THETA = 500000.0
BLK = 128
EPS = 1e-6
NEG = -1e30

kernel_name = "yoco_conformer_dilated_hybrid"

def rms_norm(x, g):
    xf = x.astype(jnp.float32)
    y = xf * lax.rsqrt(jnp.mean(xf * xf, axis=-1, keepdims=True) + EPS)
    return (y * g.astype(jnp.float32)).astype(x.dtype)

def layer_norm(x, g, b):
    xf = x.astype(jnp.float32)
    mu = jnp.mean(xf, axis=-1, keepdims=True)
    var = jnp.mean(jnp.square(xf - mu), axis=-1, keepdims=True)
    y = (xf - mu) * lax.rsqrt(var + EPS)
    return (y * g.astype(jnp.float32) + b.astype(jnp.float32)).astype(x.dtype)

def modulate(x, g, shift, scale):
    return rms_norm(x, g) * (1 + scale[:, None, :]) + shift[:, None, :]

def causal_dwconv(x, w, b):
    k, ch = w.shape
    y = lax.conv_general_dilated(
        x, w[:, None, :].astype(x.dtype), window_strides=(1,), padding=[(k - 1, 0)],
        dimension_numbers=("NWC", "WIO", "NWC"), feature_group_count=ch)
    return y + b

def rope_partial(x, positions):
    inv_freq = ROPE_THETA ** (-jnp.arange(0, ROT_DIM, 2, dtype=jnp.float32) / ROT_DIM)
    ang = positions.astype(jnp.float32)[..., None] * inv_freq
    ang = ang.reshape(ang.shape[:2] + (1,) * (x.ndim - 3) + ang.shape[-1:])
    cos, sin = jnp.cos(ang), jnp.sin(ang)
    xf = x.astype(jnp.float32)
    x1 = xf[..., : ROT_DIM // 2]
    x2 = xf[..., ROT_DIM // 2: ROT_DIM]
    out = jnp.concatenate([x1 * cos - x2 * sin, x2 * cos + x1 * sin, xf[..., ROT_DIM:]], axis=-1)
    return out.astype(x.dtype)

def conformer_conv(h, pw1_w, pw1_b, dw_w, dw_b, ln_g, ln_b, pw2_w, pw2_b):
    u = h @ pw1_w + pw1_b
    a, gt = jnp.split(u, 2, axis=-1)
    u = a * jax.nn.sigmoid(gt)
    u = causal_dwconv(u, dw_w, dw_b)
    u = jax.nn.silu(layer_norm(u, ln_g, ln_b))
    return u @ pw2_w + pw2_b

def conv_ffn(h, up_w, dw_w, dw_b, down_w):
    u = h @ up_w
    gt, val = jnp.split(u, 2, axis=-1)
    gt = causal_dwconv(gt, dw_w, dw_b)
    return (jax.nn.silu(gt) * val) @ down_w

def shared_kv(x, c, kv_mod_w, kv_mod_b, kv_norm_g, w_kv, k_norm_g, positions):
    b, s, _ = x.shape
    m = jax.nn.silu(c) @ kv_mod_w + kv_mod_b
    shift, scale = jnp.split(m, 2, axis=-1)
    h = modulate(x, kv_norm_g, shift, scale)
    kv = (h @ w_kv).reshape(b, s, 2, N_GROUPS, HEADS_PER_GROUP, HEAD_DIM)
    k = rope_partial(rms_norm(kv[:, :, 0], k_norm_g), positions)
    v = kv[:, :, 1]
    return k, v

def dilated_band_attn(q, k, v, span, r):
    b, s, h, dh = q.shape
    chunk = r * BLK
    s_pad = -(-s // chunk) * chunk
    nb = s_pad // chunk
    padw = ((0, 0), (0, s_pad - s), (0, 0), (0, 0))
    split = lambda t: jnp.pad(t, padw).reshape(b, nb, BLK, r, h, dh)
    qb, kb, vb = split(q), split(k), split(v)
    shift_prev = lambda t: jnp.concatenate([jnp.zeros_like(t[:, :1]), t[:, :-1]], axis=1)
    kcat = jnp.concatenate([shift_prev(kb), kb], axis=2)
    vcat = jnp.concatenate([shift_prev(vb), vb], axis=2)
    sc = jnp.einsum("bnqrhd,bnkrhd->bnrhqk", qb, kcat,
                    preferred_element_type=jnp.float32) * (1.0 / math.sqrt(dh))
    qi = jnp.arange(BLK)[:, None]
    kj = jnp.arange(2 * BLK)[None, :]
    dist = qi + BLK - kj
    band = (dist >= 0) & (dist <= span)
    kpos = jnp.arange(nb)[:, None, None] * BLK + kj[None] - BLK
    mask = band[None] & (kpos >= 0)
    sc = jnp.where(mask[None, :, None, None], sc, NEG)
    lse = jax.nn.logsumexp(sc, axis=-1)
    p = jnp.exp(sc - lse[..., None])
    o = jnp.einsum("bnrhqk,bnkrhd->bnqrhd", p.astype(v.dtype), vcat)
    o = o.reshape(b, s_pad, h, dh)[:, :s]
    lse = lse.transpose(0, 1, 4, 2, 3).reshape(b, s_pad, h)[:, :s]
    return o, lse

def dilated_mixture_attn(h, k, v, w_q, q_norm_g, w_o, positions):
    b, s, _ = h.shape
    q = (h @ w_q).reshape(b, s, N_GROUPS, HEADS_PER_GROUP, HEAD_DIM)
    q = rope_partial(rms_norm(q, q_norm_g), positions)
    outs, lses = [], []
    for g, (window, dil) in enumerate(GROUPS):
        o_g, lse_g = dilated_band_attn(q[:, :, g], k[:, :, g], v[:, :, g], window // dil, dil)
        outs.append(o_g)
        lses.append(lse_g)
    alpha = jax.nn.softmax(jnp.stack(lses, axis=0), axis=0)
    o = jnp.einsum("gbsh,gbshd->bshd", alpha, jnp.stack(outs, 0).astype(jnp.float32))
    return o.astype(h.dtype).reshape(b, s, O_WIDTH) @ w_o

def setup_inputs(seed: int = 0) -> dict:
    key = jax.random.key(seed)
    ks = iter(jax.random.split(key, 40))
    D = D_MODEL
    nrm = lambda shape, scale: jax.random.normal(next(ks), shape, jnp.float32) * scale
    gain = lambda shape: 1.0 + nrm(shape, 0.02)
    return {
        "x": nrm((BATCH, SEQ, D), 1.0),
        "c": nrm((BATCH, D), 1.0),
        "positions": jnp.broadcast_to(jnp.arange(SEQ, dtype=jnp.int32)[None], (BATCH, SEQ)),
        "mod_w": nrm((DEPTH, D, 6 * D), 0.5 * D ** -0.5),
        "mod_b": nrm((DEPTH, 6 * D), 0.01),
        "norm_mix_g": gain((DEPTH, D)),
        "norm_ffn_g": gain((DEPTH, D)),
        "conv_pw1_w": nrm((N_A, D, 2 * D), D ** -0.5),
        "conv_pw1_b": nrm((N_A, 2 * D), 0.01),
        "conv_dw_w": nrm((N_A, CONV_K, D), CONV_K ** -0.5),
        "conv_dw_b": nrm((N_A, D), 0.01),
        "conv_ln_g": gain((N_A, D)),
        "conv_ln_b": nrm((N_A, D), 0.01),
        "conv_pw2_w": nrm((N_A, D, D), D ** -0.5),
        "conv_pw2_b": nrm((N_A, D), 0.01),
        "kv_mod_w": nrm((D, 2 * D), 0.5 * D ** -0.5),
        "kv_mod_b": nrm((2 * D,), 0.01),
        "kv_norm_g": gain((D,)),
        "w_kv": nrm((D, 2 * Q_WIDTH), D ** -0.5),
        "k_norm_g": gain((HEAD_DIM,)),
        "w_q": nrm((N_B, D, Q_WIDTH), D ** -0.5),
        "q_norm_g": gain((N_B, HEAD_DIM)),
        "w_o": nrm((N_B, O_WIDTH, D), O_WIDTH ** -0.5),
        "ffn_up_w": nrm((DEPTH, D, 2 * D_FF), D ** -0.5),
        "ffn_dw_w": nrm((DEPTH, FFN_CONV_K, D_FF), FFN_CONV_K ** -0.5),
        "ffn_dw_b": nrm((DEPTH, D_FF), 0.01),
        "ffn_down_w": nrm((DEPTH, D_FF, D), D_FF ** -0.5),
    }

def reference(x, c, positions, mod_w, mod_b, norm_mix_g, norm_ffn_g,
              conv_pw1_w, conv_pw1_b, conv_dw_w, conv_dw_b, conv_ln_g, conv_ln_b,
              conv_pw2_w, conv_pw2_b, kv_mod_w, kv_mod_b, kv_norm_g, w_kv, k_norm_g,
              w_q, q_norm_g, w_o, ffn_up_w, ffn_dw_w, ffn_dw_b, ffn_down_w):
    k_sh = v_sh = None
    for l in range(DEPTH):
        m = jax.nn.silu(c) @ mod_w[l] + mod_b[l]
        sh_m, sc_m, g_m, sh_f, sc_f, g_f = jnp.split(m, 6, axis=-1)
        if l < N_A:
            h = modulate(x, norm_mix_g[l], sh_m, sc_m)
            y = conformer_conv(h, conv_pw1_w[l], conv_pw1_b[l], conv_dw_w[l], conv_dw_b[l],
                               conv_ln_g[l], conv_ln_b[l], conv_pw2_w[l], conv_pw2_b[l])
        else:
            if l == N_A:
                k_sh, v_sh = shared_kv(x, c, kv_mod_w, kv_mod_b, kv_norm_g, w_kv,
                                       k_norm_g, positions)
            j = l - N_A
            h = modulate(x, norm_mix_g[l], sh_m, sc_m)
            y = dilated_mixture_attn(h, k_sh, v_sh, w_q[j], q_norm_g[j], w_o[j], positions)
        x = x + g_m[:, None, :] * y
        h = modulate(x, norm_ffn_g[l], sh_f, sc_f)
        x = x + g_f[:, None, :] * conv_ffn(h, ffn_up_w[l], ffn_dw_w[l], ffn_dw_b[l], ffn_down_w[l])
    return x


_drawn_inputs = setup_inputs


def setup_inputs(seed=0):
    import zlib

    import numpy as np

    out = dict(_drawn_inputs(seed))
    spreads = {}
    factors = {'mod_b': 4.066,
     'norm_mix_g': 8.0,
     'norm_ffn_g': 6.392,
     'conv_pw1_b': 8.0,
     'conv_dw_b': 8.0,
     'conv_ln_g': 8.0,
     'conv_ln_b': 8.0,
     'conv_pw2_b': 8.0,
     'kv_mod_b': 8.0,
     'kv_norm_g': 8.0,
     'k_norm_g': 8.0,
     'q_norm_g': 8.0,
     'ffn_dw_b': 8.0}
    for name, (base, spread) in spreads.items():
        noise = np.random.default_rng([zlib.crc32(name.encode()), seed]).standard_normal(out[name].shape)
        drawn = base * np.exp(spread * noise) if base else spread * noise
        out[name] = __import__('jax').numpy.asarray(drawn.astype(out[name].dtype))
    for name, factor in factors.items():
        out[name] = (out[name] * factor).astype(out[name].dtype)
    return out
```

```python
from contextlib import ExitStack

import numpy as np

import concourse.bass as bass
from concourse import mybir

P = 128
D = 2048
S = 256
TB = S // P
DB = D // P
N = 512
DFF = 5632
FB = DFF // P
CONV_K = 31
FFN_K = 3
GROUPS = ((128, 1), (512, 4), (2048, 16))
NG = len(GROUPS)
HPG = 8
DH = 128
NH = NG * HPG
QW = NH * DH
OW = HPG * DH
ROT = DH // 4
HR = ROT // 2
THETA = 500000.0
EPS = 1e-6
NEG = -1e30
SCALE = 1.0 / float(np.sqrt(DH))

SLOT = 4 * N
PIECE = SLOT // 2
NP_ = 4
NRAW = 4
MSLOT = 2 * N
NMRAW = 4
MOPS = DB

KS = D // P // 4
PAIRS_PW1 = D // N
PAIRS_UP = DFF // N
DGROUPS = FB // 4
SLOTS = {}
CHUNKS = {}
_s = _c = 0
for _name, _chunks, _slots in (
        ("pw1", 2 * PAIRS_PW1, 2 * PAIRS_PW1 * KS), ("pw2", D // N, D // N * KS),
        ("up0", 2 * PAIRS_UP, 2 * PAIRS_UP * KS), ("down0", 4, 4 * DGROUPS),
        ("k", QW // N, QW // N * KS), ("v", QW // N, QW // N * KS), ("q", QW // N, QW // N * KS),
        ("wo", D // N, D // N * (OW // P // 4)),
        ("up1", 2 * PAIRS_UP, 2 * PAIRS_UP * KS), ("down1", 4, 4 * DGROUPS)):
    SLOTS[_name], CHUNKS[_name] = _s, _c
    _s += _slots
    _c += _chunks
NSLOTS, NCHUNKS = _s, _c

MODS = {"head": 0, "pw1": 8, "pw2": 16, "up0": 20, "down0": 31, "v": 41, "q": 47, "up1": 53}
NMODS = 56
MC0, MCKV, MC1 = 0, 6 * DB, 8 * DB

ROWS = {}
_r = 0
for _name, _n in (("c", DB), ("mod_b", 14 * DB), ("mix_g", 2 * DB), ("ffn_g", 2 * DB), ("kv_g", DB),
                  ("pw1_b", 2 * DB), ("dw_b", DB), ("ln_g", DB), ("ln_b", DB), ("pw2_b", DB),
                  ("head_g", 2), ("conv_w", CONV_K * DB), ("ffn_w", 2 * FFN_K * FB), ("ffn_b", 2 * FB)):
    ROWS[_name] = _r
    _r += _n
NROWS = _r
NRB = -(-NROWS // P)

UNITS = {}
_u = 0
for _name, _n in (("table", -(-NRB // 4)), ("head_g", 1), ("norm0", 8), ("pw1", 4 * PAIRS_PW1), ("ln", 2),
                  ("gate0", 4), ("bias0", 4), ("norm1", 8), ("up0", 4 * PAIRS_UP), ("gate1", 4),
                  ("norm2", 8), ("k", 12), ("norm3", 8), ("q", 12), ("attn", 3 * HPG), ("gate2", 4),
                  ("norm4", 8), ("up1", 4 * PAIRS_UP), ("gate3", 4)):
    UNITS[_name] = _u
    _u += _n

AREA = 18432
A_HID, A_CONV, A_GATE = 0, 11264, 12288
A_Y, A_SIG, A_U, A_MU, A_RS, A_YC = 0, 4096, 5120, 6272, 6528, 8192
UPAD = CONV_K - 1
A_KT, A_V, A_QT = 0, 6144, 12288
NORM_AT = [(0, 7168), (0, 7168), (0, 7168), (12288, 16384), (0, 7168)]

ATTN_UNITS = [3 * (j // 2) + (1, 3)[j % 2] for j in range(2 * HPG)]
HO = 40

PI = float(np.pi)
PI_BELOW = 3.1415925
ROUND = 1.5 * 2.0 ** 23
TWO_PI = (6.28125, float(np.round((2 * np.pi - 6.28125) * 2.0 ** 20) / 2.0 ** 20))
TWO_PI += (float(2 * np.pi - TWO_PI[0] - TWO_PI[1]),)


def inv_freq():
    return np.power(np.float32(THETA), -np.arange(0, ROT, 2, dtype=np.float32) / np.float32(ROT)).astype(np.float32)


def build(nc, wstream, mstream, x_in, rows_in, pos_in, out):
    F32, F32R, I32 = mybir.dt.float32, mybir.dt.float32r, mybir.dt.int32
    ALU, ACT, AX = mybir.AluOpType, mybir.ActivationFunctionType, mybir.AxisListType.X

    with ExitStack() as ctx:
        def sb(name, shape, dt=F32):
            return ctx.enter_context(nc.sbuf_tensor(name, shape, dt))

        def pb(name, shape):
            return ctx.enter_context(nc.psum_tensor(name, shape, F32))

        def sem(name):
            return ctx.enter_context(nc.semaphore(name))

        raw = sb("raw", [P, NRAW, SLOT])
        mraw = sb("mraw", [P, NMRAW, MSLOT])
        whi = sb("whi", [P, NP_, PIECE], F32R)
        wlo = sb("wlo", [P, NP_, PIECE], F32R)
        hhi = sb("hhi", [P, DB, S], F32R)
        hlo = sb("hlo", [P, DB, S], F32R)
        x = sb("x", [P, TB, D])
        acc = sb("acc", [P, 2, N])
        stage = sb("stage", [P, 2, TB, N])
        area = sb("area", [P, AREA])
        table = sb("table", [P, NRB * P])
        modcol = sb("modcol", [P, 14 * DB])
        ident = sb("ident", [P, P])
        ones = sb("ones", [P, P])
        headg = sb("headg", [P, 2, DH])
        cs = sb("cs", [P, 2, TB, HR])
        csil = sb("csil", [P, DB])
        nsh = sb("nsh", [P, DB])
        nsc = sb("nsc", [P, DB])
        small = sb("small", [P, 64])
        posi = sb("posi", [P, TB], I32)
        posf = sb("posf", [P, TB])

        psG = [pb(f"psG{i}", [P, TB, N]) for i in range(2)]
        psT = [pb(f"psT{i}", [P, N]) for i in range(3)]
        psM = pb("psM", [P, N])

        raw_full = [sem(f"raw_full{i}") for i in range(NRAW)]
        mod_full = [sem(f"mod_full{i}") for i in range(NMRAW)]
        params_in = sem("params_in")
        x_loaded = sem("x_loaded")
        out_done = sem("out_done")
        const_ready = sem("const_ready")
        hi_ready = sem("hi_ready")
        lo_ready = sem("lo_ready")
        used = sem("used")
        mod_ops = sem("mod_ops")
        mod_summed = sem("mod_summed")
        mod_ready = sem("mod_ready")
        evac = sem("evac")
        tr_done = sem("tr_done")
        tr_free = sem("tr_free")
        csil_ready = sem("csil_ready")
        angle_ready = sem("angle_ready")
        trig_ready = sem("trig_ready")
        x_ready = sem("x_ready")
        ssq_ready = sem("ssq_ready")
        xn_ready = sem("xn_ready")
        hhi_ready = sem("hhi_ready")
        hlo_ready = sem("hlo_ready")
        conv_ready = sem("conv_ready")
        silu_ready = sem("silu_ready")
        diag_ready = sem("diag_ready")
        ln_step = sem("ln_step")
        ln_sq = sem("ln_sq")
        ln_std = sem("ln_std")
        hid_hi = sem("hid_hi")
        hid_lo = sem("hid_lo")
        head_ssq = sem("head_ssq")
        head_std = sem("head_std")
        head_ready = sem("head_ready")
        iota_ready = sem("iota_ready")
        dil_ready = sem("dil_ready")
        mask_ready = sem("mask_ready")
        score_done = sem("score_done")
        score_read = sem("score_read")
        max_ready = sem("max_ready")
        exp_ready = sem("exp_ready")
        prob_ready = sem("prob_ready")
        o_done = sem("o_done")
        o_read = sem("o_read")

        xn_of = [area[:, a:a + TB * D].rearrange("p (t d) -> p t d", t=TB) for a, _ in NORM_AT]
        h32_of = [area[:, b:b + 2 * N].rearrange("p (u b s) -> p u b s", u=2, b=2) for _, b in NORM_AT]
        hidden = area[:, A_HID:A_HID + FB * S].rearrange("p (b s) -> p b s", s=S)
        convb = area[:, A_CONV:A_CONV + 4 * S].rearrange("p (b s) -> p b s", s=S)
        gate = area[:, A_GATE:A_GATE + D]
        yln = area[:, A_Y:A_Y + DB * S].rearrange("p (b s) -> p b s", s=S)
        sigb = area[:, A_SIG:A_SIG + 4 * S].rearrange("p (b s) -> p b s", s=S)
        upad = area[:, A_U:A_U + 4 * (S + UPAD)].rearrange("p (b s) -> p b s", b=4)
        mu = area[:, A_MU:A_MU + S]
        rs = area[:, A_RS:A_RS + S]
        ysq = area[:, A_YC:A_YC + DB * S].rearrange("p (b s) -> p b s", s=S)
        kT = area[:, A_KT:A_KT + NH * S].rearrange("p (n s) -> p n s", s=S)
        vv = area[:, A_V:A_V + TB * QW].rearrange("p (t n) -> p t n", t=TB)
        qT = area[:, A_QT:A_QT + NH * S].rearrange("p (n s) -> p n s", s=S)
        diag = stage[:, 0].rearrange("p t (b c) -> p (t b) c", c=P)
        NKEY = [NG * P, NG * S]
        masks = [stage[:, 0].rearrange("p t n -> p (t n)")[:, 0:NKEY[1]],
                 stage[:, 1].rearrange("p t n -> p (t n)")[:, 0:NKEY[0]]]
        mask1, mask0 = masks
        attn = mraw[:].rearrange("p a b -> p (a b)")
        prob = [attn[:, i * NKEY[1]:(i + 1) * NKEY[1]] for i in range(2)]
        probT = [attn[:, (2 + i) * NKEY[1]:(3 + i) * NKEY[1]].rearrange("p (b q) -> p b q", q=P) for i in range(2)]
        eps_c, ssq, rstd = small[:, 0:1], small[:, 2:4], small[:, 4:6]
        hss, hsd, hrs = small[:, 8:16], small[:, 16:24], small[:, 24:32]
        mx, nmx, den, rden = small[:, 32:34], small[:, 34:36], small[:, 36:38], small[:, 38:40]
        trig = acc[:, 0, 0:8 * TB * HR].rearrange("p (k t f) -> p k t f", k=8, t=TB)

        tbl_in = area[:, 0:NRB * P]

        def col(name, i):
            return table[:, ROWS[name] + i:ROWS[name] + i + 1]

        def cols(name, i=0, n=DB):
            return table[:, ROWS[name] + i:ROWS[name] + i + n]

        NORMS = [("mix_g", 0, MC0, MC0 + DB, 8, 0),
                 ("ffn_g", 0, MC0 + 3 * DB, MC0 + 4 * DB, 20, SLOTS["up0"]),
                 ("kv_g", 0, MCKV, MCKV + DB, 32, SLOTS["k"]),
                 ("mix_g", DB, MC1, MC1 + DB, 40, SLOTS["q"]),
                 ("ffn_g", DB, MC1 + 3 * DB, MC1 + 4 * DB, 52, SLOTS["up1"])]
        HB = [0, 16, 24, 32, 48]
        HL = [0, 16, 24, 32, 40]
        LNH = 8
        X_STAGE = [0, 1, 2, 2, 3]

        block = ctx.enter_context(nc.Block())

        @block.sync
        def _(sp):
            sp.dma_start(tbl_in.rearrange("p (b c) -> p b c", c=P), rows_in.rearrange("(b p) c -> p b c", p=P)
                         ).then_inc(params_in, 16)
            sp.dma_start(posi[:], pos_in).then_inc(params_in, 16)

            def w_slot(rnd, r):
                if not (isinstance(rnd, int) and rnd == 0):
                    sp.wait_ge(lo_ready, ((rnd - 1) * NRAW + r + 1) * 2)
                sp.dma_start(raw[:, r], wstream[rnd * NRAW + r]).then_inc(raw_full[r], 16)

            def m_chunk(m, part=range(8)):
                for u in part:
                    if isinstance(m, int) and 8 * m + u < NMRAW:
                        pass
                    else:
                        sp.wait_ge(mod_ops, m * MOPS + 2 * u - 6)
                    sp.dma_start(mraw[:, u % NMRAW], mstream[m * 8 + u]).then_inc(mod_full[u % NMRAW], 16)

            def chunk(rnd, mod=None):
                for k in range(KS):
                    w_slot(rnd, k)
                    if mod is not None:
                        m_chunk(mod, ((0, 1, 2, 3), (4, 5), (6, 7), ())[k])

            m_chunk(0)
            sp.dma_start(x[:], x_in.rearrange("(t p) d -> p t d", p=P)).then_inc(x_loaded, 16)
            with sp.Fori(1, MODS["pw1"]) as m:
                m_chunk(m)

            def chunks(name, n, mods):
                def pair(i):
                    for j in range(2):
                        chunk(i * 2 + (SLOTS[name] // 4 + j), mods(i, j))
                pair(0)
                with sp.Fori(1, n) as i:
                    pair(i)

            chunks("pw1", PAIRS_PW1, lambda i, j: i * 2 + (MODS["pw1"] + j))
            for k in range(D // N):
                chunk(SLOTS["pw2"] // 4 + k, MODS["pw2"] + k)
            chunks("up0", PAIRS_UP, lambda i, j: i + MODS["up0"] if j == 0 else None)

            def down(name, m0):
                for half in range(2):
                    base = SLOTS[name] + half * 2 * DGROUPS

                    def group(g_rnd, r, mod, part):
                        w_slot(g_rnd, r)
                        if mod is not None:
                            m_chunk(mod, part[:2])
                        w_slot(g_rnd + (r + 1) // 4, (r + 1) % 4)
                        if mod is not None:
                            m_chunk(mod, part[2:])

                    def two(i, m):
                        group(i + (base + 2) // 4, (base + 2) % 4, m, (0, 1, 2, 3))
                        group(i + (base + 4) // 4, (base + 4) % 4, m, (4, 5, 6, 7))

                    group(base // 4, base % 4, None, ())
                    with sp.Fori(0, 4) as i:
                        two(i, None if m0 is None else i + (m0 + 5 * half))
                    two(4, None if m0 is None else m0 + 5 * half + 4)

            down("down0", MODS["down0"])
            chunks("k", 3, lambda i, j: None)
            chunks("v", 3, lambda i, j: i * 2 + (MODS["v"] + j))
            chunks("q", 3, lambda i, j: i * 2 + (MODS["q"] + j))
            for rnd in range(SLOTS["wo"] // 4, SLOTS["up1"] // 4):
                for r in range(4):
                    w_slot(rnd, r)
            r1 = SLOTS["up1"] // 4
            for i in range(3):
                w_slot(r1 + 2 * i, 0)
                if i == 0:
                    sp.wait_ge(tr_done, UNITS["attn"] + 3 * HPG)
                    sp.wait_ge(o_done, 2 * HPG)
                m_chunk(MODS["up1"] + i, (0, 1, 2, 3))
                w_slot(r1 + 2 * i, 1)
                m_chunk(MODS["up1"] + i, (4, 5))
                w_slot(r1 + 2 * i, 2)
                m_chunk(MODS["up1"] + i, (6, 7))
                w_slot(r1 + 2 * i, 3)
                chunk(r1 + 2 * i + 1)
            with sp.Fori(3, PAIRS_UP) as i:
                chunk(i * 2 + r1)
                chunk(i * 2 + (r1 + 1))
            down("down1", None)
            for half in range(2):
                sp.wait_ge(x_ready, X_STAGE[4] + 1 + half)
                sp.dma_start(out.rearrange("(t p) d -> p t d", p=P)[:, :, half * 1024:half * 1024 + 1024],
                             x[:, :, half * 1024:half * 1024 + 1024]).then_inc(out_done, 16)
            sp.wait_ge(out_done, 32)

        @block.gpsimd
        def _(pool):
            pool.memset(ident[:], 0.0).then_inc(const_ready, 1)
            pool.memset(ones[:], 1.0).then_inc(const_ready, 1)
            pool.wait_ge(const_ready, 1)
            pool.affine_select(out=ident[:], in_=ident[:], compare_op=ALU.not_equal, fill=1.0, base=0,
                               pattern=[[-1, P]], channel_multiplier=1).then_inc(const_ready, 1)
            pool.wait_ge(tr_done, UNITS["q"] + 12)
            pool.iota(mask1.bitcast(I32).rearrange("p (g s) -> p g s", g=NG), pattern=[[0, NG], [-1, S]],
                      base=P, channel_multiplier=1).then_inc(iota_ready, 1)
            pool.iota(mask0.bitcast(I32).rearrange("p (g s) -> p g s", g=NG), pattern=[[0, NG], [-1, P]],
                      base=0, channel_multiplier=1).then_inc(iota_ready, 1)
            pool.wait_ge(dil_ready, 2)
            for n, (mk, keys, base) in enumerate(((mask1, S, P), (mask0, P, 0))):
                v = mk.rearrange("p (g s) -> p g s", g=NG)
                pool.affine_select(out=v, in_=v, compare_op=ALU.is_ge, fill=NEG, base=base,
                                   pattern=[[0, NG], [-1, keys]], channel_multiplier=1).then_inc(mask_ready, 1)
            pool.wait_ge(mask_ready, 1)
            pool.affine_select(out=mask1[:, 0:S], in_=mask1[:, 0:S], compare_op=ALU.is_ge, fill=NEG,
                               base=GROUPS[0][0] // GROUPS[0][1] - P, pattern=[[1, S]],
                               channel_multiplier=-1).then_inc(mask_ready, 1)

        @block.scalar
        def _(act):
            def hi(rnd, r, h):
                if h == 0:
                    act.wait_ge(raw_full[r], (rnd + 1) * 16)
                if not (isinstance(rnd, int) and rnd == 0 and r < 2):
                    act.wait_ge(used, rnd * 8 + (2 * r + h - 3))
                act.activation(whi[:, (2 * r + h) % NP_], raw[:, r, h * PIECE:(h + 1) * PIECE],
                               ACT.Copy).then_inc(hi_ready, 1)

            def mod_out(m):
                act.wait_ge(mod_summed, m + 1)
                act.activation(modcol[:, bass.ds(m * 4, 4)], psM[:, 0:4], ACT.Copy).then_inc(mod_ready, 1)

            def norm(n):
                xn = xn_of[n]
                if n == 0:
                    act.wait_ge(x_loaded, 16)
                else:
                    act.wait_ge(x_ready, X_STAGE[n])
                for t in range(TB):
                    act.activation(xn[:, t], x[:, t], ACT.Square, accum_out=ssq[:, t:t + 1])
                act.drain()
                act.activation(ssq, ssq, ACT.Sqrt, bias=eps_c, scale=1.0 / D).then_inc(ssq_ready, 1)
                if NORMS[n][5]:
                    act.wait_ge(used, 2 * NORMS[n][5])
                for u in range(8):
                    act.wait_ge(tr_free, UNITS[f"norm{n}"] + u + 1)
                    act.activation(hhi[:, 2 * u:2 * u + 2], h32_of[n][:, u % 2], ACT.Copy).then_inc(hhi_ready, 1)

            def evac_stage(par, c, units_before):
                act.wait_ge(used, units_before[0] * 2)
                act.wait_ge(tr_done, units_before[1])
                act.activation(stage[:, par], psG[par][:], ACT.Copy).then_inc(evac, 1)

            def chunk(rnd, prev_evac=None, prev_mid=None, prev_late=None, mod=None):
                for q in range(2 * KS):
                    hi(rnd, q // 2, q % 2)
                    if q == 3 and prev_evac:
                        prev_evac()
                    if q == 5 and prev_mid:
                        prev_mid()
                if mod is not None:
                    mod_out(mod)
                if prev_late:
                    prev_late()

            def gate_rows(unit):
                for k in range(4):
                    act.wait_ge(tr_done, UNITS[unit] + k + 1)
                    act.activation(gate[:, k * N:(k + 1) * N], psT[k % 3][:], ACT.Copy).then_inc(tr_free, 1)

            act.wait_ge(tr_free, UNITS["head_g"])
            act.activation(csil[:], cols("c"), ACT.Silu).then_inc(csil_ready, 1)
            act.wait_ge(angle_ready, 1)
            act.activation(cs[:], trig[:, 0:2], ACT.Sin).then_inc(trig_ready, 1)
            with act.Fori(0, MODS["pw1"]) as m:
                mod_out(m)
            norm(0)

            r0, u0, c0 = SLOTS["pw1"] // 4, UNITS["pw1"], CHUNKS["pw1"]

            def sigmoid(i):
                for u in range(2):
                    act.wait_ge(tr_done, i * 4 + (u0 + u + 1))
                    for b in range(2):
                        ins = act.activation(sigb[:, 2 * u + b], psT[u][:, b * S:(b + 1) * S], ACT.Sigmoid,
                                             bias=table[:, bass.ds(i * 4 + (ROWS["pw1_b"] + DB + 2 * u + b), 1)])
                    ins.then_inc(tr_free, 1)

            def pw1_pair(i, first):
                chunk(i * 2 + r0,
                      None if first else lambda: evac_stage(1, None, ((i * 2 + r0) * 4, i * 4 + (u0 - 4))),
                      mod=i * 2 + MODS["pw1"])
                chunk(i * 2 + (r0 + 1),
                      lambda: evac_stage(0, None, ((i * 2 + r0 + 1) * 4, i * 4 + (u0 - 2) if not first else u0)),
                      mod=i * 2 + (MODS["pw1"] + 1))
                sigmoid(i)

            pw1_pair(0, True)
            with act.Fori(1, PAIRS_PW1) as i:
                pw1_pair(i, False)
            evac_stage(1, None, (SLOTS["pw2"], UNITS["ln"] - 4))

            act.wait_ge(ln_step, 1)
            for b in range(0, DB, 4):
                act.activation(ysq[:, b:b + 4], yln[:, b:b + 4], ACT.Square).then_inc(ln_sq, 1)
            act.wait_ge(ln_step, 2)
            act.activation(rs, rs, ACT.Sqrt, bias=eps_c).then_inc(ln_std, 1)
            act.wait_ge(ln_step, 3)
            gate_rows("gate0")
            for u in range(8):
                h32 = ysq[:, 2 * u:2 * u + 2]
                for b in range(2):
                    act.activation(h32[:, b], yln[:, 2 * u + b], ACT.Silu, bias=col("ln_b", 2 * u + b),
                                   scale=col("ln_g", 2 * u + b))
                act.drain()
                act.activation(hhi[:, 2 * u:2 * u + 2], h32, ACT.Copy).then_inc(hhi_ready, 1)

            for c in range(D // N):
                chunk(SLOTS["pw2"] // 4 + c, mod=MODS["pw2"] + c)
            norm(1)

            def ffn_up(name, layer, mods):
                r0, u0 = SLOTS[name] // 4, UNITS[name]

                def silu(i):
                    act.wait_ge(tr_free, i * 4 + (u0 + 2))
                    act.activation(convb, convb, ACT.Silu).then_inc(silu_ready, 1)

                def pair(i, first, mod):
                    chunk(i * 2 + r0,
                          None if first else lambda: (silu(i - 1), evac_stage(1, None, (
                              (i * 2 + r0) * 4, i * 4 + (u0 - 4)))),
                          mod=i + MODS[name] if mod else None)
                    chunk(i * 2 + (r0 + 1),
                          lambda: evac_stage(0, None, ((i * 2 + r0 + 1) * 4, u0 if first else i * 4 + (u0 - 2))))

                pair(0, True, mods > 0)
                if mods > 1:
                    with act.Fori(1, mods) as i:
                        pair(i, False, True)
                if mods < PAIRS_UP:
                    with act.Fori(mods, PAIRS_UP) as i:
                        pair(i, False, False)
                silu(PAIRS_UP - 1)
                evac_stage(1, None, ((r0 + 2 * PAIRS_UP) * 4, u0 + 4 * PAIRS_UP - 4))

            def ffn_down(name, layer, m0):
                for half in range(2):
                    base = SLOTS[name] + half * 2 * DGROUPS
                    gb = half * DGROUPS
                    gall = layer * 2 * DGROUPS + gb

                    def group(i, g, mod=None):
                        s0 = base + 2 * g
                        ring = (gb + g) % 2
                        if not (half == 0 and isinstance(i, int) and g + 2 * i < 2):
                            act.wait_ge(used, (i * 4 + (s0 - 2)) * 2)
                        if isinstance(i, int) and half == 0 and g == 0:
                            act.wait_ge(silu_ready, (layer + 1) * (PAIRS_UP + 1))
                        act.activation(hhi[:, 4 * ring:4 * ring + 4],
                                       hidden[:, bass.ds(i * 8 + 4 * g, 4)], ACT.Copy).then_inc(hid_hi, 1)
                        for sl in (s0, s0 + 1):
                            for h in range(2):
                                hi(i + sl // 4, sl % 4, h)

                    group(0, 0)
                    with act.Fori(0, 4) as i:
                        group(i, 1)
                        group(i, 2)
                        if m0 is not None:
                            mod_out(i + (m0 + 5 * half))
                    group(4, 1)
                    group(4, 2)
                    if m0 is not None:
                        mod_out(m0 + 5 * half + 4)

            ffn_up("up0", 0, PAIRS_UP)
            gate_rows("gate1")
            ffn_down("down0", 0, MODS["down0"])
            norm(2)

            def heads_root(n):
                act.wait_ge(head_ssq, n + 1)
                act.activation(hsd, hss, ACT.Sqrt, bias=eps_c, scale=1.0 / DH).then_inc(head_std, 1)

            def heads_evac(name, slots_done, n, par):
                act.wait_ge(used, slots_done * 2)
                if not (isinstance(n, int) and n == 0):
                    act.wait_ge(tr_done, UNITS[name] + (n - (0 if name == "k" else QW // N)) * 2)
                act.activation(stage[:, 0], psG[par][:], ACT.Copy)
                act.activation(stage[:, 1], psG[par][:], ACT.Square).then_inc(evac, 1)

            def heads_out(name, n):
                dst = kT if name == "k" else qT
                for u in range(2):
                    act.wait_ge(tr_done, n * 2 + (UNITS[name] + u + 1))
                    act.activation(dst[:, bass.ds(n * 4 + 2 * u, 2)], psT[u][:].rearrange("p (b s) -> p b s", s=S),
                                   ACT.Copy).then_inc(tr_free, 1)

            def heads_chunk(name, n, par, first, mod=None, also_first=None):
                base = 0 if name == "k" else QW // N
                rnd = n + SLOTS[name] // 4
                if first:
                    chunk(rnd, mod=mod)
                else:
                    chunk(rnd, lambda: heads_evac(name, rnd * 4, n + (base - 1), 1 - par),
                          lambda: heads_root(n + (base - 1)), lambda: heads_out(name, n - 1), mod)

            def heads_last(name):
                base = 0 if name == "k" else QW // N
                n = QW // N
                heads_evac(name, SLOTS[name] + 4 * n, n - 1 + base, 1)
                heads_root(n - 1 + base)
                heads_out(name, n - 1)

            def heads(name, mods):
                m0 = MODS.get(name)
                heads_chunk(name, 0, 0, True, m0)
                heads_chunk(name, 1, 1, False, m0 + 1 if mods else None)
                with act.Fori(1, 3) as i:
                    for j in range(2):
                        heads_chunk(name, i * 2 + j, j, False, i * 2 + (m0 + j) if mods else None)
                heads_last(name)

            def v_evac(slots_done, n, par):
                act.wait_ge(used, slots_done * 2)
                act.activation(vv[:, :, bass.ds(n * N, N)], psG[par][:], ACT.Copy).then_inc(evac, 1)

            heads("k", False)
            r0 = SLOTS["v"] // 4

            def v_chunk(n, par, first):
                chunk(n + r0, None if first else lambda: v_evac((n + r0) * 4, n - 1, 1 - par), mod=n + MODS["v"])

            v_chunk(0, 0, True)
            v_chunk(1, 1, False)
            with act.Fori(1, 3) as i:
                for j in range(2):
                    v_chunk(i * 2 + j, j, False)
            v_evac(SLOTS["q"], 5, 1)
            norm(3)
            heads("q", True)

            def prob_out(j):
                h, qb = j // 2, j % 2
                for u in range(1 + qb):
                    act.wait_ge(tr_done, UNITS["attn"] + 3 * h + qb + u + 1)
                    if u == 0 and j >= 2:
                        act.wait_ge(o_done, j - 1)
                    k0, k1 = (0, 3) if qb == 0 else ((0, 4), (4, 6))[u]
                    act.activation(probT[j % 2][:, k0:k1].rearrange("p b q -> p (b q)"),
                                   psT[qb + u][:, 0:(k1 - k0) * P], ACT.Copy).then_inc(tr_free, 1)

            def o_split(h):
                act.wait_ge(o_done, 2 * h + 2)
                act.activation(hhi[:, h], psM[:, 0:S], ACT.Copy).then_inc(hhi_ready, 1)

            for j in range(2 * HPG + 1):
                if j < 2 * HPG:
                    act.wait_ge(max_ready, j + 1)
                    w = NKEY[j % 2]
                    act.activation(prob[j % 2][:, 0:w], prob[j % 2][:, 0:w], ACT.Exp, bias=nmx[:, j % 2:j % 2 + 1],
                                   scale=SCALE, accum_out=den[:, j % 2:j % 2 + 1]).then_inc(exp_ready, 1)
                if j >= 1:
                    prob_out(j - 1)
                if j >= 3 and j % 2 == 1:
                    o_split((j - 3) // 2)
            o_split(HPG - 1)

            gate_rows("gate2")
            r0 = SLOTS["wo"] // 4
            for rnd in range(2):
                for q in range(8):
                    hi(r0 + rnd, q // 2, q % 2)
            norm(4)
            ffn_up("up1", 1, 3)
            gate_rows("gate3")
            ffn_down("down1", 1, None)

        @block.vector
        def _(dve):
            TT, TS, STT = dve.tensor_tensor, dve.tensor_scalar, dve.scalar_tensor_tensor

            def lo(rnd, r, h):
                dve.wait_ge(hi_ready, rnd * 8 + (2 * r + h + 1))
                q = (2 * r + h) % NP_
                TT(wlo[:, q], raw[:, r, h * PIECE:(h + 1) * PIECE], whi[:, q].bitcast(F32),
                   ALU.subtract).then_inc(lo_ready, 1)

            def mod_mul(m, part):
                for u in part:
                    dve.wait_ge(mod_full[u % NMRAW], m * 32 + 16 * (u // NMRAW + 1))
                    for j in range(2):
                        k = 2 * u + j
                        w = mraw[:, u % NMRAW, j * N:(j + 1) * N]
                        if k == 0:
                            if not (isinstance(m, int) and m == 0):
                                dve.wait_ge(mod_summed, m)
                        if k < 2:
                            TS(acc[:, j], w, csil[:, k:k + 1], None, ALU.mult).then_inc(mod_ops, 1)
                        else:
                            dve.wait_ge(mod_ops, m * MOPS + (k - 1))
                            STT(acc[:, j], w, csil[:, k:k + 1], acc[:, j], ALU.mult, ALU.add).then_inc(mod_ops, 1)

            def chunk(rnd, work=None, mod=None):
                for q in range(2 * KS):
                    lo(rnd, q // 2, q % 2)
                    if work and q in work:
                        work[q]()
                    if mod is not None and q < 7:
                        mod_mul(mod, (0, 1) if q == 0 else (q + 1,))

            def norm(n):
                gain, g0, sh, sc, chunks_needed, slots_needed = NORMS[n]
                xn, h32 = xn_of[n], h32_of[n]
                dve.wait_ge(mod_ready, chunks_needed)
                TT(nsc[:], modcol[:, sc:sc + DB], cols("mod_b", sc), ALU.add)
                TT(nsh[:], modcol[:, sh:sh + DB], cols("mod_b", sh), ALU.add)
                dve.drain()
                STT(nsc[:], nsc[:], 1.0, cols(gain, g0), ALU.add, ALU.mult)
                dve.wait_ge(ssq_ready, n + 1)
                dve.reciprocal(rstd, ssq)
                dve.drain()
                for t in range(TB):
                    TS(xn[:, t], x[:, t], rstd[:, t:t + 1], None, ALU.mult).then_inc(xn_ready, 1)
                if slots_needed:
                    dve.wait_ge(used, 2 * slots_needed)

                def low(u):
                    dve.wait_ge(hhi_ready, HB[n] + u + 1)
                    TT(hlo[:, 2 * u:2 * u + 2], h32[:, u % 2], hhi[:, 2 * u:2 * u + 2].bitcast(F32),
                       ALU.subtract).then_inc(hlo_ready, 1)

                for u in range(8):
                    if u >= 2:
                        low(u - 2)
                        dve.drain()
                    dve.wait_ge(tr_done, UNITS[f"norm{n}"] + u + 1)
                    for b in range(2):
                        k = 2 * u + b
                        ins = TS(h32[:, u % 2, b], psT[u % 3][:, b * S:(b + 1) * S], nsc[:, k:k + 1], nsh[:, k:k + 1],
                                 ALU.mult, ALU.add)
                    ins.then_inc(tr_free, 1)
                low(6)
                low(7)
                dve.drain()

            def diagonals(vec, unit, read=None):
                base = UNITS[unit]
                for k in range(4):
                    if k >= 2:
                        dve.wait_ge(tr_done, base + k - 1)
                        if read:
                            read(k - 2)
                    for b in range(4):
                        ins = TS(diag[:, 4 * (k % 2) + b], ident[:], vec[:, 4 * k + b:4 * k + b + 1], None, ALU.mult)
                    ins.then_inc(diag_ready, 1)
                if read:
                    read(2)
                    read(3)

            def gate_cols(g, chunks_needed):
                dve.wait_ge(mod_ready, chunks_needed)
                TT(nsh[:], modcol[:, g:g + DB], cols("mod_b", g), ALU.add)
                dve.drain()

            def residual(par, col0, slots_done, last=False):
                dve.wait_ge(used, slots_done * 2)
                tmp = stage[:, 1]
                for t in range(TB):
                    ins = TT(tmp[:, t], psG[par][:, t], gate[:, col0:col0 + N], ALU.mult)
                ins.then_inc(evac, 1)
                dve.drain()
                xs = x[:, :, col0:col0 + N]
                ins = TT(xs, xs, tmp, ALU.add)
                if last:
                    ins.then_inc(x_ready, 1)
                dve.drain()

            dve.memset(eps_c, EPS)
            freq = inv_freq()
            for i in range(HR):
                dve.memset(trig[:, 7, :, i:i + 1], float(freq[i]))
            for u in range(UNITS["head_g"]):
                dve.wait_ge(tr_done, u + 1)
                k0, k1 = 4 * u, min(4 * u + 4, NRB)
                dve.tensor_copy(table[:, k0 * P:k1 * P], psT[u][:, 0:(k1 - k0) * P]).then_inc(tr_free, 1)
            dve.drain()
            dve.wait_ge(const_ready, 3)
            for i in range(2):
                ins = TS(headg[:, i], ident[:], col("head_g", i), None, ALU.mult)
            ins.then_inc(diag_ready, 1)
            dve.wait_ge(tr_done, UNITS["head_g"] + 1)
            dve.tensor_copy(headg[:], psT[0][:, 0:2 * DH].rearrange("p (a b) -> p a b", a=2)).then_inc(tr_free, 1)
            k_, r_, a_, b_ = trig[:, 4], trig[:, 1], trig[:, 2], trig[:, 3]
            dve.wait_ge(params_in, 32)
            dve.tensor_copy(posf[:], posi[:])
            dve.drain()
            for t in range(TB):
                TS(a_[:, t], trig[:, 7, t], posf[:, t:t + 1], None, ALU.mult)
            dve.drain()
            TS(b_, a_, 1.0 / (2 * PI), ROUND, ALU.mult, ALU.add)
            dve.drain()
            TS(k_, b_, ROUND, None, ALU.subtract)
            dve.drain()
            STT(b_, k_, -TWO_PI[0], a_, ALU.mult, ALU.add)
            dve.drain()
            STT(a_, k_, -TWO_PI[1], b_, ALU.mult, ALU.add)
            dve.drain()
            STT(b_, k_, -TWO_PI[2], a_, ALU.mult, ALU.add)
            dve.drain()
            TS(r_, b_, PI_BELOW, -PI_BELOW, ALU.min, ALU.max)
            TS(a_, b_, PI / 2, None, ALU.add)
            dve.drain()
            TS(k_, a_, PI, -2 * PI, ALU.is_gt, ALU.mult)
            dve.drain()
            TT(b_, a_, k_, ALU.add)
            dve.drain()
            TS(trig[:, 0], b_, PI_BELOW, -PI_BELOW, ALU.min, ALU.max).then_inc(angle_ready, 1)
            dve.wait_ge(trig_ready, 1)
            dve.wait_ge(csil_ready, 1)

            mod_mul(0, range(8))
            with dve.Fori(1, MODS["pw1"]) as m:
                mod_mul(m, range(8))
            norm(0)

            r0, u0 = SLOTS["pw1"] // 4, UNITS["pw1"]
            dve.memset(upad[:, :, 0:UPAD], 0.0)
            dve.drain()

            def glu(i):
                dve.wait_ge(tr_free, i * 4 + (u0 + 2))
                for u in range(2):
                    dve.wait_ge(tr_done, i * 4 + (u0 + 2 + u + 1))
                    for b in range(2):
                        k = 2 * u + b
                        ins = STT(upad[:, k, UPAD:UPAD + S], psT[(2, 0)[u]][:, b * S:(b + 1) * S],
                                  table[:, bass.ds(i * 4 + (ROWS["pw1_b"] + k), 1)], sigb[:, k], ALU.add, ALU.mult)
                    ins.then_inc(tr_free, 1)
                dve.drain()

            def conv(i, taps):
                for j in taps:
                    for b in range(4):
                        y = yln[:, bass.ds(i * 4 + b, 1)]
                        w = table[:, bass.ds(i * 4 + (ROWS["conv_w"] + j * DB + b), 1)]
                        src = upad[:, b:b + 1, j:j + S]
                        if j == 0:
                            ins = TS(y, src, w, table[:, bass.ds(i * 4 + (ROWS["dw_b"] + b), 1)], ALU.mult, ALU.add)
                        else:
                            ins = STT(y, src, w, y, ALU.mult, ALU.add)
                    if j == CONV_K - 1:
                        ins.then_inc(conv_ready, 1)
                    dve.drain()

            def pw1_pair(i, first):
                def taps(a, b):
                    return lambda: conv(i - 1, range(a, b))
                chunk(i * 2 + r0, None if first else {5: lambda: glu(i - 1), 6: taps(0, 3), 7: taps(3, 6)},
                      mod=i * 2 + MODS["pw1"])
                chunk(i * 2 + (r0 + 1), None if first else {q: taps(6 + q * 3, min(9 + q * 3, CONV_K)) for q in range(8)
                                                            } | {7: taps(27, CONV_K)},
                      mod=i * 2 + (MODS["pw1"] + 1))

            pw1_pair(0, True)
            with dve.Fori(1, PAIRS_PW1) as i:
                pw1_pair(i, False)
            glu(PAIRS_PW1 - 1)
            conv(PAIRS_PW1 - 1, range(CONV_K))

            dve.wait_ge(tr_done, UNITS["ln"] + 1)
            TS(mu, psT[0][:, 0:S], 1.0 / D, None, ALU.mult).then_inc(tr_free, 1)
            dve.drain()
            mub = mu.rearrange("p (a s) -> p a s", a=1).to_broadcast([P, DB, S])
            TT(yln, yln, mub, ALU.subtract).then_inc(ln_step, 1)
            dve.wait_ge(tr_done, UNITS["ln"] + 2)
            TS(rs, psT[1][:, 0:S], 1.0 / D, None, ALU.mult).then_inc(tr_free, 1)
            dve.drain()
            dve.sem_inc(ln_step, 1)
            dve.wait_ge(ln_std, 1)
            dve.reciprocal(mu, rs)
            dve.drain()
            TT(yln, yln, mub, ALU.mult).then_inc(ln_step, 1)
            gate_cols(MC0 + 2 * DB, 12)
            diagonals(nsh, "gate0")
            dve.wait_ge(tr_free, UNITS["gate0"] + 4)
            TT(nsh[:], nsh[:], cols("pw2_b"), ALU.mult)
            dve.drain()

            def add_bias(k):
                dve.wait_ge(tr_done, UNITS["bias0"] + k + 1)
                for t in range(TB):
                    xs = x[:, t, k * N:(k + 1) * N]
                    ins = TT(xs, psT[k % 3][:], xs, ALU.add)
                ins.then_inc(tr_free, 1)

            diagonals(nsh, "bias0", add_bias)
            for u in range(8):
                dve.wait_ge(hhi_ready, LNH + u + 1)
                TT(hlo[:, 2 * u:2 * u + 2], ysq[:, 2 * u:2 * u + 2], hhi[:, 2 * u:2 * u + 2].bitcast(F32),
                   ALU.subtract).then_inc(hlo_ready, 1)
            dve.drain()

            for c in range(D // N):
                rnd = SLOTS["pw2"] // 4 + c
                chunk(rnd, {3: lambda: residual((c - 1) % 2, (c - 1) * N, rnd * 4)} if c else None,
                      mod=MODS["pw2"] + c)
            residual(1, D - N, SLOTS["up0"], last=True)
            norm(1)

            def ffn_up(name, layer, mods):
                r0, u0 = SLOTS[name] // 4, UNITS[name]
                wrow, brow = ROWS["ffn_w"] + layer * FFN_K * FB, ROWS["ffn_b"] + layer * FB

                def conv3(i, u):
                    if u in (0, 1):
                        dve.wait_ge(tr_done, i * 4 + (u0 + u + 1))
                        for j in reversed(range(FFN_K)):
                            back = FFN_K - 1 - j
                            for b in range(2):
                                k = 2 * u + b
                                g = psT[u][:, b * S:(b + 1) * S - back]
                                w = table[:, bass.ds(i * 4 + (wrow + j * FB + k), 1)]
                                y = convb[:, k, back:S]
                                if back == 0:
                                    ins = TS(y, g, w, table[:, bass.ds(i * 4 + (brow + k), 1)], ALU.mult, ALU.add)
                                else:
                                    ins = STT(y, g, w, y, ALU.mult, ALU.add)
                            if j:
                                dve.drain()
                        ins.then_inc(tr_free, 1)

                def multiply(i):
                    dve.wait_ge(silu_ready, i + (layer * (PAIRS_UP + 1) + 1))
                    for u in range(2):
                        dve.wait_ge(tr_done, i * 4 + (u0 + 2 + u + 1))
                        ins = TT(hidden[:, bass.ds(i * 4 + 2 * u, 2)], convb[:, 2 * u:2 * u + 2],
                                 psT[(2, 0)[u]][:].rearrange("p (b s) -> p b s", s=S), ALU.mult)
                        ins.then_inc(tr_free, 1)
                    dve.drain()

                def pair(i, first, mod):
                    chunk(i * 2 + r0, None if first else {5: lambda: multiply(i - 1)},
                          mod=i + MODS[name] if mod else None)
                    chunk(i * 2 + (r0 + 1), {5: lambda: conv3(i, 0), 6: lambda: conv3(i, 1)})

                pair(0, True, mods > 0)
                if mods > 1:
                    with dve.Fori(1, mods) as i:
                        pair(i, False, True)
                if mods < PAIRS_UP:
                    with dve.Fori(mods, PAIRS_UP) as i:
                        pair(i, False, False)
                multiply(PAIRS_UP - 1)
                dve.sem_inc(silu_ready, 1)

            def ffn_down(name, layer, m0):
                for half in range(2):
                    base = SLOTS[name] + half * 2 * DGROUPS
                    gb = half * DGROUPS

                    def group(i, g, mod=None, part=()):
                        s0 = base + 2 * g
                        ring = (gb + g) % 2
                        dve.wait_ge(hid_hi, i * 2 + (layer * 2 * DGROUPS + gb + g + 1))
                        TT(hlo[:, 4 * ring:4 * ring + 4], hidden[:, bass.ds(i * 8 + 4 * g, 4)],
                           hhi[:, 4 * ring:4 * ring + 4].bitcast(F32), ALU.subtract).then_inc(hid_lo, 1)
                        for q in range(4):
                            sl = s0 + q // 2
                            lo(i + sl // 4, sl % 4, q % 2)
                            if mod is not None:
                                mod_mul(mod, (part[q],))

                    def two(i, m):
                        group(i, 1, m, (0, 1, 2, 3))
                        group(i, 2, m, (4, 5, 6, 7))

                    group(0, 0)
                    with dve.Fori(0, 4) as i:
                        two(i, None if m0 is None else i + (m0 + 5 * half))
                    two(4, None if m0 is None else m0 + 5 * half + 4)
                    for nt in range(2):
                        last = layer == 1 and nt == 1 or half == 1 and nt == 1
                        residual(nt, half * 2 * N + nt * N, base + 2 * DGROUPS, last=last)

            ffn_up("up0", 0, PAIRS_UP)
            gate_cols(MC0 + 5 * DB, 24)
            diagonals(nsh, "gate1")
            dve.wait_ge(tr_free, UNITS["gate1"] + 4)
            ffn_down("down0", 0, MODS["down0"])
            norm(2)

            heads8 = stage[:, 0].rearrange("p t (h c) -> p (t h) c", c=DH)
            sq8 = stage[:, 1].rearrange("p t (h c) -> p (t h) c", c=DH)
            heads = stage[:, 0].rearrange("p t (h c) -> p t h c", c=DH)
            rtmp = stage[:, 1].rearrange("p t (k h c) -> p k t h c", k=8, c=HR)
            cosb, sinb = (cs[:, n].rearrange("p t (a f) -> p t a f", a=1).to_broadcast([P, TB, 4, HR]) for n in range(2))

            def heads_squares(n):
                dve.wait_ge(evac, n)
                dve.tensor_reduce(hss, sq8, AX, ALU.add).then_inc(head_ssq, 1)

            def heads_norm(n, which):
                dve.wait_ge(head_std, n)
                dve.reciprocal(hrs, hsd)
                dve.drain()
                TT(heads8, heads8, hrs.rearrange("p (a c) -> p a c", c=1).to_broadcast([P, 8, DH]), ALU.mult)
                dve.drain()
                TT(heads8, heads8, headg[:, which].rearrange("p (a c) -> p a c", a=1).to_broadcast([P, 8, DH]), ALU.mult)
                dve.drain()
                x1, x2 = heads[:, :, :, 0:HR], heads[:, :, :, HR:ROT]
                TT(rtmp[:, 0], x1, cosb, ALU.mult)
                TT(rtmp[:, 1], x2, sinb, ALU.mult)
                TT(rtmp[:, 2], x2, cosb, ALU.mult)
                TT(rtmp[:, 3], x1, sinb, ALU.mult)
                dve.drain()
                TT(x1, rtmp[:, 0], rtmp[:, 1], ALU.subtract)
                TT(x2, rtmp[:, 2], rtmp[:, 3], ALU.add).then_inc(head_ready, 1)

            def heads_stage(name, mods):
                base = 0 if name == "k" else QW // N
                m0 = MODS.get(name)

                def one(n, first=False, mod=None):
                    p = n - 1
                    chunk(n + SLOTS[name] // 4,
                          None if first else {4: lambda: heads_squares(p + (CHUNKS[name] + 1)),
                                              5: lambda: heads_norm(p + (base + 1), name == "q")}, mod=mod)

                one(0, True, m0 if mods else None)
                one(1, False, m0 + 1 if mods else None)
                with dve.Fori(1, 3) as i:
                    for j in range(2):
                        one(i * 2 + j, False, i * 2 + (m0 + j) if mods else None)
                heads_squares(CHUNKS[name] + QW // N)
                heads_norm(QW // N + base, name == "q")

            heads_stage("k", False)
            chunk(SLOTS["v"] // 4, mod=MODS["v"])
            chunk(SLOTS["v"] // 4 + 1, mod=MODS["v"] + 1)
            with dve.Fori(1, 3) as i:
                for j in range(2):
                    chunk(i * 2 + (SLOTS["v"] // 4 + j), mod=i * 2 + (MODS["v"] + j))
            norm(3)
            heads_stage("q", True)

            for n, mk in enumerate((mask1, mask0)):
                v = mk.rearrange("p (g s) -> p g s", g=NG)
                dve.wait_ge(iota_ready, n + 1)
                for g, (_, dil) in enumerate(GROUPS):
                    TS(v[:, g].bitcast(I32), v[:, g].bitcast(I32), dil - 1, None, ALU.bitwise_and)
                dve.drain()
                TS(mk, mk.bitcast(I32), 0, NEG, ALU.is_gt, ALU.mult).then_inc(dil_ready, 1)
            dve.wait_ge(mask_ready, 3)

            def softmax_max(j):
                w = NKEY[j % 2]
                dve.wait_ge(score_done, j + 1)
                if j >= 2:
                    dve.wait_ge(tr_done, UNITS["attn"] + ATTN_UNITS[j - 2])
                TT(prob[j % 2][:, 0:w], psG[j % 2][:].rearrange("p t n -> p (t n)")[:, 0:w],
                   masks[1 - j % 2], ALU.add).then_inc(score_read, 1)
                dve.drain()
                dve.reduce_max(mx[:, j % 2:j % 2 + 1], prob[j % 2][:, 0:w], AX)
                dve.drain()
                TS(nmx[:, j % 2:j % 2 + 1], mx[:, j % 2:j % 2 + 1], -SCALE, None, ALU.mult).then_inc(max_ready, 1)

            def softmax_divide(j):
                w = NKEY[j % 2]
                dve.wait_ge(exp_ready, j + 1)
                dve.reciprocal(rden[:, j % 2:j % 2 + 1], den[:, j % 2:j % 2 + 1])
                dve.drain()
                TS(prob[j % 2][:, 0:w], prob[j % 2][:, 0:w], rden[:, j % 2:j % 2 + 1], None, ALU.mult).then_inc(prob_ready, 1)

            def o_low(h):
                dve.wait_ge(hhi_ready, HO + h + 1)
                TT(hlo[:, h], psM[:, 0:S], hhi[:, h].bitcast(F32), ALU.subtract).then_inc(o_read, 1)

            for j in range(2 * HPG + 1):
                if j < 2 * HPG:
                    softmax_max(j)
                if j >= 1:
                    softmax_divide(j - 1)
                if j >= 3 and j % 2 == 1:
                    o_low((j - 3) // 2)
            o_low(HPG - 1)
            dve.drain()

            gate_cols(MC1 + 2 * DB, 44)
            diagonals(nsh, "gate2")
            dve.wait_ge(tr_free, UNITS["gate2"] + 4)
            for c in range(D // N):
                rnd, r = SLOTS["wo"] // 4 + c // 2, c % 2 * 2
                for q in range(4):
                    lo(rnd, r + q // 2, q % 2)
                    if q == 3 and c:
                        residual((c - 1) % 2, (c - 1) * N, rnd * 4 + r)
            residual(1, D - N, SLOTS["up1"], last=True)
            norm(4)
            ffn_up("up1", 1, 3)
            gate_cols(MC1 + 5 * DB, 56)
            diagonals(nsh, "gate3")
            dve.wait_ge(tr_free, UNITS["gate3"] + 4)
            ffn_down("down1", 1, None)

        @block.tensor
        def _(pe):
            def split_matmul(out_, act_hi, act_lo, q, col0, first, last, done=False):
                w = slice(col0, col0 + N)
                pe.matmul(out_, act_hi, whi[:, q, w], start=first, stop=False)
                pe.matmul(out_, act_hi, wlo[:, q, w], start=False, stop=False)
                ins = pe.matmul(out_, act_lo, whi[:, q, w], start=False, stop=last)
                if done:
                    ins.then_inc(used, 1)

            def mod_sum(m, first=False):
                pe.wait_ge(mod_ops, (m + 1) * MOPS)
                if not first:
                    pe.wait_ge(mod_ready, m)
                for k in range(4):
                    for j in range(2):
                        ins = pe.matmul(psM[:, k:k + 1], acc[:, j, k * P:(k + 1) * P], ones[:, 0:1],
                                        start=j == 0, stop=j == 1)
                ins.then_inc(mod_summed, 1)

            def chunk(rnd, c, par, work=None, mod=None, r0=0, slots=KS):
                if not (isinstance(c, int) and c < 2):
                    pe.wait_ge(evac, c - 1)
                for q in range(2 * slots):
                    pe.wait_ge(lo_ready, rnd * 8 + (2 * r0 + q + 1))
                    for kb in range(2):
                        for t in range(TB):
                            b, ts = 2 * q + kb, slice(t * P, (t + 1) * P)
                            split_matmul(psG[par][:, t], hhi[:, b, ts], hlo[:, b, ts], (2 * r0 + q) % NP_, kb * N,
                                         b == 0, b == 4 * slots - 1, kb == 1 and t == TB - 1)
                    if work and q in work:
                        work[q]()
                    if mod is not None and q == 5:
                        mod_sum(mod)

            def transposes(src_of, n, bank, free):
                pe.wait_ge(tr_free, free)
                for b in range(2):
                    for t in range(TB):
                        ins = pe.transpose(psT[bank][:, b * S + t * P:b * S + (t + 1) * P], src_of(b, t), ident[:])
                ins.then_inc(tr_done, 1)

            def norm(n):
                u0 = UNITS[f"norm{n}"]
                pe.wait_ge(xn_ready, 2 * n + 2)
                for u in range(8):
                    transposes(lambda b, t: xn_of[n][:, t, (2 * u + b) * P:(2 * u + b + 1) * P],
                               u0 + u, u % 3, max(u0, u0 + u - 2))
                pe.wait_ge(hlo_ready, HL[n] + 8)

            def broadcast_rows(unit, d0):
                u0 = UNITS[unit]
                for k in range(4):
                    pe.wait_ge(diag_ready, d0 + k + 1)
                    pe.wait_ge(tr_free, max(u0, u0 + k - 2))
                    ins = pe.matmul(psT[k % 3][:], ones[:], diag[:, 4 * (k % 2):4 * (k % 2) + 4].rearrange(
                        "p b c -> p (b c)"), start=True, stop=True)
                    ins.then_inc(tr_done, 1)

            pe.wait_ge(const_ready, 3)
            pe.wait_ge(params_in, 32)
            for u in range(UNITS["head_g"]):
                for k in range(4 * u, min(4 * u + 4, NRB)):
                    ins = pe.transpose(psT[u][:, (k - 4 * u) * P:(k - 4 * u + 1) * P], tbl_in[:, k * P:(k + 1) * P],
                                       ident[:])
                ins.then_inc(tr_done, 1)
            pe.wait_ge(diag_ready, 1)
            pe.wait_ge(tr_free, UNITS["head_g"])
            pe.matmul(psT[0][:, 0:2 * DH], ones[:], headg[:].rearrange("p a b -> p (a b)"), start=True,
                      stop=True).then_inc(tr_done, 1)

            mod_sum(0, first=True)
            with pe.Fori(1, MODS["pw1"]) as m:
                mod_sum(m)
            norm(0)

            def pair_transposes(i, u0, value):
                n = i * 4 + (u0 + 2 * value)
                for u in range(2):
                    transposes(lambda b, t: stage[:, value, t, (2 * u + b) * P:(2 * u + b + 1) * P],
                               n + u, ((0, 1), (2, 0))[value][u], n if not value else n - 2 + u)

            def pairs(name, count, mods, mod_of):
                r0, u0, c0 = SLOTS[name] // 4, UNITS[name], CHUNKS[name]

                def value_transposes(i):
                    pe.wait_ge(evac, i * 2 + (c0 + 2))
                    pair_transposes(i, u0, 1)

                def gate_transposes(i):
                    pe.wait_ge(evac, i * 2 + (c0 + 1))
                    pair_transposes(i, u0, 0)

                def pair(i, first, mod):
                    chunk(i * 2 + r0, i * 2 + c0, 0, None if first else {1: lambda: value_transposes(i - 1)},
                          mod=mod_of(i, 0) if mod else None)
                    chunk(i * 2 + (r0 + 1), i * 2 + (c0 + 1), 1, {1: lambda: gate_transposes(i)},
                          mod=mod_of(i, 1) if mod else None)

                pair(0, True, mods > 0)
                if mods > 1:
                    with pe.Fori(1, mods) as i:
                        pair(i, False, True)
                if mods < count:
                    with pe.Fori(mods, count) as i:
                        pair(i, False, False)
                value_transposes(count - 1)

            pairs("pw1", PAIRS_PW1, PAIRS_PW1, lambda i, j: i * 2 + (MODS["pw1"] + j))

            pe.wait_ge(conv_ready, PAIRS_PW1)
            pe.wait_ge(tr_free, UNITS["ln"])
            for b in range(DB):
                ins = pe.matmul(psT[0][:, 0:S], ones[:], yln[:, b], start=b == 0, stop=b == DB - 1)
            ins.then_inc(tr_done, 1)
            for b in range(DB):
                if b % 4 == 0:
                    pe.wait_ge(ln_sq, b // 4 + 1)
                ins = pe.matmul(psT[1][:, 0:S], ones[:], ysq[:, b], start=b == 0, stop=b == DB - 1)
            ins.then_inc(tr_done, 1)
            broadcast_rows("gate0", 1)
            broadcast_rows("bias0", 5)
            pe.wait_ge(hlo_ready, LNH + 8)

            for c in range(D // N):
                chunk(SLOTS["pw2"] // 4 + c, CHUNKS["pw2"] + c, c % 2, mod=MODS["pw2"] + c)
            norm(1)

            def ffn_down(name, layer, m0):
                for half in range(2):
                    base = SLOTS[name] + half * 2 * DGROUPS
                    gb = half * DGROUPS

                    def group(i, g, first=False, last=False):
                        ring = (gb + g) % 2
                        pe.wait_ge(hid_lo, i * 2 + (layer * 2 * DGROUPS + gb + g + 1))
                        for q in range(4):
                            n = 2 * (base + 2 * g) + q
                            pe.wait_ge(lo_ready, i * 8 + (n + 1))
                            b = 4 * ring + q
                            for nt in range(2):
                                if first and q == 0:
                                    pe.wait_ge(evac, CHUNKS[name] + 2 * half - 1 + nt)
                                for t in range(TB):
                                    split_matmul(psG[nt][:, t], hhi[:, b, t * P:(t + 1) * P],
                                                 hlo[:, b, t * P:(t + 1) * P], n % NP_, nt * N,
                                                 first and q == 0, last and q == 3, nt == 1 and t == TB - 1)

                    group(0, 0, first=True)
                    with pe.Fori(0, 4) as i:
                        group(i, 1)
                        group(i, 2)
                        if m0 is not None:
                            mod_sum(i + (m0 + 5 * half))
                    group(4, 1)
                    group(4, 2, last=True)
                    if m0 is not None:
                        mod_sum(m0 + 5 * half + 4)

            pairs("up0", PAIRS_UP, PAIRS_UP, lambda i, j: i + MODS["up0"] if j == 0 else None)
            broadcast_rows("gate1", 9)
            ffn_down("down0", 0, MODS["down0"])
            norm(2)

            def heads(name, mods):
                base = 0 if name == "k" else QW // N
                u0, m0 = UNITS[name], MODS.get(name)

                def out_of(n):
                    pe.wait_ge(head_ready, n + (base + 1))
                    for u in range(2):
                        transposes(lambda b, t: stage[:, 0, t, (2 * u + b) * P:(2 * u + b + 1) * P],
                                   None, u, n * 2 + u0)

                def one(n, par, first=False, mod=None):
                    chunk(n + SLOTS[name] // 4, n + CHUNKS[name], par,
                          None if first else {5: lambda: out_of(n - 1)}, mod=mod)

                one(0, 0, True, m0 if mods else None)
                one(1, 1, False, m0 + 1 if mods else None)
                with pe.Fori(1, 3) as i:
                    for j in range(2):
                        one(i * 2 + j, j, False, i * 2 + (m0 + j) if mods else None)
                out_of(QW // N - 1)

            heads("k", False)
            r0, c0, m0 = SLOTS["v"] // 4, CHUNKS["v"], MODS["v"]
            with pe.Fori(0, 3) as i:
                for j in range(2):
                    chunk(i * 2 + (r0 + j), i * 2 + (c0 + j), j, mod=i * 2 + (m0 + j))
            norm(3)
            heads("q", True)

            def scores(j):
                h, qb = j // 2, j % 2
                nk = P * (1 + qb)
                if j >= 2:
                    pe.wait_ge(score_read, j - 1)
                else:
                    pe.wait_ge(evac, CHUNKS["wo"])
                flat = psG[j % 2][:].rearrange("p t n -> p (t n)")
                for g in range(NG):
                    n = g * HPG + h
                    ins = pe.matmul(flat[:, g * nk:(g + 1) * nk], qT[:, n, qb * P:(qb + 1) * P], kT[:, n, 0:nk],
                                    start=True, stop=True)
                ins.then_inc(score_done, 1)

            def prob_transposes(j):
                h, qb = j // 2, j % 2
                u0 = UNITS["attn"] + 3 * h + qb
                pe.wait_ge(prob_ready, j + 1)
                for u in range(1 + qb):
                    pe.wait_ge(tr_free, max(UNITS["attn"], u0 + u - 2))
                    k0, k1 = (0, 3) if qb == 0 else ((0, 4), (4, 6))[u]
                    for k in range(k0, k1):
                        ins = pe.transpose(psT[qb + u][:, (k - k0) * P:(k - k0 + 1) * P],
                                           prob[j % 2][:, k * P:(k + 1) * P], ident[:])
                    ins.then_inc(tr_done, 1)

            def outputs(j):
                h, qb = j // 2, j % 2
                pe.wait_ge(tr_free, UNITS["attn"] + ATTN_UNITS[j])
                if h >= 1 and qb == 0:
                    pe.wait_ge(o_read, h)
                nb = NG * (1 + qb)
                for k in range(nb):
                    g, kb = k // (1 + qb), k % (1 + qb)
                    n = g * HPG + h
                    ins = pe.matmul(psM[:, qb * P:(qb + 1) * P], vv[:, kb, n * DH:(n + 1) * DH],
                                    probT[j % 2][:, k], start=k == 0, stop=k == nb - 1)
                ins.then_inc(o_done, 1)

            pe.wait_ge(tr_free, UNITS["attn"])
            pe.wait_ge(mod_ready, MODS["up1"])
            scores(0)
            scores(1)
            for j in range(2 * HPG):
                prob_transposes(j)
                if j + 2 < 2 * HPG:
                    scores(j + 2)
                outputs(j)
            broadcast_rows("gate2", 13)
            pe.wait_ge(o_read, HPG)
            for c in range(D // N):
                chunk(SLOTS["wo"] // 4 + c // 2, CHUNKS["wo"] + c, c % 2, r0=c % 2 * 2, slots=OW // P // 4)
            norm(4)
            pairs("up1", PAIRS_UP, 3, lambda i, j: i + MODS["up1"] if j == 0 else None)
            broadcast_rows("gate3", 17)
            ffn_down("down1", 1, None)


def _slots(w, order=None):
    k, n = w.shape
    t = w.reshape(k // (4 * P), 4, P, n // N, N).transpose(3, 0, 2, 1, 4)
    if order is not None:
        t = t[order]
    return t.reshape(-1, P, SLOT)


def _mod_slots(w):
    k, n = w.shape
    return w.reshape(k // (2 * P), 2, P, n // N, N).transpose(3, 0, 2, 1, 4).reshape(-1, P, MSLOT)


def _down_slots(w):
    return w.reshape(DFF // (2 * P), 2, P, 2, 2 * N).transpose(3, 0, 2, 1, 4).reshape(-1, P, SLOT)


def _pairs(n):
    return [c for i in range(n) for c in (i, n + i)]


def kernel(x, c, positions, mod_w, mod_b, norm_mix_g, norm_ffn_g, conv_pw1_w, conv_pw1_b, conv_dw_w, conv_dw_b,
           conv_ln_g, conv_ln_b, conv_pw2_w, conv_pw2_b, kv_mod_w, kv_mod_b, kv_norm_g, w_kv, k_norm_g, w_q,
           q_norm_g, w_o, ffn_up_w, ffn_dw_w, ffn_dw_b, ffn_down_w):
    import concourse.bacc as _bacc
    from concourse.bass_utils import run_bass_kernel_spmd as _run

    gate_first = [ch for i in range(PAIRS_PW1) for ch in (PAIRS_PW1 + i, i)]
    wstream = np.concatenate([
        _slots(conv_pw1_w[0], gate_first), _slots(conv_pw2_w[0]),
        _slots(ffn_up_w[0], _pairs(PAIRS_UP)), _down_slots(ffn_down_w[0]),
        _slots(w_kv), _slots(w_q[0]), _slots(w_o[0]),
        _slots(ffn_up_w[1], _pairs(PAIRS_UP)), _down_slots(ffn_down_w[1])])
    mstream = np.concatenate([_mod_slots(mod_w[0]), _mod_slots(kv_mod_w), _mod_slots(mod_w[1])])
    rows = [c, mod_b[0], kv_mod_b, mod_b[1], norm_mix_g, norm_ffn_g, kv_norm_g, conv_pw1_b, conv_dw_b, conv_ln_g,
            conv_ln_b, conv_pw2_b, k_norm_g, q_norm_g, conv_dw_w, ffn_dw_w, ffn_dw_b]
    rows = np.concatenate([r.reshape(-1, P) for r in rows] + [np.zeros((NRB * P - NROWS, P), np.float32)])
    assert wstream.shape[0] == NSLOTS and mstream.shape[0] == 8 * NMODS

    nc = _bacc.Bacc("TRN2", target_bir_lowering=False, num_devices=1, dynamic_dma_scratch_size=1024)
    arrays = {"wstream": wstream, "mstream": mstream, "x_in": np.ascontiguousarray(x[0]), "rows_in": rows,
              "pos_in": np.ascontiguousarray(positions.reshape(TB, P).T)}
    args = [nc.dram_tensor(n, a.shape, mybir.dt.from_np(a.dtype), kind="ExternalInput").ap()
            for n, a in arrays.items()]
    out = nc.dram_tensor("out", (1, S, D), mybir.dt.float32, kind="ExternalOutput").ap()
    build(nc, *args, out[0])
    r = _run(nc, [arrays], core_ids=[0])
    return r.results[0]["out"]
```

```python
from contextlib import ExitStack

import numpy as np

import concourse.bass as bass
from concourse import mybir

P = 128
D = 2048
S = 256
TB = S // P
DB = D // P
N = 512
DFF = 5632
FB = DFF // P
CONV_K = 31
V_TAPS = 15
TAPG = 4
FFN_K = 3
GROUPS = ((128, 1), (512, 4), (2048, 16))
NG = len(GROUPS)
HPG = 8
DH = 128
NH = NG * HPG
QW = NH * DH
OW = HPG * DH
ROT = DH // 4
HR = ROT // 2
THETA = 500000.0
EPS = 1e-6
NEG = -1e30
SCALE = 1.0 / float(np.sqrt(DH))

SLOT = 4 * N
PIECE = SLOT // 2
NP_ = 4
NRAW = 4
MSLOT = D // 2
NMRAW = 4
MPC = 8

KS = D // P // 4
PAIRS_PW1 = D // N
PAIRS_UP = DFF // N
DGROUPS = FB // 4
SLOTS = {}
CHUNKS = {}
_s = _c = 0
for _name, _chunks, _slots in (
        ("pw1", 2 * PAIRS_PW1, 2 * PAIRS_PW1 * KS), ("pw2", D // N, D // N * KS),
        ("up0", 2 * PAIRS_UP, 2 * PAIRS_UP * KS), ("down0", 4, 4 * DGROUPS),
        ("q", QW // N, QW // N * KS), ("k", QW // N, QW // N * KS), ("v", QW // N, QW // N * KS),
        ("wo", D // N, D // N * (OW // P // 4)),
        ("up1", 2 * PAIRS_UP, 2 * PAIRS_UP * KS), ("down1", 4, 4 * DGROUPS)):
    SLOTS[_name], CHUNKS[_name] = _s, _c
    _s += _slots
    _c += _chunks
NSLOTS, NCHUNKS = _s, _c

MODS = {"head": 0, "pw1": 8, "pw2": 16, "up0": 20, "down0": 31, "q": 41, "k": 44, "v": 47, "up1": 52}
NMODS = 56
MC0, MCKV, MC1 = 0, 6 * DB, 8 * DB

ROWS = {}
_r = 0
for _name, _n in (("c", DB), ("mod_b", 14 * DB), ("mix_g", 2 * DB), ("ffn_g", 2 * DB), ("kv_g", DB),
                  ("pw1_b", 2 * DB), ("dw_b", DB), ("ln_g", DB), ("ln_b", DB), ("pw2_b", DB),
                  ("head_g", 2), ("ffn_w", 2 * FFN_K * FB), ("ffn_b", 2 * FB), ("conv_w", CONV_K * DB)):
    ROWS[_name] = _r
    _r += _n
NROWS = _r
GROUPS_PB = (CONV_K - V_TAPS) // TAPG
CONV_GROUPS = 4 * GROUPS_PB
V_GROUPS = 4
NKEPT = ROWS["conv_w"]
NRB = -(-NROWS // P)

UNITS = {}
_u = 0
for _name, _n in (("table", -(-NRB // 4)), ("head_g", 1), ("c", 4), ("norm0", 8), ("pw1", 4 * PAIRS_PW1), ("ln", 2),
                  ("gate0", 4), ("bias0", 4), ("norm1", 8), ("up0", 4 * PAIRS_UP), ("gate1", 4),
                  ("norm2", 8), ("q", 10), ("norm3", 8), ("q_last", 2), ("k", 12), ("attn", 3 * HPG), ("gate2", 4),
                  ("norm4", 8), ("up1", 4 * PAIRS_UP), ("gate3", 4)):
    UNITS[_name] = _u
    _u += _n


def head_units(name, n):
    return UNITS["q_last"] if name == "q" and isinstance(n, int) and n == QW // N - 1 else n * 2 + UNITS[name]


AREA = 18432
A_HID, A_CONV, A_GATE = 0, 11264, 12288
A_Y, A_SIG, A_U, A_MU, A_RS, A_YC = 0, 4096, 5120, 6272, 6528, 8192
A_TRIG, A_CW = 2048, 14336
A_CWH, A_CWL, A_UH, A_UL, A_TAP = 14848, 15360, 12288, 15872, 8192
UPAD = CONV_K - 1
A_KT, A_V, A_QT = 0, 6144, 12288
A_H32, A_DIAG = 7168, 8192

ATTN_UNITS = [3 * (j // 2) + (1, 3)[j % 2] for j in range(2 * HPG)]
HO = 40

PI = float(np.pi)
PI_BELOW = 3.1415925
ROUND = 1.5 * 2.0 ** 23
TWO_PI = (6.28125, float(np.round((2 * np.pi - 6.28125) * 2.0 ** 20) / 2.0 ** 20))
TWO_PI += (float(2 * np.pi - TWO_PI[0] - TWO_PI[1]),)


def inv_freq():
    return np.power(np.float32(THETA), -np.arange(0, ROT, 2, dtype=np.float32) / np.float32(ROT)).astype(np.float32)


def build(nc, wstream, mstream, x_in, rows_in, pos_in, out):
    F32, F32R, I32 = mybir.dt.float32, mybir.dt.float32r, mybir.dt.int32
    ALU, ACT, AX = mybir.AluOpType, mybir.ActivationFunctionType, mybir.AxisListType.X

    with ExitStack() as ctx:
        def sb(name, shape, dt=F32):
            return ctx.enter_context(nc.sbuf_tensor(name, shape, dt))

        def pb(name, shape):
            return ctx.enter_context(nc.psum_tensor(name, shape, F32))

        def sem(name):
            return ctx.enter_context(nc.semaphore(name))

        raw = sb("raw", [P, NRAW, SLOT])
        mraw = sb("mraw", [P, NMRAW, MSLOT])
        whi = sb("whi", [P, NP_, PIECE], F32R)
        wlo = sb("wlo", [P, NP_, PIECE], F32R)
        hhi = sb("hhi", [P, DB, S], F32R)
        hlo = sb("hlo", [P, DB, S], F32R)
        x = sb("x", [P, TB, D])
        cbc = sb("cbc", [P, D])
        stage = sb("stage", [P, 2, TB, N])
        area_at = nc.sbuf_base
        area = sb("area", [P, AREA])

        def in_area(name, first, shape):
            return nc.alloc_sbuf_tensor_at(name, shape, F32R, offset=area_at + 4 * first)

        table = sb("table", [P, NKEPT])
        modcol = sb("modcol", [P, 14 * DB])
        halfsum = sb("halfsum", [P, 2, 4])
        ident = sb("ident", [P, P])
        ones = sb("ones", [P, P])
        headg = sb("headg", [P, 2, DH])
        cs = sb("cs", [P, 2, TB, HR])
        csil = sb("csil", [P, DB])
        nsh = sb("nsh", [P, DB])
        nsc = sb("nsc", [P, DB])
        small = sb("small", [P, 64])
        posi = sb("posi", [P, TB], I32)
        posf = sb("posf", [P, TB])

        psG = [pb(f"psG{i}", [P, TB, N]) for i in range(2)]
        psT = [pb(f"psT{i}", [P, N]) for i in range(3)]
        psM = pb("psM", [P, N])
        psC = [psM, psT[2]]

        raw_full = [sem(f"raw_full{i}") for i in range(NRAW)]
        mod_full = [sem(f"mod_full{i}") for i in range(NMRAW)]
        params_in = sem("params_in")
        x_loaded = sem("x_loaded")
        out_done = sem("out_done")
        const_ready = sem("const_ready")
        hi_ready = sem("hi_ready")
        lo_ready = sem("lo_ready")
        used = sem("used")
        mod_ops = sem("mod_ops")
        evac = sem("evac")
        tr_done = sem("tr_done")
        tr_free = sem("tr_free")
        csil_ready = sem("csil_ready")
        angle_ready = sem("angle_ready")
        trig_ready = sem("trig_ready")
        x_ready = sem("x_ready")
        ssq_ready = sem("ssq_ready")
        rdiag_ready = sem("rdiag_ready")
        cols_ready = sem("cols_ready")
        hhi_ready = sem("hhi_ready")
        hlo_ready = sem("hlo_ready")
        conv_ready = sem("conv_ready")
        convw_hi = sem("convw_hi")
        convw_lo = sem("convw_lo")
        u_ready = sem("u_ready")
        u_hi = sem("u_hi")
        u_lo = sem("u_lo")
        taps_ready = sem("taps_ready")
        vtaps_ready = sem("vtaps_ready")
        taps_used = sem("taps_used")
        silu_ready = sem("silu_ready")
        diag_ready = sem("diag_ready")
        ln_step = sem("ln_step")
        ln_sq = sem("ln_sq")
        ln_std = sem("ln_std")
        hid_hi = sem("hid_hi")
        hid_lo = sem("hid_lo")
        head_ssq = sem("head_ssq")
        head_std = sem("head_std")
        head_ready = sem("head_ready")
        iota_ready = sem("iota_ready")
        dil_ready = sem("dil_ready")
        mask_ready = sem("mask_ready")
        score_done = sem("score_done")
        score_read = sem("score_read")
        max_ready = sem("max_ready")
        exp_ready = sem("exp_ready")
        prob_ready = sem("prob_ready")
        o_done = sem("o_done")
        o_read = sem("o_read")

        h32 = area[:, A_H32:A_H32 + 2 * N].rearrange("p (u b s) -> p u b s", u=2, b=2)
        rdiag = area[:, A_DIAG:A_DIAG + TB * P].rearrange("p (t c) -> p t c", t=TB)
        hidden = area[:, A_HID:A_HID + FB * S].rearrange("p (b s) -> p b s", s=S)
        squared = area[:, A_CONV:A_CONV + TB * N].rearrange("p (t n) -> p t n", t=TB)
        convb = area[:, A_CONV:A_CONV + 4 * S].rearrange("p (b s) -> p b s", s=S)
        gate = area[:, A_GATE:A_GATE + D]
        yln = area[:, A_Y:A_Y + DB * S].rearrange("p (b s) -> p b s", s=S)
        sigb = area[:, A_SIG:A_SIG + 4 * S].rearrange("p (b s) -> p b s", s=S)
        upad = area[:, A_U:A_U + 4 * (S + UPAD)].rearrange("p (b s) -> p b s", b=4)
        mu = area[:, A_MU:A_MU + S]
        rs = area[:, A_RS:A_RS + S]
        ysq = area[:, A_YC:A_YC + DB * S].rearrange("p (b s) -> p b s", s=S)
        kT = area[:, A_KT:A_KT + NH * S].rearrange("p (n s) -> p n s", s=S)
        vv = area[:, A_V:A_V + TB * QW].rearrange("p (t n) -> p t n", t=TB)
        qT = area[:, A_QT:A_QT + NH * S].rearrange("p (n s) -> p n s", s=S)
        diag = stage[:, 0].rearrange("p t (b c) -> p (t b) c", c=P)
        NKEY = [NG * P, NG * S]
        masks = [stage[:, 0].rearrange("p t n -> p (t n)")[:, 0:NKEY[1]],
                 stage[:, 1].rearrange("p t n -> p (t n)")[:, 0:NKEY[0]]]
        mask1, mask0 = masks
        attn = mraw[:].rearrange("p a b -> p (a b)")
        prob = [attn[:, i * NKEY[1]:(i + 1) * NKEY[1]] for i in range(3)]
        probT = [attn[:, (3 + i) * NKEY[1]:(4 + i) * NKEY[1]].rearrange("p (b q) -> p b q", q=P) for i in range(2)]
        eps_c, ssq, rstd = small[:, 0:1], small[:, 2:4], small[:, 4:6]
        ssq_parts = small[:, 40:48].rearrange("p (t c) -> p t c", t=TB)
        hss, hsd, hrs = small[:, 8:16], small[:, 16:24], small[:, 24:32]
        mx, nmx, den, rden = small[:, 32:34], small[:, 34:36], small[:, 36:38], small[:, 38:40]
        trig = area[:, A_TRIG:A_TRIG + 8 * TB * HR].rearrange("p (k t f) -> p k t f", k=8, t=TB)
        convw = area[:, A_CW:A_CW + NRB * P - NKEPT]
        cwhi = area[:, A_CWH:A_CWH + NRB * P - NKEPT].bitcast(F32R)
        cwlo = area[:, A_CWL:A_CWL + NRB * P - NKEPT]
        uhi, ulo = (in_area(name, a, [P, 4, S + UPAD]) for name, a in (("uhi", A_UH), ("ulo", A_UL)))
        tapd = in_area("tapd", A_TAP, [P, 4, 2, TAPG, P])

        tbl_in = area[:, 0:NRB * P]

        def col(name, i):
            return table[:, ROWS[name] + i:ROWS[name] + i + 1]

        def cols(name, i=0, n=DB):
            return table[:, ROWS[name] + i:ROWS[name] + i + n]

        NORMS = [("mix_g", 0, MC0, MC0 + DB, 8),
                 ("ffn_g", 0, MC0 + 3 * DB, MC0 + 4 * DB, 20),
                 ("mix_g", DB, MC1, MC1 + DB, 40),
                 ("kv_g", 0, MCKV, MCKV + DB, 32),
                 ("ffn_g", DB, MC1 + 3 * DB, MC1 + 4 * DB, 52)]
        HB = [0, 16, 24, 32, 48]
        HL = [0, 16, 24, 32, 40]
        LNH = 8
        DIAGONALS = {name: 1 + 4 * k for k, name in enumerate(("c", "gate0", "bias0", "gate1", "gate2", "gate3"))}
        XB = {"pw2": 0, "down0": 4, "wo": 8, "down1": 12}
        ROOT = [1, 2, 3, 3, 4]

        block = ctx.enter_context(nc.Block())

        @block.sync
        def _(sp):
            sp.dma_start(tbl_in.rearrange("p (b c) -> p b c", c=P), rows_in.rearrange("(b p) c -> p b c", p=P)
                         ).then_inc(params_in, 16)
            sp.dma_start(posi[:], pos_in).then_inc(params_in, 16)

            def w_slot(rnd, r):
                if not (isinstance(rnd, int) and rnd == 0):
                    sp.wait_ge(lo_ready, ((rnd - 1) * NRAW + r + 1) * 2)
                sp.dma_start(raw[:, r], wstream[rnd * NRAW + r]).then_inc(raw_full[r], 16)

            def m_chunk(m, part=range(8)):
                for u in part:
                    if not (isinstance(m, int) and m * MPC + u < NMRAW):
                        sp.wait_ge(mod_ops, m * (MPC + 1) + (u - NMRAW + 1))
                    sp.dma_start(mraw[:, u % NMRAW], mstream[m * MPC + u]).then_inc(mod_full[u % NMRAW], 16)

            def first_chunk(rnd, mod):
                for k in range(KS):
                    w_slot(rnd, k)
                if mod is not None:
                    m_chunk(mod)

            def chunk(rnd, mod=None):
                for k in range(KS):
                    w_slot(rnd, k)
                    if mod is not None:
                        m_chunk(mod, ((0, 1, 2, 3), (4, 5), (6, 7), ())[k])

            m_chunk(0, range(4))
            for k in range(KS):
                w_slot(0, k)
            m_chunk(0, range(4, 8))
            sp.dma_start(x[:], x_in.rearrange("(t p) d -> p t d", p=P)).then_inc(x_loaded, 16)
            with sp.Fori(1, MODS["pw1"]) as m:
                m_chunk(m)

            def chunks(name, n, mods):
                def one(i, j):
                    chunk(i * 2 + (SLOTS[name] // 4 + j), mods(i, j))
                if name == "pw1":
                    m_chunk(mods(0, 0))
                else:
                    first_chunk(SLOTS[name] // 4, mods(0, 0))
                one(0, 1)
                with sp.Fori(1, n) as i:
                    one(i, 0)
                    one(i, 1)

            chunks("pw1", PAIRS_PW1, lambda i, j: i * 2 + (MODS["pw1"] + j))
            first_chunk(SLOTS["pw2"] // 4, MODS["pw2"])
            for k in range(1, D // N):
                chunk(SLOTS["pw2"] // 4 + k, MODS["pw2"] + k)
            chunks("up0", PAIRS_UP, lambda i, j: i + MODS["up0"] if j == 0 else None)

            def down(name, m0):
                for half in range(2):
                    base = SLOTS[name] + half * 2 * DGROUPS

                    def group(g_rnd, r, mod, part):
                        w_slot(g_rnd, r)
                        if mod is not None:
                            m_chunk(mod, part[:2])
                        w_slot(g_rnd + (r + 1) // 4, (r + 1) % 4)
                        if mod is not None:
                            m_chunk(mod, part[2:])

                    def two(i, m):
                        group(i + (base + 2) // 4, (base + 2) % 4, m, (0, 1, 2, 3))
                        group(i + (base + 4) // 4, (base + 4) % 4, m, (4, 5, 6, 7))

                    group(base // 4, base % 4, None, ())
                    with sp.Fori(0, 4) as i:
                        two(i, None if m0 is None else i + (m0 + 5 * half))
                    two(4, None if m0 is None else m0 + 5 * half + 4)

            down("down0", MODS["down0"])
            chunks("q", 3, lambda i, j: i + MODS["q"] if j == 1 else None)
            chunks("k", 3, lambda i, j: i + MODS["k"] if j == 1 else None)
            chunk(SLOTS["v"] // 4, MODS["v"])
            chunk(SLOTS["v"] // 4 + 1)
            with sp.Fori(1, 3) as i:
                for j in range(2):
                    chunk(i * 2 + (SLOTS["v"] // 4 + j), i * 2 + (MODS["v"] - 1 + j))
            for rnd in range(SLOTS["wo"] // 4, SLOTS["up1"] // 4):
                for r in range(4):
                    w_slot(rnd, r)
            r1 = SLOTS["up1"] // 4
            for i in range(4):
                if i == 0:
                    first_chunk(r1, None)
                    sp.wait_ge(tr_done, UNITS["attn"] + 3 * HPG)
                    sp.wait_ge(o_done, 2 * HPG)
                    m_chunk(MODS["up1"])
                else:
                    chunk(r1 + 2 * i, MODS["up1"] + i)
                chunk(r1 + 2 * i + 1)
            with sp.Fori(4, PAIRS_UP) as i:
                chunk(i * 2 + r1)
                chunk(i * 2 + (r1 + 1))
            down("down1", None)
            for c in range(D // N):
                sp.wait_ge(x_ready, XB["down1"] + c + 1)
                sp.dma_start(out.rearrange("(t p) d -> p t d", p=P)[:, :, c * N:(c + 1) * N],
                             x[:, :, c * N:(c + 1) * N]).then_inc(out_done, 16)
            sp.wait_ge(out_done, 16 * (D // N))

        @block.gpsimd
        def _(pool):
            pool.memset(ident[:], 0.0).then_inc(const_ready, 1)
            pool.memset(ones[:], 1.0).then_inc(const_ready, 1)
            pool.wait_ge(const_ready, 1)
            pool.affine_select(out=ident[:], in_=ident[:], compare_op=ALU.not_equal, fill=1.0, base=0,
                               pattern=[[-1, P]], channel_multiplier=1).then_inc(const_ready, 1)
            pool.wait_ge(tr_done, UNITS["k"] + 12)
            pool.iota(mask1.bitcast(I32).rearrange("p (g s) -> p g s", g=NG), pattern=[[0, NG], [-1, S]],
                      base=P, channel_multiplier=1).then_inc(iota_ready, 1)
            pool.iota(mask0.bitcast(I32).rearrange("p (g s) -> p g s", g=NG), pattern=[[0, NG], [-1, P]],
                      base=0, channel_multiplier=1).then_inc(iota_ready, 1)
            pool.wait_ge(dil_ready, 2)
            for n, (mk, keys, base) in enumerate(((mask1, S, P), (mask0, P, 0))):
                v = mk.rearrange("p (g s) -> p g s", g=NG)
                pool.affine_select(out=v, in_=v, compare_op=ALU.is_ge, fill=NEG, base=base,
                                   pattern=[[0, NG], [-1, keys]], channel_multiplier=1).then_inc(mask_ready, 1)
            pool.wait_ge(mask_ready, 1)
            pool.affine_select(out=mask1[:, 0:S], in_=mask1[:, 0:S], compare_op=ALU.is_ge, fill=NEG,
                               base=GROUPS[0][0] // GROUPS[0][1] - P, pattern=[[1, S]],
                               channel_multiplier=-1).then_inc(mask_ready, 1)

        @block.scalar
        def _(act):
            def hi(rnd, r, h):
                if h == 0:
                    act.wait_ge(raw_full[r], (rnd + 1) * 16)
                if not (isinstance(rnd, int) and rnd == 0 and r < 2):
                    act.wait_ge(used, rnd * 8 + (2 * r + h - 3))
                act.activation(whi[:, (2 * r + h) % NP_], raw[:, r, h * PIECE:(h + 1) * PIECE],
                               ACT.Copy).then_inc(hi_ready, 1)

            def ahead(rnd):
                for q in range(NP_):
                    hi(rnd, q // 2, q % 2)

            def preload(function):
                act.activation(small[:, 1:2], eps_c, function)

            def squares(c, ready):
                if ready:
                    act.wait_ge(x_ready, ready)
                act.drain()
                for t in range(TB):
                    act.activation(squared[:, t], x[:, t, c * N:(c + 1) * N], ACT.Square,
                                   accum_out=ssq_parts[:, t, c:c + 1])

            def root():
                act.drain()
                for t in range(TB):
                    act.activation(squared[:, t, 0:D // N], ssq_parts[:, t], ACT.Copy, accum_out=ssq[:, t:t + 1])
                act.drain()
                act.activation(ssq, ssq, ACT.Sqrt, bias=eps_c, scale=1.0 / D).then_inc(ssq_ready, 1)

            def norm_chunk(n, rnd, work=None):
                act.wait_ge(cols_ready, n + 1)
                for u in range(8):
                    if u >= 2:
                        act.wait_ge(hlo_ready, HL[n] + u - 1)
                    act.wait_ge(tr_done, UNITS[f"norm{n}"] + u + 1)
                    for b in range(2):
                        k = 2 * u + b
                        ins = act.activation(h32[:, u % 2, b], psT[u % 3][:, b * S:(b + 1) * S], ACT.Identity,
                                             bias=nsh[:, k:k + 1], scale=nsc[:, k:k + 1])
                    ins.then_inc(tr_free, 1)
                    act.drain()
                    act.activation(hhi[:, 2 * u:2 * u + 2], h32[:, u % 2], ACT.Copy).then_inc(hhi_ready, 1)
                    if 3 <= u < 7:
                        hi(rnd, (u + 1) // 2, (u + 1) % 2)
                    if work and u in work:
                        work[u]()

            def evac_stage(par, c, units_before):
                act.wait_ge(used, units_before[0] * 2)
                act.wait_ge(tr_done, units_before[1])
                act.activation(stage[:, par], psG[par][:], ACT.Copy).then_inc(evac, 1)

            def chunk(rnd, prev_evac=None, prev_mid=None, prev_late=None, each=None):
                for q in range(2 * KS):
                    hi(rnd, q // 2, q % 2)
                    if q == 3 and prev_evac:
                        prev_evac()
                    if q == 5 and prev_mid:
                        prev_mid()
                    if each:
                        each(q)
                if prev_late:
                    prev_late()

            def gate_row(unit, k):
                act.wait_ge(tr_done, UNITS[unit] + k + 1)
                act.activation(gate[:, k * N:(k + 1) * N], psT[k % 3][:], ACT.Copy).then_inc(tr_free, 1)

            act.wait_ge(tr_free, UNITS["head_g"])
            act.activation(csil[:], cols("c"), ACT.Silu).then_inc(csil_ready, 1)
            act.wait_ge(angle_ready, 1)
            act.activation(cs[:], trig[:, 0:2], ACT.Sin).then_inc(trig_ready, 1)
            for k in range(4):
                act.wait_ge(tr_done, UNITS["c"] + k + 1)
                act.activation(cbc[:, k * N:(k + 1) * N], psT[k % 3][:], ACT.Copy).then_inc(tr_free, 1)
            ahead(0)
            act.wait_ge(x_loaded, 16)
            for c in range(D // N):
                squares(c, None)
            root()

            act.activation(cwhi, convw, ACT.Copy).then_inc(convw_hi, 1)

            def conv_input(i):
                act.wait_ge(u_ready, i + 1)
                act.wait_ge(taps_used, i * CONV_GROUPS + CONV_GROUPS)
                act.activation(uhi[:], upad, ACT.Copy).then_inc(u_hi, 1)

            def tap_diagonals(i, groups):
                for g in groups:
                    act.wait_ge(taps_used, i * CONV_GROUPS + (CONV_GROUPS + g - 3))
                    b, j0 = g // GROUPS_PB, V_TAPS + g % GROUPS_PB * TAPG
                    for part, cw in enumerate((cwhi.bitcast(F32), cwlo)):
                        for j in range(TAPG):
                            ins = act.activation(tapd[:, g % 4, part, j], ident[:], ACT.Copy,
                                                 scale=cw[:, bass.ds(i * 4 + ((j0 + j) * DB + b), 1)])
                    ins.then_inc(taps_ready, 1)

            r0, u0, c0 = SLOTS["pw1"] // 4, UNITS["pw1"], CHUNKS["pw1"]

            def sigmoid(i):
                for u in range(2):
                    act.wait_ge(tr_done, i * 4 + (u0 + u + 1))
                    for b in range(2):
                        ins = act.activation(sigb[:, 2 * u + b], psT[u][:, b * S:(b + 1) * S], ACT.Sigmoid,
                                             bias=table[:, bass.ds(i * 4 + (ROWS["pw1_b"] + DB + 2 * u + b), 1)])
                    ins.then_inc(tr_free, 1)

            def pw1_pair(i, first):
                if first:
                    norm_chunk(0, r0)
                else:
                    chunk(i * 2 + r0, lambda: evac_stage(1, None, ((i * 2 + r0) * 4, i * 4 + (u0 - 4))))
                    conv_input(i - 1)
                chunk(i * 2 + (r0 + 1),
                      lambda: evac_stage(0, None, ((i * 2 + r0 + 1) * 4, i * 4 + (u0 - 2) if not first else u0)),
                      each=None if first else lambda q: tap_diagonals(i - 1, (2 * q, 2 * q + 1)))
                sigmoid(i)

            pw1_pair(0, True)
            act.wait_ge(convw_lo, 1)
            with act.Fori(1, PAIRS_PW1) as i:
                pw1_pair(i, False)
            evac_stage(1, None, (SLOTS["pw2"], UNITS["ln"] - 4))
            conv_input(PAIRS_PW1 - 1)
            tap_diagonals(PAIRS_PW1 - 1, range(CONV_GROUPS - V_GROUPS))

            for b in range(0, DB, 4):
                act.wait_ge(ln_step, b // 4 + 1)
                act.activation(ysq[:, b:b + 4], yln[:, b:b + 4], ACT.Square).then_inc(ln_sq, 1)
            r0 = SLOTS["pw2"] // 4
            ahead(r0)
            act.wait_ge(ln_step, 5)
            act.activation(rs, rs, ACT.Sqrt, bias=eps_c).then_inc(ln_std, 1)
            for u in range(8):
                act.wait_ge(ln_step, 5 + u // 2 + 1)
                z = ysq[:, 2 * u:2 * u + 2]
                for b in range(2):
                    act.activation(z[:, b], yln[:, 2 * u + b], ACT.Silu, bias=col("ln_b", 2 * u + b),
                                   scale=col("ln_g", 2 * u + b))
                act.drain()
                act.activation(hhi[:, 2 * u:2 * u + 2], z, ACT.Copy).then_inc(hhi_ready, 1)
                if 3 <= u < 7:
                    hi(r0, (u + 1) // 2, (u + 1) % 2)
                if u == 7:
                    gate_row("gate0", 0)
            chunk(r0 + 1, each=lambda q: gate_row("gate0", q + 1) if q < 3 else None)
            for c in range(2, D // N):
                chunk(r0 + c, prev_late=lambda: squares(c - 2, XB["pw2"] + c - 1))
            ahead(SLOTS["up0"] // 4)
            preload(ACT.Sqrt)
            for c in (2, 3):
                squares(c, XB["pw2"] + c + 1)
            root()

            def ffn_up(name, n):
                r0, u0 = SLOTS[name] // 4, UNITS[name]

                def silu(i):
                    act.wait_ge(tr_free, i * 4 + (u0 + 2))
                    act.activation(convb, convb, ACT.Silu).then_inc(silu_ready, 1)

                def pair(i, first):
                    if first:
                        norm_chunk(n, r0)
                    else:
                        chunk(i * 2 + r0, lambda: (silu(i - 1), evac_stage(1, None, (
                            (i * 2 + r0) * 4, i * 4 + (u0 - 4)))))
                    chunk(i * 2 + (r0 + 1),
                          lambda: evac_stage(0, None, ((i * 2 + r0 + 1) * 4, u0 if first else i * 4 + (u0 - 2))))

                pair(0, True)
                with act.Fori(1, PAIRS_UP) as i:
                    pair(i, False)
                return (lambda: silu(PAIRS_UP - 1),
                        lambda: evac_stage(1, None, ((r0 + 2 * PAIRS_UP) * 4, u0 + 4 * PAIRS_UP - 4)))

            def ffn_down(name, layer, up_last):
                for half in range(2):
                    base = SLOTS[name] + half * 2 * DGROUPS
                    gb = half * DGROUPS
                    gall = layer * 2 * DGROUPS + gb

                    def group(i, g, rows={}):
                        s0 = base + 2 * g
                        ring = (gb + g) % 2
                        start = half == 0 and isinstance(i, int) and g == 0
                        if start:
                            act.wait_ge(used, 2 * SLOTS[name] - 6)
                        elif not (half == 0 and isinstance(i, int) and g + 2 * i < 2):
                            act.wait_ge(used, (i * 4 + (s0 - 2)) * 2)
                        act.activation(hhi[:, 4 * ring:4 * ring + 4],
                                       hidden[:, bass.ds(i * 8 + 4 * g, 4)], ACT.Copy).then_inc(hid_hi, 1)
                        if start:
                            up_last[0]()
                        for q in range(4):
                            if start and q == 3:
                                up_last[1]()
                            sl = s0 + q // 2
                            hi(i + sl // 4, sl % 4, q % 2)
                            if q in rows:
                                gate_row(("gate1", "gate3")[layer], rows[q])

                    group(0, 0)
                    if half == 0:
                        act.wait_ge(silu_ready, (layer + 1) * (PAIRS_UP + 1))
                        group(0, 1, {2: 0, 3: 1})
                        group(0, 2, {0: 2, 1: 3})
                    elif layer == 0:
                        for c in range(2):
                            squares(c, XB[name] + c + 1)
                    with act.Fori(1 - half, 4) as i:
                        group(i, 1)
                        group(i, 2)
                    group(4, 1)
                    group(4, 2)

            ffn_down("down0", 0, ffn_up("up0", 1))
            ahead(SLOTS["q"] // 4)
            preload(ACT.Sqrt)
            for c in (2, 3):
                squares(c, XB["down0"] + c + 1)
            root()

            def heads_root(n):
                act.wait_ge(head_ssq, n + 1)
                act.activation(hsd, hss, ACT.Sqrt, bias=eps_c, scale=1.0 / DH).then_inc(head_std, 1)

            def heads_evac(name, slots_done, n, par):
                act.wait_ge(used, slots_done * 2)
                act.wait_ge(tr_done, UNITS[name] + (n - (0 if name == "q" else QW // N)) * 2)
                act.activation(stage[:, 0], psG[par][:], ACT.Copy)
                act.activation(stage[:, 1], psG[par][:], ACT.Square).then_inc(evac, 1)

            def heads_out(name, n):
                dst = kT if name == "k" else qT
                for u in range(2):
                    act.wait_ge(tr_done, head_units(name, n) + u + 1)
                    act.activation(dst[:, bass.ds(n * 4 + 2 * u, 2)], psT[u][:].rearrange("p (b s) -> p b s", s=S),
                                   ACT.Copy).then_inc(tr_free, 1)

            def heads_work(name, n, par, slots_done):
                base = 0 if name == "q" else QW // N
                return (lambda: heads_evac(name, slots_done, n + base, par), lambda: heads_root(n + base),
                        lambda: heads_out(name, n))

            def heads_chunk(name, n, par):
                rnd = n + SLOTS[name] // 4
                chunk(rnd, *heads_work(name, n - 1, 1 - par, rnd * 4))

            def heads(name):
                heads_chunk(name, 1, 1)
                with act.Fori(1, 3) as i:
                    for j in range(2):
                        heads_chunk(name, i * 2 + j, j)

            def v_evac(slots_done, n, par):
                act.wait_ge(used, slots_done * 2)
                act.activation(vv[:, :, bass.ds(n * N, N)], psG[par][:], ACT.Copy).then_inc(evac, 1)

            norm_chunk(2, SLOTS["q"] // 4)
            heads("q")
            ahead(SLOTS["k"] // 4)
            last = heads_work("q", QW // N - 1, 1, SLOTS["k"])
            norm_chunk(3, SLOTS["k"] // 4, {3: last[0], 5: last[1], 7: last[2]})
            heads("k")
            r0 = SLOTS["v"] // 4

            def v_chunk(n, par):
                chunk(n + r0, lambda: v_evac((n + r0) * 4, n - 1, 1 - par))

            chunk(r0, *heads_work("k", QW // N - 1, 1, SLOTS["v"]))
            v_chunk(1, 1)
            with act.Fori(1, 3) as i:
                for j in range(2):
                    v_chunk(i * 2 + j, j)
            preload(ACT.Exp)
            v_evac(SLOTS["wo"], 5, 1)

            def prob_out(j):
                h, qb = j // 2, j % 2
                for u in range(1 + qb):
                    act.wait_ge(tr_done, UNITS["attn"] + 3 * h + qb + u + 1)
                    if u == 0 and j >= 2:
                        act.wait_ge(o_done, j - 1)
                    k0, k1 = (0, 3) if qb == 0 else ((0, 4), (4, 6))[u]
                    act.activation(probT[j % 2][:, k0:k1].rearrange("p b q -> p (b q)"),
                                   psT[qb + u][:, 0:(k1 - k0) * P], ACT.Copy).then_inc(tr_free, 1)

            def o_split(h):
                act.wait_ge(o_done, 2 * h + 2)
                act.activation(hhi[:, h], psM[:, 0:S], ACT.Copy).then_inc(hhi_ready, 1)

            for j in range(2 * HPG + 1):
                if j < 2 * HPG:
                    act.wait_ge(max_ready, j + 1)
                    w = NKEY[j % 2]
                    act.activation(prob[j % 3][:, 0:w], prob[j % 3][:, 0:w], ACT.Exp, bias=nmx[:, j % 2:j % 2 + 1],
                                   scale=SCALE, accum_out=den[:, j % 2:j % 2 + 1]).then_inc(exp_ready, 1)
                if j >= 1:
                    prob_out(j - 1)
                if j >= 3 and j % 2 == 1:
                    o_split((j - 3) // 2)
            o_split(HPG - 1)

            r0 = SLOTS["wo"] // 4
            for c in range(D // N):
                for q in range(4):
                    hi(r0 + c // 2, c % 2 * 2 + q // 2, q % 2)
                    if q == 1 and c >= 2:
                        squares(c - 2, XB["wo"] + c - 1)
                    k = 4 * c + q - 2
                    if 0 <= k < 4:
                        gate_row("gate2", k)
            ahead(SLOTS["up1"] // 4)
            preload(ACT.Sqrt)
            for c in (2, 3):
                squares(c, XB["wo"] + c + 1)
            root()
            ffn_down("down1", 1, ffn_up("up1", 4))

        @block.vector
        def _(dve):
            TT, TS, STT = dve.tensor_tensor, dve.tensor_scalar, dve.scalar_tensor_tensor

            def lo(rnd, r, h):
                dve.wait_ge(hi_ready, rnd * 8 + (2 * r + h + 1))
                q = (2 * r + h) % NP_
                TT(wlo[:, q], raw[:, r, h * PIECE:(h + 1) * PIECE], whi[:, q].bitcast(F32),
                   ALU.subtract).then_inc(lo_ready, 1)

            def mod_mul(m, part):
                for u in part:
                    dve.wait_ge(mod_full[u % NMRAW], m * 32 + 16 * (u // NMRAW + 1))
                    if u == 0 and not (isinstance(m, int) and m == 0):
                        dve.wait_ge(mod_ops, m * (MPC + 1))
                    half = u % 4 // 2
                    w, total = mraw[:, u % NMRAW], u // 4 * 2 + u % 2
                    STT(w, w, 1.0, cbc[:, half * MSLOT:(half + 1) * MSLOT], ALU.mult, ALU.mult,
                        accum_out=halfsum[:, half, total:total + 1]).then_inc(mod_ops, 1)
                if MPC - 1 in part:
                    dve.wait_ge(mod_ops, m * (MPC + 1) + MPC)
                    TT(modcol[:, bass.ds(m * 4, 4)], halfsum[:, 0], halfsum[:, 1], ALU.add).then_inc(mod_ops, 1)

            def chunk(rnd, work=None, mod=None):
                for q in range(2 * KS):
                    lo(rnd, q // 2, q % 2)
                    if work and q in work:
                        work[q]()
                    if mod is not None and q < 7:
                        mod_mul(mod, (0, 1) if q == 0 else (q + 1,))

            def ahead(rnd, pieces=range(NP_)):
                for q in pieces:
                    lo(rnd, q // 2, q % 2)

            def norm_columns(n):
                gain, g0, sh, sc, chunks_needed = NORMS[n]
                dve.wait_ge(mod_ops, (MPC + 1) * chunks_needed)
                TT(nsc[:], modcol[:, sc:sc + DB], cols("mod_b", sc), ALU.add)
                TT(nsh[:], modcol[:, sh:sh + DB], cols("mod_b", sh), ALU.add)
                dve.drain()
                STT(nsc[:], nsc[:], 1.0, cols(gain, g0), ALU.add, ALU.mult).then_inc(cols_ready, 1)

            def root_diagonals(n):
                dve.wait_ge(ssq_ready, n)
                dve.reciprocal(rstd, ssq)
                dve.drain()
                for t in range(TB):
                    ins = TS(rdiag[:, t], ident[:], rstd[:, t:t + 1], None, ALU.mult)
                ins.then_inc(rdiag_ready, 1)

            def norm_chunk(n, rnd, mod=None, work=None):
                for u in range(8):
                    dve.wait_ge(hhi_ready, HB[n] + u + 1)
                    TT(hlo[:, 2 * u:2 * u + 2], h32[:, u % 2], hhi[:, 2 * u:2 * u + 2].bitcast(F32),
                       ALU.subtract).then_inc(hlo_ready, 1)
                    if 3 <= u < 7:
                        lo(rnd, (u + 1) // 2, (u + 1) % 2)
                    if mod is not None and u >= 1:
                        mod_mul(mod, (u - 1,))
                    if work and u in work:
                        work[u]()
                if mod is not None:
                    mod_mul(mod, (7,))
                dve.drain()

            def diagonal(vec, unit, k):
                if k >= 2:
                    dve.wait_ge(tr_done, UNITS[unit] + k - 1)
                for b in range(4):
                    ins = TS(diag[:, 4 * (k % 2) + b], ident[:], vec[:, 4 * k + b:4 * k + b + 1], None, ALU.mult)
                ins.then_inc(diag_ready, 1)

            def gate_cols(g, chunks_needed):
                dve.wait_ge(mod_ops, (MPC + 1) * chunks_needed)
                TT(nsh[:], modcol[:, g:g + DB], cols("mod_b", g), ALU.add)
                dve.drain()

            def residual(chunks, slots_done):
                dve.wait_ge(used, slots_done * 2)
                tmp = [stage[:, 2 - len(chunks) + k] for k in range(len(chunks))]
                for k, (par, col0) in enumerate(chunks):
                    for t in range(TB):
                        ins = TT(tmp[k][:, t], psG[par][:, t], gate[:, col0:col0 + N], ALU.mult)
                    ins.then_inc(evac, 1)
                dve.drain()
                for k, (_, col0) in enumerate(chunks):
                    xs = x[:, :, col0:col0 + N]
                    TT(xs, xs, tmp[k], ALU.add).then_inc(x_ready, 1)
                dve.drain()

            dve.memset(eps_c, EPS)
            freq = inv_freq()
            for i in range(HR):
                dve.memset(trig[:, 7, :, i:i + 1], float(freq[i]))
            for u in range(UNITS["head_g"]):
                dve.wait_ge(tr_done, u + 1)
                k0, k1 = 4 * u * P, min(4 * u + 4, NRB) * P
                if k0 < NKEPT < k1:
                    dve.tensor_copy(convw[:, 0:k1 - NKEPT], psT[u][:, NKEPT - k0:k1 - k0])
                if k0 < NKEPT:
                    dve.tensor_copy(table[:, k0:min(k1, NKEPT)], psT[u][:, 0:min(k1, NKEPT) - k0]).then_inc(tr_free, 1)
                else:
                    dve.tensor_copy(convw[:, k0 - NKEPT:k1 - NKEPT], psT[u][:, 0:k1 - k0]).then_inc(tr_free, 1)
            dve.drain()
            dve.wait_ge(const_ready, 3)
            for i in range(2):
                ins = TS(headg[:, i], ident[:], col("head_g", i), None, ALU.mult)
            ins.then_inc(diag_ready, 1)
            dve.wait_ge(tr_done, UNITS["head_g"] + 1)
            dve.tensor_copy(headg[:], psT[0][:, 0:2 * DH].rearrange("p (a b) -> p a b", a=2)).then_inc(tr_free, 1)
            dve.wait_ge(csil_ready, 1)
            for k in range(4):
                diagonal(csil, "c", k)
            k_, r_, a_, b_ = trig[:, 4], trig[:, 1], trig[:, 2], trig[:, 3]
            dve.wait_ge(params_in, 32)
            dve.tensor_copy(posf[:], posi[:])
            dve.drain()
            for t in range(TB):
                TS(a_[:, t], trig[:, 7, t], posf[:, t:t + 1], None, ALU.mult)
            dve.drain()
            TS(b_, a_, 1.0 / (2 * PI), ROUND, ALU.mult, ALU.add)
            dve.drain()
            TS(k_, b_, ROUND, None, ALU.subtract)
            dve.drain()
            STT(b_, k_, -TWO_PI[0], a_, ALU.mult, ALU.add)
            dve.drain()
            STT(a_, k_, -TWO_PI[1], b_, ALU.mult, ALU.add)
            dve.drain()
            STT(b_, k_, -TWO_PI[2], a_, ALU.mult, ALU.add)
            dve.drain()
            TS(r_, b_, PI_BELOW, -PI_BELOW, ALU.min, ALU.max)
            TS(a_, b_, PI / 2, None, ALU.add)
            dve.drain()
            TS(k_, a_, PI, -2 * PI, ALU.is_gt, ALU.mult)
            dve.drain()
            TT(b_, a_, k_, ALU.add)
            dve.drain()
            TS(trig[:, 0], b_, PI_BELOW, -PI_BELOW, ALU.min, ALU.max).then_inc(angle_ready, 1)
            dve.wait_ge(trig_ready, 1)
            dve.wait_ge(tr_free, UNITS["c"] + 4)

            mod_mul(0, range(8))
            with dve.Fori(1, MODS["pw1"]) as m:
                mod_mul(m, range(8))
            ahead(0)
            norm_columns(0)
            root_diagonals(1)

            dve.wait_ge(convw_hi, 1)
            TT(cwlo, convw, cwhi.bitcast(F32), ALU.subtract).then_inc(convw_lo, 1)

            r0, u0 = SLOTS["pw1"] // 4, UNITS["pw1"]
            dve.memset(upad[:, :, 0:UPAD], 0.0)
            dve.drain()

            def glu(i):
                dve.wait_ge(tr_free, i * 4 + (u0 + 2))
                for u in range(2):
                    dve.wait_ge(tr_done, i * 4 + (u0 + 2 + u + 1))
                    for b in range(2):
                        k = 2 * u + b
                        ins = STT(upad[:, k, UPAD:UPAD + S], psT[u][:, b * S:(b + 1) * S],
                                  table[:, bass.ds(i * 4 + (ROWS["pw1_b"] + k), 1)], sigb[:, k], ALU.add, ALU.mult)
                    ins.then_inc(tr_free, 1)
                dve.drain()
                dve.sem_inc(u_ready, 1)

            def conv_low(i):
                dve.wait_ge(u_hi, i + 1)
                TT(ulo[:], upad, uhi[:].bitcast(F32), ALU.subtract).then_inc(u_lo, 1)

            def conv(i, taps):
                for j in taps:
                    for b in range(4):
                        y = yln[:, bass.ds(i * 4 + b, 1)]
                        w = convw[:, bass.ds(i * 4 + (j * DB + b), 1)]
                        src = upad[:, b:b + 1, j:j + S]
                        if j == 0:
                            TS(y, src, w, table[:, bass.ds(i * 4 + (ROWS["dw_b"] + b), 1)], ALU.mult, ALU.add)
                        else:
                            STT(y, src, w, y, ALU.mult, ALU.add)
                    dve.drain()

            def conv_join(i):
                dve.wait_ge(taps_used, i * CONV_GROUPS + 2 * CONV_GROUPS)
                for half in range(2):
                    y = yln[:, bass.ds(i * 4 + 2 * half, 2)]
                    ins = TT(y, psC[half][:].rearrange("p (b s) -> p b s", s=S), y, ALU.add)
                ins.then_inc(conv_ready, 1)
                dve.drain()

            def pw1_pair(i, first):
                def taps(q):
                    def work():
                        if q == 7:
                            conv_low(i - 1)
                        lo_, hi_ = {6: (0, 1), 7: (1, 2)}[q]
                        conv(i - 1, range(lo_, hi_))
                    return work

                def more(q):
                    def work():
                        conv(i - 1, range(2 + 2 * q, min(4 + 2 * q, V_TAPS)))
                        if q == 7:
                            conv_join(i - 1)
                    return work

                if first:
                    norm_chunk(0, r0, MODS["pw1"])
                else:
                    chunk(i * 2 + r0, {5: lambda: glu(i - 1), 6: taps(6), 7: taps(7)}, mod=i * 2 + MODS["pw1"])
                chunk(i * 2 + (r0 + 1), None if first else {q: more(q) for q in range(2 * KS)},
                      mod=i * 2 + (MODS["pw1"] + 1))

            pw1_pair(0, True)
            with dve.Fori(1, PAIRS_PW1) as i:
                pw1_pair(i, False)
            glu(PAIRS_PW1 - 1)
            conv(PAIRS_PW1 - 1, range(1))
            conv_low(PAIRS_PW1 - 1)
            conv(PAIRS_PW1 - 1, range(1, V_TAPS))
            for g in range(CONV_GROUPS - V_GROUPS, CONV_GROUPS):
                dve.wait_ge(taps_used, PAIRS_PW1 * CONV_GROUPS + g - 3)
                b, j0 = g // GROUPS_PB, V_TAPS + g % GROUPS_PB * TAPG
                for part, cw in enumerate((cwhi.bitcast(F32), cwlo)):
                    for j in range(TAPG):
                        k = (j0 + j) * DB + 4 * (PAIRS_PW1 - 1) + b
                        ins = TS(tapd[:, g % 4, part, j], ident[:], cw[:, k:k + 1], None, ALU.mult)
                ins.then_inc(vtaps_ready, 1)
            conv_join(PAIRS_PW1 - 1)

            dve.wait_ge(tr_done, UNITS["ln"] + 1)
            TS(mu, psT[0][:, 0:S], 1.0 / D, None, ALU.mult).then_inc(tr_free, 1)
            dve.drain()
            mub = mu.rearrange("p (a s) -> p a s", a=1).to_broadcast([P, 4, S])
            for b in range(0, DB, 4):
                TT(yln[:, b:b + 4], yln[:, b:b + 4], mub, ALU.subtract).then_inc(ln_step, 1)
            r0 = SLOTS["pw2"] // 4
            ahead(r0)
            dve.wait_ge(tr_done, UNITS["ln"] + 2)
            TS(rs, psT[1][:, 0:S], 1.0 / D, None, ALU.mult).then_inc(tr_free, 1)
            dve.drain()
            dve.sem_inc(ln_step, 1)
            dve.wait_ge(ln_std, 1)
            dve.reciprocal(mu, rs)
            dve.drain()

            def ln_low(u):
                dve.wait_ge(hhi_ready, LNH + u + 1)
                TT(hlo[:, 2 * u:2 * u + 2], ysq[:, 2 * u:2 * u + 2], hhi[:, 2 * u:2 * u + 2].bitcast(F32),
                   ALU.subtract).then_inc(hlo_ready, 1)

            for k in range(4):
                TT(yln[:, 4 * k:4 * k + 4], yln[:, 4 * k:4 * k + 4], mub, ALU.mult).then_inc(ln_step, 1)
                if k:
                    ln_low(k - 1)
            gate_cols(MC0 + 2 * DB, 12)
            for u in range(3, 8):
                ln_low(u)
                if u < 7:
                    lo(r0, (u + 1) // 2, (u + 1) % 2)
                    diagonal(nsh, "gate0", u - 3)
                    mod_mul(MODS["pw2"], (2 * u - 6, 2 * u - 5))
            dve.wait_ge(tr_done, UNITS["gate0"] + 4)
            TT(nsc[:], nsh[:], cols("pw2_b"), ALU.mult)
            dve.drain()

            def add_bias(k):
                dve.wait_ge(tr_free, UNITS["gate0"] + 4)
                dve.wait_ge(tr_done, UNITS["bias0"] + k + 1)
                for t in range(TB):
                    xs = x[:, t, k * N:(k + 1) * N]
                    ins = TT(xs, psT[k % 3][:], xs, ALU.add)
                ins.then_inc(tr_free, 1)

            def bias_step(q):
                if q < 4:
                    diagonal(nsc, "bias0", q)
                if 1 <= q < 5:
                    add_bias(q - 1)
                if q == 5:
                    dve.drain()
                    residual([(0, 0)], (r0 + 1) * 4)

            chunk(r0 + 1, {q: lambda q=q: bias_step(q) for q in range(6)}, mod=MODS["pw2"] + 1)
            for c in range(2, D // N):
                rnd = r0 + c
                chunk(rnd, {3: lambda: residual([((c - 1) % 2, (c - 1) * N)], rnd * 4)}, mod=MODS["pw2"] + c)
            ahead(SLOTS["up0"] // 4, range(3))
            norm_columns(1)
            residual([(1, D - N)], SLOTS["up0"])
            ahead(SLOTS["up0"] // 4, (3,))
            root_diagonals(2)

            def ffn_up(name, layer, n, mods):
                r0, u0 = SLOTS[name] // 4, UNITS[name]
                wrow, brow = ROWS["ffn_w"] + layer * FFN_K * FB, ROWS["ffn_b"] + layer * FB

                def conv3(i, u):
                    if u in (0, 1):
                        dve.wait_ge(tr_done, i * 4 + (u0 + u + 1))
                        for j in reversed(range(FFN_K)):
                            back = FFN_K - 1 - j
                            for b in range(2):
                                k = 2 * u + b
                                g = psT[u][:, b * S:(b + 1) * S - back]
                                w = table[:, bass.ds(i * 4 + (wrow + j * FB + k), 1)]
                                y = convb[:, k, back:S]
                                if back == 0:
                                    ins = TS(y, g, w, table[:, bass.ds(i * 4 + (brow + k), 1)], ALU.mult, ALU.add)
                                else:
                                    ins = STT(y, g, w, y, ALU.mult, ALU.add)
                            if j:
                                dve.drain()
                        ins.then_inc(tr_free, 1)

                def multiply(i):
                    dve.wait_ge(silu_ready, i + (layer * (PAIRS_UP + 1) + 1))
                    for u in range(2):
                        dve.wait_ge(tr_done, i * 4 + (u0 + 2 + u + 1))
                        ins = TT(hidden[:, bass.ds(i * 4 + 2 * u, 2)], convb[:, 2 * u:2 * u + 2],
                                 psT[(2, 0)[u]][:].rearrange("p (b s) -> p b s", s=S), ALU.mult)
                        ins.then_inc(tr_free, 1)
                    dve.drain()

                def pair(i, first, mod):
                    m = i + MODS[name] if mod else None
                    if first:
                        norm_chunk(n, r0, m)
                    else:
                        chunk(i * 2 + r0, {5: lambda: multiply(i - 1)}, mod=m)
                    chunk(i * 2 + (r0 + 1), {5: lambda: conv3(i, 0), 6: lambda: conv3(i, 1)})

                pair(0, True, mods > 0)
                if mods > 1:
                    with dve.Fori(1, mods) as i:
                        pair(i, False, True)
                if mods < PAIRS_UP:
                    with dve.Fori(mods, PAIRS_UP) as i:
                        pair(i, False, False)

                def finish():
                    multiply(PAIRS_UP - 1)
                    dve.sem_inc(silu_ready, 1)
                return finish

            def ffn_down(name, layer, m0, up_last):
                def columns(half):
                    parts = [(nt, (2 * half + nt) * N) for nt in range(2)]
                    done = SLOTS[name] + (half + 1) * 2 * DGROUPS
                    if half == 0:
                        residual(parts, done)
                    else:
                        residual(parts[:1], done)
                        residual(parts[1:], done)

                for half in range(2):
                    base = SLOTS[name] + half * 2 * DGROUPS
                    gb = half * DGROUPS

                    def group(i, g, mod=None, part=(), before_last=None, gate=None):
                        s0 = base + 2 * g
                        ring = (gb + g) % 2
                        dve.wait_ge(hid_hi, i * 2 + (layer * 2 * DGROUPS + gb + g + 1))
                        TT(hlo[:, 4 * ring:4 * ring + 4], hidden[:, bass.ds(i * 8 + 4 * g, 4)],
                           hhi[:, 4 * ring:4 * ring + 4].bitcast(F32), ALU.subtract).then_inc(hid_lo, 1)
                        for q in range(4):
                            sl = s0 + q // 2
                            if q == 3 and before_last:
                                before_last()
                            lo(i + sl // 4, sl % 4, q % 2)
                            if gate:
                                diagonal(nsh, gate, q)
                            if mod is not None:
                                mod_mul(mod, (part[q],))

                    def two(i, m, gate=None):
                        group(i, 1, m, (0, 1, 2, 3), gate=gate)
                        group(i, 2, m, (4, 5, 6, 7))

                    m = None if m0 is None else m0 + 5 * half
                    if half == 0:
                        group(0, 0)
                        up_last()
                        gate_cols((MC0, MC1)[layer] + 5 * DB, (24, 56)[layer])
                        two(0, m, ("gate1", "gate3")[layer])
                    else:
                        group(0, 0, before_last=lambda: columns(0))
                    with dve.Fori(1 - half, 4) as i:
                        two(i, None if m0 is None else i + m)
                    two(4, None if m0 is None else m0 + 5 * half + 4)
                if layer == 0:
                    ahead(SLOTS["q"] // 4, range(3))
                    norm_columns(2)
                columns(1)
                if layer == 0:
                    ahead(SLOTS["q"] // 4, (3,))

            ffn_down("down0", 0, MODS["down0"], ffn_up("up0", 0, 1, PAIRS_UP))
            root_diagonals(3)

            heads8 = stage[:, 0].rearrange("p t (h c) -> p (t h) c", c=DH)
            sq8 = stage[:, 1].rearrange("p t (h c) -> p (t h) c", c=DH)
            heads = stage[:, 0].rearrange("p t (h c) -> p t h c", c=DH)
            rtmp = stage[:, 1].rearrange("p t (k h c) -> p k t h c", k=8, c=HR)
            cosb, sinb = (cs[:, n].rearrange("p t (a f) -> p t a f", a=1).to_broadcast([P, TB, 4, HR]) for n in range(2))

            def heads_squares(n):
                dve.wait_ge(evac, n)
                dve.tensor_reduce(hss, sq8, AX, ALU.add).then_inc(head_ssq, 1)

            def heads_norm(n, which):
                dve.wait_ge(head_std, n)
                dve.reciprocal(hrs, hsd)
                dve.drain()
                TT(heads8, heads8, hrs.rearrange("p (a c) -> p a c", c=1).to_broadcast([P, 8, DH]), ALU.mult)
                dve.drain()
                TT(heads8, heads8, headg[:, which].rearrange("p (a c) -> p a c", a=1).to_broadcast([P, 8, DH]), ALU.mult)
                dve.drain()
                x1, x2 = heads[:, :, :, 0:HR], heads[:, :, :, HR:ROT]
                TT(rtmp[:, 0], x1, cosb, ALU.mult)
                TT(rtmp[:, 1], x2, sinb, ALU.mult)
                TT(rtmp[:, 2], x2, cosb, ALU.mult)
                TT(rtmp[:, 3], x1, sinb, ALU.mult)
                dve.drain()
                TT(x1, rtmp[:, 0], rtmp[:, 1], ALU.subtract)
                TT(x2, rtmp[:, 2], rtmp[:, 3], ALU.add).then_inc(head_ready, 1)

            def heads_work(name, n):
                base = 0 if name == "q" else QW // N
                return {4: lambda: heads_squares(n + (CHUNKS[name] + 1)),
                        5: lambda: heads_norm(n + (base + 1), name == "q")}

            def heads_stage(name):
                m0 = MODS[name]
                chunk(SLOTS[name] // 4 + 1, heads_work(name, 0), mod=m0)
                with dve.Fori(1, 3) as i:
                    for j in range(2):
                        chunk(i * 2 + (SLOTS[name] // 4 + j), heads_work(name, i * 2 + (j - 1)),
                              mod=i + m0 if j == 1 else None)

            norm_chunk(2, SLOTS["q"] // 4)
            heads_stage("q")
            ahead(SLOTS["k"] // 4)
            norm_columns(3)
            norm_chunk(3, SLOTS["k"] // 4, work=heads_work("q", QW // N - 1))
            heads_stage("k")
            chunk(SLOTS["v"] // 4, heads_work("k", QW // N - 1), mod=MODS["v"])
            chunk(SLOTS["v"] // 4 + 1)

            for n, mk in enumerate((mask1, mask0)):
                v = mk.rearrange("p (g s) -> p g s", g=NG)
                dve.wait_ge(iota_ready, n + 1)
                for g, (_, dil) in enumerate(GROUPS):
                    TS(v[:, g].bitcast(I32), v[:, g].bitcast(I32), dil - 1, None, ALU.bitwise_and)
                dve.drain()
                TS(mk, mk.bitcast(I32), 0, NEG, ALU.is_gt, ALU.mult).then_inc(dil_ready, 1)
            with dve.Fori(1, 3) as i:
                for j in range(2):
                    chunk(i * 2 + (SLOTS["v"] // 4 + j), mod=i * 2 + (MODS["v"] - 1 + j))
            dve.drain()
            dve.wait_ge(mask_ready, 3)

            def softmax_max(j):
                w = NKEY[j % 2]
                dve.wait_ge(score_done, j + 1)
                if j >= 3:
                    dve.wait_ge(tr_done, UNITS["attn"] + ATTN_UNITS[j - 3])
                TT(prob[j % 3][:, 0:w], psG[j % 2][:].rearrange("p t n -> p (t n)")[:, 0:w],
                   masks[1 - j % 2], ALU.add).then_inc(score_read, 1)
                dve.drain()
                dve.reduce_max(mx[:, j % 2:j % 2 + 1], prob[j % 3][:, 0:w], AX)
                dve.drain()
                TS(nmx[:, j % 2:j % 2 + 1], mx[:, j % 2:j % 2 + 1], -SCALE, None, ALU.mult).then_inc(max_ready, 1)

            def softmax_divide(j):
                w = NKEY[j % 2]
                dve.wait_ge(exp_ready, j + 1)
                dve.reciprocal(rden[:, j % 2:j % 2 + 1], den[:, j % 2:j % 2 + 1])
                dve.drain()
                TS(prob[j % 3][:, 0:w], prob[j % 3][:, 0:w], rden[:, j % 2:j % 2 + 1], None, ALU.mult).then_inc(prob_ready, 1)

            def o_low(h):
                dve.wait_ge(hhi_ready, HO + h + 1)
                TT(hlo[:, h], psM[:, 0:S], hhi[:, h].bitcast(F32), ALU.subtract).then_inc(o_read, 1)

            for j in range(2 * HPG + 1):
                if j < 2 * HPG:
                    softmax_max(j)
                if j >= 1:
                    softmax_divide(j - 1)
                if j >= 3 and j % 2 == 1:
                    o_low((j - 3) // 2)
            o_low(HPG - 1)
            dve.drain()

            for c in range(D // N):
                rnd, r = SLOTS["wo"] // 4 + c // 2, c % 2 * 2
                if c == 0:
                    gate_cols(MC1 + 2 * DB, 44)
                for q in range(4):
                    lo(rnd, r + q // 2, q % 2)
                    if c == 0:
                        diagonal(nsh, "gate2", q)
                if c == 1:
                    dve.wait_ge(tr_free, UNITS["gate2"] + 4)
                if c:
                    residual([((c - 1) % 2, (c - 1) * N)], rnd * 4 + r)
            ahead(SLOTS["up1"] // 4, range(3))
            norm_columns(4)
            residual([(1, D - N)], SLOTS["up1"])
            ahead(SLOTS["up1"] // 4, (3,))
            root_diagonals(4)
            ffn_down("down1", 1, None, ffn_up("up1", 1, 4, 4))

        @block.tensor
        def _(pe):
            def split_matmul(out_, act_hi, act_lo, q, col0, first, last, done=False):
                w = slice(col0, col0 + N)
                pe.matmul(out_, act_hi, whi[:, q, w], start=first, stop=False)
                pe.matmul(out_, act_hi, wlo[:, q, w], start=False, stop=False)
                ins = pe.matmul(out_, act_lo, whi[:, q, w], start=False, stop=last)
                if done:
                    ins.then_inc(used, 1)

            def chunk(rnd, c, par, work=None, r0=0, slots=KS, units_before=None):
                if not (isinstance(c, int) and c < 2):
                    pe.wait_ge(evac, c - 1)
                for q in range(2 * slots):
                    pe.wait_ge(lo_ready, rnd * 8 + (2 * r0 + q + 1))
                    if units_before is not None:
                        pe.wait_ge(hlo_ready, units_before + q + 1)
                    for kb in range(2):
                        for t in range(TB):
                            b, ts = 2 * q + kb, slice(t * P, (t + 1) * P)
                            split_matmul(psG[par][:, t], hhi[:, b, ts], hlo[:, b, ts], (2 * r0 + q) % NP_, kb * N,
                                         b == 0, b == 4 * slots - 1, kb == 1 and t == TB - 1)
                    if work and q in work:
                        work[q]()

            def transposes(src_of, n, bank, free, scale=None):
                pe.wait_ge(tr_free, free)
                for b in range(2):
                    for t in range(TB):
                        to = psT[bank][:, b * S + t * P:b * S + (t + 1) * P]
                        if scale is None:
                            ins = pe.transpose(to, src_of(b, t), ident[:])
                        else:
                            ins = pe.matmul(to, src_of(b, t), scale[:, t], start=True, stop=True)
                ins.then_inc(tr_done, 1)

            def norm_chunk(n, rnd, c, late=None):
                u0 = UNITS[f"norm{n}"]

                def unit(u):
                    transposes(lambda b, t: x[:, t, (2 * u + b) * P:(2 * u + b + 1) * P],
                               u0 + u, u % 3, max(u0, u0 + u - 2), rdiag)

                pe.wait_ge(rdiag_ready, ROOT[n])
                for u in range(3):
                    unit(u)
                steps = {q: lambda q=q: unit(q + 3) for q in range(5)}
                if late:
                    steps[6] = late
                chunk(rnd, c, 0, steps, units_before=HL[n])

            def broadcast(unit, k):
                u0 = UNITS[unit]
                pe.wait_ge(diag_ready, DIAGONALS[unit] + k + 1)
                pe.wait_ge(tr_free, max(u0, u0 + k - 2))
                pe.matmul(psT[k % 3][:], ones[:], diag[:, 4 * (k % 2):4 * (k % 2) + 4].rearrange("p b c -> p (b c)"),
                          start=True, stop=True).then_inc(tr_done, 1)

            pe.wait_ge(const_ready, 3)
            pe.wait_ge(params_in, 32)
            for u in range(UNITS["head_g"]):
                for k in range(4 * u, min(4 * u + 4, NRB)):
                    ins = pe.transpose(psT[u][:, (k - 4 * u) * P:(k - 4 * u + 1) * P], tbl_in[:, k * P:(k + 1) * P],
                                       ident[:])
                ins.then_inc(tr_done, 1)
            pe.wait_ge(diag_ready, 1)
            pe.wait_ge(tr_free, UNITS["head_g"])
            pe.matmul(psT[0][:, 0:2 * DH], ones[:], headg[:].rearrange("p a b -> p (a b)"), start=True,
                      stop=True).then_inc(tr_done, 1)

            for k in range(4):
                broadcast("c", k)

            def pair_transposes(i, u0, value, value_banks):
                n = i * 4 + (u0 + 2 * value)
                for u in range(2):
                    transposes(lambda b, t: stage[:, value, t, (2 * u + b) * P:(2 * u + b + 1) * P],
                               n + u, ((0, 1), value_banks)[value][u],
                               n if not value else n - value_banks[0] // 2 - 1 + u)

            def pairs(name, n, count, value_banks=(2, 0), conv=None):
                r0, u0, c0 = SLOTS[name] // 4, UNITS[name], CHUNKS[name]

                def value_transposes(i):
                    pe.wait_ge(evac, i * 2 + (c0 + 2))
                    pair_transposes(i, u0, 1, value_banks)

                def gate_transposes(i):
                    pe.wait_ge(evac, i * 2 + (c0 + 1))
                    pair_transposes(i, u0, 0, value_banks)

                def pair(i, first):
                    if first:
                        norm_chunk(n, r0, c0)
                    else:
                        chunk(i * 2 + r0, i * 2 + c0, 0, {1: lambda: value_transposes(i - 1)})
                    work = {1: lambda: gate_transposes(i)}
                    if conv and not first:
                        def beside(q):
                            def both():
                                if q == 1:
                                    gate_transposes(i)
                                conv(i - 1, (2 * q, 2 * q + 1))
                            return both
                        work = {q: beside(q) for q in range(2 * KS)}
                    chunk(i * 2 + (r0 + 1), i * 2 + (c0 + 1), 1, work)

                pair(0, True)
                with pe.Fori(1, count) as i:
                    pair(i, False)
                return lambda: value_transposes(count - 1)

            def conv_groups(i, groups):
                for g in groups:
                    pe.wait_ge(u_lo, i + 1)
                    late = g - (CONV_GROUPS - V_GROUPS)
                    if isinstance(i, int) and i == PAIRS_PW1 - 1 and late >= 0:
                        pe.wait_ge(vtaps_ready, late + 1)
                    else:
                        pe.wait_ge(taps_ready, i * CONV_GROUPS + g + 1)
                    b, j0 = g // GROUPS_PB, V_TAPS + g % GROUPS_PB * TAPG
                    acc = psC[b // 2][:, b % 2 * S:(b % 2 + 1) * S]
                    for j in range(TAPG):
                        at = slice(j0 + j, j0 + j + S)
                        dhi, dlo = (tapd[:, g % 4, part, j] for part in range(2))
                        pe.matmul(acc, dhi, uhi[:, b, at], start=g % GROUPS_PB == 0 and j == 0, stop=False)
                        pe.matmul(acc, dhi, ulo[:, b, at], start=False, stop=False)
                        ins = pe.matmul(acc, dlo, uhi[:, b, at], start=False,
                                        stop=g % GROUPS_PB == GROUPS_PB - 1 and j == TAPG - 1)
                    ins.then_inc(taps_used, 1)

            pe.sem_inc(taps_used, CONV_GROUPS)
            pairs("pw1", 0, PAIRS_PW1, (0, 1), conv_groups)()
            pe.wait_ge(conv_ready, PAIRS_PW1 - 1)
            pe.wait_ge(tr_free, UNITS["ln"])
            for b in range(DB - 4):
                pe.matmul(psT[0][:, 0:S], ones[:], yln[:, b], start=b == 0, stop=False)
            conv_groups(PAIRS_PW1 - 1, range(CONV_GROUPS))

            pe.wait_ge(conv_ready, PAIRS_PW1)
            for b in range(DB - 4, DB):
                ins = pe.matmul(psT[0][:, 0:S], ones[:], yln[:, b], start=False, stop=b == DB - 1)
            ins.then_inc(tr_done, 1)
            for b in range(DB):
                if b % 4 == 0:
                    pe.wait_ge(ln_sq, b // 4 + 1)
                ins = pe.matmul(psT[1][:, 0:S], ones[:], ysq[:, b], start=b == 0, stop=b == DB - 1)
            ins.then_inc(tr_done, 1)

            for c in range(D // N):
                chunk(SLOTS["pw2"] // 4 + c, CHUNKS["pw2"] + c, c % 2,
                      [{q + 4: lambda q=q: broadcast("gate0", q) for q in range(4)},
                       {q: lambda q=q: broadcast("bias0", q) for q in range(4)}, None, None][c],
                      units_before=LNH if c == 0 else None)

            def ffn_down(name, layer, up_last):
                for half in range(2):
                    base = SLOTS[name] + half * 2 * DGROUPS
                    gb = half * DGROUPS

                    def group(i, g, first=False, last=False, gate=None):
                        ring = (gb + g) % 2
                        pe.wait_ge(hid_lo, i * 2 + (layer * 2 * DGROUPS + gb + g + 1))
                        for q in range(4):
                            n = 2 * (base + 2 * g) + q
                            pe.wait_ge(lo_ready, i * 8 + (n + 1))
                            b = 4 * ring + q
                            for nt in range(2):
                                if first and q == 0:
                                    pe.wait_ge(evac, CHUNKS[name] + 2 * half - 1 + nt)
                                for t in range(TB):
                                    split_matmul(psG[nt][:, t], hhi[:, b, t * P:(t + 1) * P],
                                                 hlo[:, b, t * P:(t + 1) * P], n % NP_, nt * N,
                                                 first and q == 0, last and q == 3, nt == 1 and t == TB - 1)
                            if gate:
                                broadcast(gate, q)

                    group(0, 0, first=True)
                    if half == 0:
                        up_last()
                        group(0, 1, gate=("gate1", "gate3")[layer])
                        group(0, 2)
                    with pe.Fori(1 - half, 4) as i:
                        group(i, 1)
                        group(i, 2)
                    group(4, 1)
                    group(4, 2, last=True)

            ffn_down("down0", 0, pairs("up0", 1, PAIRS_UP))

            def heads_out(name, n):
                pe.wait_ge(head_ready, n + (1 if name == "q" else QW // N + 1))
                for u in range(2):
                    transposes(lambda b, t: stage[:, 0, t, (2 * u + b) * P:(2 * u + b + 1) * P],
                               None, u, head_units(name, n))

            def heads(name):
                def one(n, par):
                    chunk(n + SLOTS[name] // 4, n + CHUNKS[name], par, {5: lambda: heads_out(name, n - 1)})

                one(1, 1)
                with pe.Fori(1, 3) as i:
                    for j in range(2):
                        one(i * 2 + j, j)

            norm_chunk(2, SLOTS["q"] // 4, CHUNKS["q"])
            heads("q")
            norm_chunk(3, SLOTS["k"] // 4, CHUNKS["k"], lambda: heads_out("q", QW // N - 1))
            heads("k")
            r0, c0 = SLOTS["v"] // 4, CHUNKS["v"]
            chunk(r0, c0, 0, {5: lambda: heads_out("k", QW // N - 1)})
            chunk(r0 + 1, c0 + 1, 1)
            with pe.Fori(1, 3) as i:
                for j in range(2):
                    chunk(i * 2 + (r0 + j), i * 2 + (c0 + j), j)

            def scores(j):
                h, qb = j // 2, j % 2
                nk = P * (1 + qb)
                if j >= 2:
                    pe.wait_ge(score_read, j - 1)
                else:
                    pe.wait_ge(evac, CHUNKS["wo"])
                flat = psG[j % 2][:].rearrange("p t n -> p (t n)")
                for g in range(NG):
                    n = g * HPG + h
                    ins = pe.matmul(flat[:, g * nk:(g + 1) * nk], qT[:, n, qb * P:(qb + 1) * P], kT[:, n, 0:nk],
                                    start=True, stop=True)
                ins.then_inc(score_done, 1)

            def prob_transposes(j):
                h, qb = j // 2, j % 2
                u0 = UNITS["attn"] + 3 * h + qb
                pe.wait_ge(prob_ready, j + 1)
                for u in range(1 + qb):
                    pe.wait_ge(tr_free, max(UNITS["attn"], u0 + u - 2))
                    k0, k1 = (0, 3) if qb == 0 else ((0, 4), (4, 6))[u]
                    for k in range(k0, k1):
                        ins = pe.transpose(psT[qb + u][:, (k - k0) * P:(k - k0 + 1) * P],
                                           prob[j % 3][:, k * P:(k + 1) * P], ident[:])
                    ins.then_inc(tr_done, 1)

            def outputs(j):
                h, qb = j // 2, j % 2
                pe.wait_ge(tr_free, UNITS["attn"] + ATTN_UNITS[j])
                if h >= 1 and qb == 0:
                    pe.wait_ge(o_read, h)
                nb = NG * (1 + qb)
                for k in range(nb):
                    g, kb = k // (1 + qb), k % (1 + qb)
                    n = g * HPG + h
                    ins = pe.matmul(psM[:, qb * P:(qb + 1) * P], vv[:, kb, n * DH:(n + 1) * DH],
                                    probT[j % 2][:, k], start=k == 0, stop=k == nb - 1)
                ins.then_inc(o_done, 1)

            pe.wait_ge(tr_free, UNITS["attn"])
            scores(0)
            scores(1)
            for j in range(2 * HPG):
                if j + 2 < 2 * HPG:
                    scores(j + 2)
                if j >= 1:
                    outputs(j - 1)
                prob_transposes(j)
            outputs(2 * HPG - 1)
            pe.wait_ge(o_read, HPG)
            for c in range(D // N):
                chunk(SLOTS["wo"] // 4 + c // 2, CHUNKS["wo"] + c, c % 2,
                      {q: lambda q=q: broadcast("gate2", q) for q in range(4)} if c == 0 else None,
                      r0=c % 2 * 2, slots=OW // P // 4)
            ffn_down("down1", 1, pairs("up1", 4, PAIRS_UP))


def _slots(w, order=None):
    k, n = w.shape
    t = w.reshape(k // (4 * P), 4, P, n // N, N).transpose(3, 0, 2, 1, 4)
    if order is not None:
        t = t[order]
    return t.reshape(-1, P, SLOT)


def _mod_slots(w):
    return w.reshape(2, MSLOT, w.shape[1] // (2 * P), 2, P).transpose(2, 0, 3, 4, 1).reshape(-1, P, MSLOT)


def _down_slots(w):
    return w.reshape(DFF // (2 * P), 2, P, 2, 2 * N).transpose(3, 0, 2, 1, 4).reshape(-1, P, SLOT)


def _pairs(n):
    return [c for i in range(n) for c in (i, n + i)]


def kernel(x, c, positions, mod_w, mod_b, norm_mix_g, norm_ffn_g, conv_pw1_w, conv_pw1_b, conv_dw_w, conv_dw_b,
           conv_ln_g, conv_ln_b, conv_pw2_w, conv_pw2_b, kv_mod_w, kv_mod_b, kv_norm_g, w_kv, k_norm_g, w_q,
           q_norm_g, w_o, ffn_up_w, ffn_dw_w, ffn_dw_b, ffn_down_w):
    import concourse.bacc as _bacc
    from concourse.bass_utils import run_bass_kernel_spmd as _run

    gate_first = [ch for i in range(PAIRS_PW1) for ch in (PAIRS_PW1 + i, i)]
    wstream = np.concatenate([
        _slots(conv_pw1_w[0], gate_first), _slots(conv_pw2_w[0]),
        _slots(ffn_up_w[0], _pairs(PAIRS_UP)), _down_slots(ffn_down_w[0]),
        _slots(w_q[0]), _slots(w_kv), _slots(w_o[0]),
        _slots(ffn_up_w[1], _pairs(PAIRS_UP)), _down_slots(ffn_down_w[1])])
    mstream = np.concatenate([_mod_slots(mod_w[0]), _mod_slots(kv_mod_w), _mod_slots(mod_w[1])])
    rows = [c, mod_b[0], kv_mod_b, mod_b[1], norm_mix_g, norm_ffn_g, kv_norm_g, conv_pw1_b, conv_dw_b, conv_ln_g,
            conv_ln_b, conv_pw2_b, k_norm_g, q_norm_g, ffn_dw_w, ffn_dw_b, conv_dw_w]
    rows = np.concatenate([r.reshape(-1, P) for r in rows] + [np.zeros((NRB * P - NROWS, P), np.float32)])
    assert wstream.shape[0] == NSLOTS and mstream.shape[0] == 8 * NMODS

    nc = _bacc.Bacc("TRN2", target_bir_lowering=False, num_devices=1, dynamic_dma_scratch_size=1024)
    arrays = {"wstream": wstream, "mstream": mstream, "x_in": np.ascontiguousarray(x[0]), "rows_in": rows,
              "pos_in": np.ascontiguousarray(positions.reshape(TB, P).T)}
    args = [nc.dram_tensor(n, a.shape, mybir.dt.from_np(a.dtype), kind="ExternalInput").ap()
            for n, a in arrays.items()]
    out = nc.dram_tensor("out", (1, S, D), mybir.dt.float32, kind="ExternalOutput").ap()
    build(nc, *args, out[0])
    r = _run(nc, [arrays], core_ids=[0])
    return r.results[0]["out"]
```

```python
from contextlib import ExitStack

import numpy as np

import concourse.bass as bass
from concourse import mybir

P = 128
D = 2048
S = 256
TB = S // P
DB = D // P
N = 512
DFF = 5632
FB = DFF // P
CONV_K = 31
V_TAPS = 15
TAPG = 4
FFN_K = 3
GROUPS = ((128, 1), (512, 4), (2048, 16))
NG = len(GROUPS)
HPG = 8
DH = 128
NH = NG * HPG
QW = NH * DH
OW = HPG * DH
ROT = DH // 4
HR = ROT // 2
THETA = 500000.0
EPS = 1e-6
NEG = -1e30
SCALE = 1.0 / float(np.sqrt(DH))

SLOT = 4 * N
PIECE = SLOT // 2
NP_ = 4
NRAW = 4
MSLOT = D // 2
NMRAW = 4
MPC = 8

KS = D // P // 4
PAIRS_PW1 = D // N
PAIRS_UP = DFF // N
DGROUPS = FB // 4
SLOTS = {}
CHUNKS = {}
_s = _c = 0
for _name, _chunks, _slots in (
        ("pw1", 2 * PAIRS_PW1, 2 * PAIRS_PW1 * KS), ("pw2", D // N, D // N * KS),
        ("up0", 2 * PAIRS_UP, 2 * PAIRS_UP * KS), ("down0", 4, 4 * DGROUPS),
        ("q", QW // N, QW // N * KS), ("k", QW // N, QW // N * KS), ("v", QW // N, QW // N * KS),
        ("wo", D // N, D // N * (OW // P // 4)),
        ("up1", 2 * PAIRS_UP, 2 * PAIRS_UP * KS), ("down1", 4, 4 * DGROUPS)):
    SLOTS[_name], CHUNKS[_name] = _s, _c
    _s += _slots
    _c += _chunks
NSLOTS, NCHUNKS = _s, _c

STEPS = D // N
MODS = {"head": 0, "pw1": 8, "conv": 14, "pw2": 16, "up0": 20, "down0": 32, "q": 41, "k": 44, "v": 47, "up1": 52}
NMODS = 56
MC0, MCKV, MC1 = 0, 6 * DB, 8 * DB

ROWS = {}
_r = 0
for _name, _n in (("c", DB), ("mod_b", 14 * DB), ("mix_g", 2 * DB), ("ffn_g", 2 * DB), ("kv_g", DB),
                  ("pw1_b", 2 * DB), ("dw_b", DB), ("ln_g", DB), ("ln_b", DB), ("pw2_b", DB),
                  ("head_g", 2), ("ffn_w", 2 * FFN_K * FB), ("ffn_b", 2 * FB), ("conv_w", CONV_K * DB)):
    ROWS[_name] = _r
    _r += _n
NROWS = _r
GROUPS_PB = (CONV_K - V_TAPS) // TAPG
CONV_GROUPS = 4 * GROUPS_PB
NTAPD = 6
NKEPT = ROWS["conv_w"]
NRB = -(-NROWS // P)

UNITS = {}
_u = 0
for _name, _n in (("table", -(-NRB // 4)), ("head_g", 1), ("c", 4), ("norm0", 8), ("pw1", 4 * PAIRS_PW1), ("ln", 2),
                  ("gate0", 4), ("bias0", 4), ("norm1", 8), ("up0", 4 * PAIRS_UP), ("gate1", 4),
                  ("norm2", 8), ("q", 10), ("norm3", 8), ("q_last", 2), ("k", 12), ("attn", 3 * HPG), ("gate2", 4),
                  ("norm4", 8), ("up1", 4 * PAIRS_UP), ("gate3", 4)):
    UNITS[_name] = _u
    _u += _n


def head_units(name, n):
    return UNITS["q_last"] if name == "q" and isinstance(n, int) and n == QW // N - 1 else n * 2 + UNITS[name]


AREA = 18432
A_HID, A_CONV, A_GATE = 0, 11264, 12288
A_Y, A_SIG, A_U, A_MU, A_RS, A_YC = 0, 4096, 5120, 6272, 6528, 8192
A_TRIG, A_CW = 2048, 14336
A_CWH, A_CWL, A_UH, A_UL, A_TAP = 14848, 15360, 17024, 15872, 8192
UPAD = CONV_K - 1
A_KT, A_V, A_QT = 0, 6144, 12288
A_XN, A_H32 = 0, 7168

ATTN_UNITS = [3 * (j // 2) + (1, 3)[j % 2] for j in range(2 * HPG)]
HO = 40

PI = float(np.pi)
PI_BELOW = 3.1415925
ROUND = 1.5 * 2.0 ** 23
TWO_PI = (6.28125, float(np.round((2 * np.pi - 6.28125) * 2.0 ** 20) / 2.0 ** 20))
TWO_PI += (float(2 * np.pi - TWO_PI[0] - TWO_PI[1]),)


def inv_freq():
    return np.power(np.float32(THETA), -np.arange(0, ROT, 2, dtype=np.float32) / np.float32(ROT)).astype(np.float32)


def build(nc, wstream, mstream, x_in, rows_in, pos_in, out):
    F32, F32R, I32 = mybir.dt.float32, mybir.dt.float32r, mybir.dt.int32
    ALU, ACT, AX = mybir.AluOpType, mybir.ActivationFunctionType, mybir.AxisListType.X

    with ExitStack() as ctx:
        def sb(name, shape, dt=F32):
            return ctx.enter_context(nc.sbuf_tensor(name, shape, dt))

        def pb(name, shape):
            return ctx.enter_context(nc.psum_tensor(name, shape, F32))

        def sem(name):
            return ctx.enter_context(nc.semaphore(name))

        raw = sb("raw", [P, NRAW, SLOT])
        mraw = sb("mraw", [P, NMRAW, MSLOT])
        whi = sb("whi", [P, NP_, PIECE], F32R)
        wlo = sb("wlo", [P, NP_, PIECE], F32R)
        hhi = sb("hhi", [P, DB, S], F32R)
        hlo = sb("hlo", [P, DB, S], F32R)
        x = sb("x", [P, TB, D])
        cbc = sb("cbc", [P, D])
        stage = sb("stage", [P, 2, TB, N])
        area_at = nc.sbuf_base
        area = sb("area", [P, AREA])

        def in_area(name, first, shape):
            return nc.alloc_sbuf_tensor_at(name, shape, F32R, offset=area_at + 4 * first)

        table = sb("table", [P, NKEPT])
        modcol = sb("modcol", [P, 14 * DB])
        halfsum = sb("halfsum", [P, 2, 4])
        ident = sb("ident", [P, P])
        ones = sb("ones", [P, P])
        headg = sb("headg", [P, 2, DH])
        cs = sb("cs", [P, 2, TB, HR])
        csil = sb("csil", [P, DB])
        nsh = sb("nsh", [P, DB])
        nsc = sb("nsc", [P, DB])
        small = sb("small", [P, 64])
        posi = sb("posi", [P, TB], I32)
        posf = sb("posf", [P, TB])

        psG = [pb(f"psG{i}", [P, TB, N]) for i in range(2)]
        psT = [pb(f"psT{i}", [P, N]) for i in range(3)]
        psM = pb("psM", [P, N])
        psC = [psM, psT[2]]

        raw_full = [sem(f"raw_full{i}") for i in range(NRAW)]
        mod_full = [sem(f"mod_full{i}") for i in range(NMRAW)]
        params_in = sem("params_in")
        x_loaded = sem("x_loaded")
        out_done = sem("out_done")
        const_ready = sem("const_ready")
        hi_ready = sem("hi_ready")
        lo_ready = sem("lo_ready")
        used = sem("used")
        mod_ops = sem("mod_ops")
        evac = sem("evac")
        tr_done = sem("tr_done")
        tr_free = sem("tr_free")
        csil_ready = sem("csil_ready")
        angle_ready = sem("angle_ready")
        trig_ready = sem("trig_ready")
        x_ready = sem("x_ready")
        ssq_ready = sem("ssq_ready")
        xn_ready = sem("xn_ready")
        cols_ready = sem("cols_ready")
        hhi_ready = sem("hhi_ready")
        hlo_ready = sem("hlo_ready")
        conv_ready = sem("conv_ready")
        convw_hi = sem("convw_hi")
        convw_lo = sem("convw_lo")
        u_ready = sem("u_ready")
        u_hi = sem("u_hi")
        u_lo = sem("u_lo")
        taps_ready = sem("taps_ready")
        taps_used = sem("taps_used")
        silu_ready = sem("silu_ready")
        diag_ready = sem("diag_ready")
        ln_step = sem("ln_step")
        ln_sq = sem("ln_sq")
        ln_std = sem("ln_std")
        hid_hi = sem("hid_hi")
        hid_lo = sem("hid_lo")
        head_ssq = sem("head_ssq")
        head_std = sem("head_std")
        head_ready = sem("head_ready")
        iota_ready = sem("iota_ready")
        dil_ready = sem("dil_ready")
        mask_ready = sem("mask_ready")
        score_done = sem("score_done")
        score_read = sem("score_read")
        max_ready = sem("max_ready")
        exp_ready = sem("exp_ready")
        prob_ready = sem("prob_ready")
        o_done = sem("o_done")
        o_read = sem("o_read")

        h32 = area[:, A_H32:A_H32 + 2 * N].rearrange("p (u b s) -> p u b s", u=2, b=2)
        xn = area[:, A_XN:A_XN + TB * D].rearrange("p (t d) -> p t d", t=TB)
        hidden = area[:, A_HID:A_HID + FB * S].rearrange("p (b s) -> p b s", s=S)
        squared = area[:, A_CONV:A_CONV + TB * N].rearrange("p (t n) -> p t n", t=TB)
        convb = area[:, A_CONV:A_CONV + 4 * S].rearrange("p (b s) -> p b s", s=S)
        gate = area[:, A_GATE:A_GATE + D]
        yln = area[:, A_Y:A_Y + DB * S].rearrange("p (b s) -> p b s", s=S)
        sigb = area[:, A_SIG:A_SIG + 4 * S].rearrange("p (b s) -> p b s", s=S)
        upad = area[:, A_U:A_U + 4 * (S + UPAD)].rearrange("p (b s) -> p b s", b=4)
        mu = area[:, A_MU:A_MU + S]
        rs = area[:, A_RS:A_RS + S]
        ysq = area[:, A_YC:A_YC + DB * S].rearrange("p (b s) -> p b s", s=S)
        kT = area[:, A_KT:A_KT + NH * S].rearrange("p (n s) -> p n s", s=S)
        vv = area[:, A_V:A_V + TB * QW].rearrange("p (t n) -> p t n", t=TB)
        qT = area[:, A_QT:A_QT + NH * S].rearrange("p (n s) -> p n s", s=S)
        diag = stage[:, 0].rearrange("p t (b c) -> p (t b) c", c=P)
        NKEY = [NG * P, NG * S]
        masks = [stage[:, 0].rearrange("p t n -> p (t n)")[:, 0:NKEY[1]],
                 stage[:, 1].rearrange("p t n -> p (t n)")[:, 0:NKEY[0]]]
        mask1, mask0 = masks
        attn = mraw[:].rearrange("p a b -> p (a b)")
        prob = [attn[:, i * NKEY[1]:(i + 1) * NKEY[1]] for i in range(3)]
        probT = [attn[:, (3 + i) * NKEY[1]:(4 + i) * NKEY[1]].rearrange("p (b q) -> p b q", q=P) for i in range(2)]
        eps_c, ssq, rstd = small[:, 0:1], small[:, 2:4], small[:, 4:6]
        ssq_parts = small[:, 40:48].rearrange("p (t c) -> p t c", t=TB)
        hss, hsd, hrs = small[:, 8:16], small[:, 16:24], small[:, 24:32]
        mx, nmx, den, rden = small[:, 32:34], small[:, 34:36], small[:, 36:38], small[:, 38:40]
        trig = area[:, A_TRIG:A_TRIG + 8 * TB * HR].rearrange("p (k t f) -> p k t f", k=8, t=TB)
        convw = area[:, A_CW:A_CW + NRB * P - NKEPT]
        cwhi = area[:, A_CWH:A_CWH + NRB * P - NKEPT].bitcast(F32R)
        cwlo = area[:, A_CWL:A_CWL + NRB * P - NKEPT]
        uhi, ulo = (in_area(name, a, [P, 4, S + UPAD]) for name, a in (("uhi", A_UH), ("ulo", A_UL)))
        tapd = in_area("tapd", A_TAP, [P, NTAPD, 2, TAPG, P])

        tbl_in = area[:, 0:NRB * P]

        def col(name, i):
            return table[:, ROWS[name] + i:ROWS[name] + i + 1]

        def cols(name, i=0, n=DB):
            return table[:, ROWS[name] + i:ROWS[name] + i + n]

        NORMS = [("mix_g", 0, MC0, MC0 + DB, 8),
                 ("ffn_g", 0, MC0 + 3 * DB, MC0 + 4 * DB, 20),
                 ("mix_g", DB, MC1, MC1 + DB, 40),
                 ("kv_g", 0, MCKV, MCKV + DB, 32),
                 ("ffn_g", DB, MC1 + 3 * DB, MC1 + 4 * DB, 52)]
        HB = [0, 16, 24, 32, 48]
        HL = [0, 16, 24, 32, 40]
        LNH = 8
        DIAGONALS = {name: 1 + 4 * k for k, name in enumerate(("c", "gate0", "bias0", "gate1", "gate2", "gate3"))}
        XB = {"pw2": 0, "down0": 4, "wo": 8, "down1": 12}
        ROOT = [1, 2, 3, 3, 4]

        block = ctx.enter_context(nc.Block())

        @block.sync
        def _(sp):
            sp.dma_start(tbl_in.rearrange("p (b c) -> p b c", c=P), rows_in.rearrange("(b p) c -> p b c", p=P)
                         ).then_inc(params_in, 16)
            sp.dma_start(posi[:], pos_in).then_inc(params_in, 16)

            def w_slot(rnd, r):
                if not (isinstance(rnd, int) and rnd == 0):
                    sp.wait_ge(lo_ready, ((rnd - 1) * NRAW + r + 1) * 2)
                sp.dma_start(raw[:, r], wstream[rnd * NRAW + r]).then_inc(raw_full[r], 16)

            def m_chunk(m, part=range(8)):
                for u in part:
                    if not (isinstance(m, int) and m * MPC + u < NMRAW):
                        sp.wait_ge(mod_ops, m * (MPC + 1) + (u - NMRAW + 1))
                    sp.dma_start(mraw[:, u % NMRAW], mstream[m * MPC + u]).then_inc(mod_full[u % NMRAW], 16)

            def first_chunk(rnd, mod):
                for k in range(KS):
                    w_slot(rnd, k)
                if mod is not None:
                    m_chunk(mod)

            def chunk(rnd, mod=None):
                for k in range(KS):
                    w_slot(rnd, k)
                    if mod is not None:
                        m_chunk(mod, ((0, 1), (2, 3), (4, 5), (6, 7))[k])

            m_chunk(0, range(4))
            for k in range(NRAW):
                w_slot(0, k)
            m_chunk(0, range(4, 8))
            sp.dma_start(x[:], x_in.rearrange("(t p) d -> p t d", p=P)).then_inc(x_loaded, 16)
            m_chunk(1)
            for j in range(1, STEPS):
                for half in range(2):
                    m_chunk(2 * j, range(4 * half, 4 * half + 4))
                    if j < 3:
                        w_slot(1, 2 * j - 2 + half)
                m_chunk(2 * j + 1)

            def chunks(name, n, mods):
                def one(i, j):
                    chunk(i * 2 + (SLOTS[name] // 4 + j), mods(i, j))
                if name != "pw1":
                    first_chunk(SLOTS[name] // 4, mods(0, 0))
                    one(0, 1)
                with sp.Fori(1, n) as i:
                    one(i, 0)
                    one(i, 1)

            chunks("pw1", PAIRS_PW1, lambda i, j: i * 2 + (MODS["pw1"] - 2 + j))
            m_chunk(MODS["conv"])
            m_chunk(MODS["conv"] + 1)
            first_chunk(SLOTS["pw2"] // 4, MODS["pw2"])
            for k in range(1, D // N):
                chunk(SLOTS["pw2"] // 4 + k, MODS["pw2"] + k)
            chunks("up0", PAIRS_UP - 1, lambda i, j: i + MODS["up0"] if j == 0 else None)
            for j in range(2):
                chunk(SLOTS["down0"] // 4 - 2 + j, MODS["down0"] - 2 + j)

            def down(name, m0):
                for half in range(2):
                    base = SLOTS[name] + half * 2 * DGROUPS

                    def group(g_rnd, r, mod, part):
                        w_slot(g_rnd, r)
                        if mod is not None:
                            m_chunk(mod, part[:0])
                        w_slot(g_rnd + (r + 1) // 4, (r + 1) % 4)
                        if mod is not None:
                            m_chunk(mod, part[0:])

                    def two(i, m):
                        group(i + (base + 2) // 4, (base + 2) % 4, m, (0, 1, 2, 3))
                        group(i + (base + 4) // 4, (base + 4) % 4, m, (4, 5, 6, 7))

                    group(base // 4, base % 4, None, ())
                    m = None if m0 is None else m0 - 1 + 5 * half
                    two(0, m if half else None)
                    with sp.Fori(1, 4) as i:
                        two(i, None if m is None else i + m)
                    two(4, None if m is None else m + 4)

            down("down0", MODS["down0"])
            chunks("q", 3, lambda i, j: i + MODS["q"] if j == 1 else None)
            chunks("k", 3, lambda i, j: i + MODS["k"] if j == 1 else None)
            chunk(SLOTS["v"] // 4, MODS["v"])
            chunk(SLOTS["v"] // 4 + 1)
            with sp.Fori(1, 3) as i:
                for j in range(2):
                    chunk(i * 2 + (SLOTS["v"] // 4 + j), i * 2 + (MODS["v"] - 1 + j))
            for rnd in range(SLOTS["wo"] // 4, SLOTS["up1"] // 4):
                for r in range(4):
                    w_slot(rnd, r)
            r1 = SLOTS["up1"] // 4
            for i in range(4):
                if i == 0:
                    first_chunk(r1, None)
                    sp.wait_ge(tr_done, UNITS["attn"] + 3 * HPG)
                    sp.wait_ge(o_done, 2 * HPG)
                    m_chunk(MODS["up1"])
                else:
                    chunk(r1 + 2 * i, MODS["up1"] + i)
                chunk(r1 + 2 * i + 1)
            with sp.Fori(4, PAIRS_UP) as i:
                chunk(i * 2 + r1)
                chunk(i * 2 + (r1 + 1))
            down("down1", None)
            for c in range(D // N):
                sp.wait_ge(x_ready, XB["down1"] + c + 1)
                sp.dma_start(out.rearrange("(t p) d -> p t d", p=P)[:, :, c * N:(c + 1) * N],
                             x[:, :, c * N:(c + 1) * N]).then_inc(out_done, 16)
            sp.wait_ge(out_done, 16 * (D // N))

        @block.gpsimd
        def _(pool):
            pool.memset(ident[:], 0.0).then_inc(const_ready, 1)
            pool.memset(ones[:], 1.0).then_inc(const_ready, 1)
            pool.wait_ge(const_ready, 1)
            pool.affine_select(out=ident[:], in_=ident[:], compare_op=ALU.not_equal, fill=1.0, base=0,
                               pattern=[[-1, P]], channel_multiplier=1).then_inc(const_ready, 1)
            pool.wait_ge(tr_done, UNITS["k"] + 12)
            pool.iota(mask1.bitcast(I32).rearrange("p (g s) -> p g s", g=NG), pattern=[[0, NG], [-1, S]],
                      base=P, channel_multiplier=1).then_inc(iota_ready, 1)
            pool.iota(mask0.bitcast(I32).rearrange("p (g s) -> p g s", g=NG), pattern=[[0, NG], [-1, P]],
                      base=0, channel_multiplier=1).then_inc(iota_ready, 1)
            pool.wait_ge(dil_ready, 2)
            for n, (mk, keys, base) in enumerate(((mask1, S, P), (mask0, P, 0))):
                v = mk.rearrange("p (g s) -> p g s", g=NG)
                pool.affine_select(out=v, in_=v, compare_op=ALU.is_ge, fill=NEG, base=base,
                                   pattern=[[0, NG], [-1, keys]], channel_multiplier=1).then_inc(mask_ready, 1)
            pool.wait_ge(mask_ready, 1)
            pool.affine_select(out=mask1[:, 0:S], in_=mask1[:, 0:S], compare_op=ALU.is_ge, fill=NEG,
                               base=GROUPS[0][0] // GROUPS[0][1] - P, pattern=[[1, S]],
                               channel_multiplier=-1).then_inc(mask_ready, 1)

        @block.scalar
        def _(act):
            def hi(rnd, r, h):
                if h == 0:
                    act.wait_ge(raw_full[r], (rnd + 1) * 16)
                if not (isinstance(rnd, int) and rnd == 0 and r < 2):
                    act.wait_ge(used, rnd * 8 + (2 * r + h - 3))
                act.activation(whi[:, (2 * r + h) % NP_], raw[:, r, h * PIECE:(h + 1) * PIECE],
                               ACT.Copy).then_inc(hi_ready, 1)

            def ahead(rnd):
                for q in range(NP_):
                    hi(rnd, q // 2, q % 2)

            def preload(function):
                act.activation(small[:, 1:2], eps_c, function)

            def squares(c, ready):
                if ready:
                    act.wait_ge(x_ready, ready)
                act.drain()
                for t in range(TB):
                    act.activation(squared[:, t], x[:, t, c * N:(c + 1) * N], ACT.Square,
                                   accum_out=ssq_parts[:, t, c:c + 1])

            def root():
                act.drain()
                for t in range(TB):
                    act.activation(squared[:, t, 0:D // N], ssq_parts[:, t], ACT.Copy, accum_out=ssq[:, t:t + 1])
                act.drain()
                act.activation(ssq, ssq, ACT.Sqrt, bias=eps_c, scale=1.0 / D).then_inc(ssq_ready, 1)

            def norm_unit(n, u):
                if u >= 2:
                    act.wait_ge(hlo_ready, HL[n] + u - 1)
                act.wait_ge(tr_done, UNITS[f"norm{n}"] + u + 1)
                for b in range(2):
                    k = 2 * u + b
                    ins = act.activation(h32[:, u % 2, b], psT[u % 3][:, b * S:(b + 1) * S], ACT.Identity,
                                         bias=nsh[:, k:k + 1], scale=nsc[:, k:k + 1])
                ins.then_inc(tr_free, 1)
                act.drain()
                act.activation(hhi[:, 2 * u:2 * u + 2], h32[:, u % 2], ACT.Copy).then_inc(hhi_ready, 1)

            def norm_chunk(n, rnd, work=None):
                act.wait_ge(cols_ready, STEPS + n)
                for u in range(8):
                    norm_unit(n, u)
                    if 3 <= u < 7:
                        hi(rnd, (u + 1) // 2, (u + 1) % 2)
                    if work and u in work:
                        work[u]()

            def evac_stage(par, slots_done, units_done):
                act.wait_ge(used, slots_done * 2)
                act.wait_ge(tr_done, units_done)
                act.activation(stage[:, par], psG[par][:], ACT.Copy).then_inc(evac, 1)

            def chunk(rnd, prev_evac=None, prev_mid=None, prev_late=None, each=None):
                for q in range(2 * KS):
                    hi(rnd, q // 2, q % 2)
                    if q == 3 and prev_evac:
                        prev_evac()
                    if q == 5 and prev_mid:
                        prev_mid()
                    if each:
                        each(q)
                if prev_late:
                    prev_late()

            def gate_row(unit, k):
                act.wait_ge(tr_done, UNITS[unit] + k + 1)
                act.activation(gate[:, k * N:(k + 1) * N], psT[k % 3][:], ACT.Copy).then_inc(tr_free, 1)

            act.wait_ge(tr_free, UNITS["head_g"])
            act.activation(csil[:], cols("c"), ACT.Silu).then_inc(csil_ready, 1)
            for k in range(4):
                act.wait_ge(tr_done, UNITS["c"] + k + 1)
                act.activation(cbc[:, k * N:(k + 1) * N], psT[k % 3][:], ACT.Copy).then_inc(tr_free, 1)
            act.wait_ge(angle_ready, 1)
            act.activation(cs[:], trig[:, 0:2], ACT.Sin).then_inc(trig_ready, 1)
            ahead(0)
            act.wait_ge(x_loaded, 16)
            for c in range(D // N):
                squares(c, None)
            root()

            act.activation(cwhi, convw, ACT.Copy).then_inc(convw_hi, 1)

            def conv_input(i):
                act.wait_ge(u_ready, i + 1)
                act.wait_ge(taps_used, i * CONV_GROUPS + CONV_GROUPS)
                act.activation(uhi[:], upad, ACT.Copy).then_inc(u_hi, 1)

            def tap_diagonals(i, groups):
                for g in groups:
                    if g >= NTAPD:
                        act.wait_ge(taps_used, i * CONV_GROUPS + (CONV_GROUPS + g - NTAPD + 1))
                    b, j0 = g // GROUPS_PB, V_TAPS + g % GROUPS_PB * TAPG
                    for part, cw in enumerate((cwhi.bitcast(F32), cwlo)):
                        for j in range(TAPG):
                            ins = act.activation(tapd[:, g % NTAPD, part, j], ident[:], ACT.Copy,
                                                 scale=cw[:, bass.ds(i * 4 + ((j0 + j) * DB + b), 1)])
                    ins.then_inc(taps_ready, 1)

            r0, u0 = SLOTS["pw1"] // 4, UNITS["pw1"]

            def sigmoid(i):
                for u in range(2):
                    act.wait_ge(tr_done, i * 4 + (u0 + u + 1))
                    for b in range(2):
                        ins = act.activation(sigb[:, 2 * u + b], psT[u][:, b * S:(b + 1) * S], ACT.Sigmoid,
                                             bias=table[:, bass.ds(i * 4 + (ROWS["pw1_b"] + DB + 2 * u + b), 1)])
                    ins.then_inc(tr_free, 1)

            def pw1_pair(i, sigmoid_before=False):
                chunk(i * 2 + r0, lambda: evac_stage(1, (i * 2 + r0) * 4, i * 4 + (u0 - 4)),
                      each=(lambda q: sigmoid(i - 1) if q == 1 else None) if sigmoid_before else None)
                conv_input(i - 1)
                chunk(i * 2 + (r0 + 1),
                      lambda: evac_stage(0, (i * 2 + r0 + 1) * 4, i * 4 + (u0 - 2)),
                      each=lambda q: tap_diagonals(i - 1, (2 * q, 2 * q + 1)))
                sigmoid(i)

            for j in range(STEPS):
                if j:
                    for q in range(4 * j, 4 * j + 4):
                        hi(q // 8, q % 8 // 2, q % 2)
                act.wait_ge(cols_ready, j + 1)
                norm_unit(0, 2 * j)
                norm_unit(0, 2 * j + 1)
            evac_stage(0, 2 * STEPS - 1, u0)
            act.wait_ge(convw_lo, 1)
            pw1_pair(1, True)
            with act.Fori(2, PAIRS_PW1) as i:
                pw1_pair(i)
            evac_stage(1, SLOTS["pw2"], UNITS["ln"] - 4)
            conv_input(PAIRS_PW1 - 1)
            tap_diagonals(PAIRS_PW1 - 1, range(CONV_GROUPS))

            for b in range(0, DB, 4):
                act.wait_ge(ln_step, b // 4 + 1)
                act.activation(ysq[:, b:b + 4], yln[:, b:b + 4], ACT.Square).then_inc(ln_sq, 1)
            r0 = SLOTS["pw2"] // 4
            ahead(r0)
            act.wait_ge(ln_step, 5)
            act.activation(rs, rs, ACT.Sqrt, bias=eps_c).then_inc(ln_std, 1)
            for u in range(8):
                act.wait_ge(ln_step, 5 + u // 2 + 1)
                z = ysq[:, 2 * u:2 * u + 2]
                for b in range(2):
                    act.activation(z[:, b], yln[:, 2 * u + b], ACT.Silu, bias=col("ln_b", 2 * u + b),
                                   scale=col("ln_g", 2 * u + b))
                act.drain()
                act.activation(hhi[:, 2 * u:2 * u + 2], z, ACT.Copy).then_inc(hhi_ready, 1)
                if 3 <= u < 7:
                    hi(r0, (u + 1) // 2, (u + 1) % 2)
                if u == 7:
                    gate_row("gate0", 0)
            chunk(r0 + 1, each=lambda q: gate_row("gate0", q + 1) if q < 3 else None)
            for c in range(2, D // N):
                chunk(r0 + c, prev_late=lambda: squares(c - 2, XB["pw2"] + c - 1))
            ahead(SLOTS["up0"] // 4)
            preload(ACT.Sqrt)
            for c in (2, 3):
                squares(c, XB["pw2"] + c + 1)
            root()

            def ffn_up(name, n):
                r0, u0 = SLOTS[name] // 4, UNITS[name]

                def silu(i):
                    act.wait_ge(tr_free, i * 4 + (u0 + 2))
                    act.activation(convb, convb, ACT.Silu).then_inc(silu_ready, 1)

                def pair(i, first):
                    if first:
                        norm_chunk(n, r0)
                    else:
                        chunk(i * 2 + r0, lambda: (silu(i - 1), evac_stage(1, (i * 2 + r0) * 4, i * 4 + (u0 - 4))))
                    chunk(i * 2 + (r0 + 1),
                          lambda: evac_stage(0, (i * 2 + r0 + 1) * 4, u0 if first else i * 4 + (u0 - 2)))

                pair(0, True)
                with act.Fori(1, PAIRS_UP) as i:
                    pair(i, False)
                return (lambda: silu(PAIRS_UP - 1),
                        lambda: evac_stage(1, (r0 + 2 * PAIRS_UP) * 4, u0 + 4 * PAIRS_UP - 4))

            def ffn_down(name, layer, up_last):
                for half in range(2):
                    base = SLOTS[name] + half * 2 * DGROUPS
                    gb = half * DGROUPS
                    gall = layer * 2 * DGROUPS + gb

                    def group(i, g, rows={}):
                        s0 = base + 2 * g
                        ring = (gb + g) % 2
                        start = half == 0 and isinstance(i, int) and g == 0
                        if start:
                            act.wait_ge(used, 2 * SLOTS[name] - 6)
                        elif not (half == 0 and isinstance(i, int) and g + 2 * i < 2):
                            act.wait_ge(used, (i * 4 + (s0 - 2)) * 2)
                        act.activation(hhi[:, 4 * ring:4 * ring + 4],
                                       hidden[:, bass.ds(i * 8 + 4 * g, 4)], ACT.Copy).then_inc(hid_hi, 1)
                        if start:
                            up_last[0]()
                        for q in range(4):
                            if start and q == 3:
                                up_last[1]()
                            sl = s0 + q // 2
                            hi(i + sl // 4, sl % 4, q % 2)
                            if q in rows:
                                gate_row(("gate1", "gate3")[layer], rows[q])

                    group(0, 0)
                    if half == 0:
                        act.wait_ge(silu_ready, (layer + 1) * (PAIRS_UP + 1))
                        group(0, 1, {2: 0, 3: 1})
                        group(0, 2, {0: 2, 1: 3})
                    elif layer == 0:
                        for c in range(2):
                            squares(c, XB[name] + c + 1)
                    with act.Fori(1 - half, 4) as i:
                        group(i, 1)
                        group(i, 2)
                    group(4, 1)
                    group(4, 2)

            ffn_down("down0", 0, ffn_up("up0", 1))
            ahead(SLOTS["q"] // 4)
            preload(ACT.Sqrt)
            for c in (2, 3):
                squares(c, XB["down0"] + c + 1)
            root()

            def heads_root(n):
                act.wait_ge(head_ssq, n + 1)
                act.activation(hsd, hss, ACT.Sqrt, bias=eps_c, scale=1.0 / DH).then_inc(head_std, 1)

            def heads_evac(name, slots_done, n, par):
                act.wait_ge(used, slots_done * 2)
                act.wait_ge(tr_done, UNITS[name] + (n - (0 if name == "q" else QW // N)) * 2)
                act.activation(stage[:, 0], psG[par][:], ACT.Copy)
                act.activation(stage[:, 1], psG[par][:], ACT.Square).then_inc(evac, 1)

            def heads_out(name, n):
                dst = kT if name == "k" else qT
                for u in range(2):
                    act.wait_ge(tr_done, head_units(name, n) + u + 1)
                    act.activation(dst[:, bass.ds(n * 4 + 2 * u, 2)], psT[u][:].rearrange("p (b s) -> p b s", s=S),
                                   ACT.Copy).then_inc(tr_free, 1)

            def heads_work(name, n, par, slots_done):
                base = 0 if name == "q" else QW // N
                return (lambda: heads_evac(name, slots_done, n + base, par), lambda: heads_root(n + base),
                        lambda: heads_out(name, n))

            def heads_chunk(name, n, par):
                rnd = n + SLOTS[name] // 4
                chunk(rnd, *heads_work(name, n - 1, 1 - par, rnd * 4))

            def heads(name):
                heads_chunk(name, 1, 1)
                with act.Fori(1, 3) as i:
                    for j in range(2):
                        heads_chunk(name, i * 2 + j, j)

            def v_evac(slots_done, n, par):
                act.wait_ge(used, slots_done * 2)
                act.activation(vv[:, :, bass.ds(n * N, N)], psG[par][:], ACT.Copy).then_inc(evac, 1)

            norm_chunk(2, SLOTS["q"] // 4)
            heads("q")
            ahead(SLOTS["k"] // 4)
            last = heads_work("q", QW // N - 1, 1, SLOTS["k"])
            norm_chunk(3, SLOTS["k"] // 4, {3: last[0], 5: last[1], 7: last[2]})
            heads("k")
            r0 = SLOTS["v"] // 4

            def v_chunk(n, par):
                chunk(n + r0, lambda: v_evac((n + r0) * 4, n - 1, 1 - par))

            chunk(r0, *heads_work("k", QW // N - 1, 1, SLOTS["v"]))
            v_chunk(1, 1)
            with act.Fori(1, 3) as i:
                for j in range(2):
                    v_chunk(i * 2 + j, j)
            preload(ACT.Exp)
            v_evac(SLOTS["wo"], 5, 1)

            def prob_out(j):
                h, qb = j // 2, j % 2
                for u in range(1 + qb):
                    act.wait_ge(tr_done, UNITS["attn"] + 3 * h + qb + u + 1)
                    if u == 0 and j >= 2:
                        act.wait_ge(o_done, j - 1)
                    k0, k1 = (0, 3) if qb == 0 else ((0, 4), (4, 6))[u]
                    act.activation(probT[j % 2][:, k0:k1].rearrange("p b q -> p (b q)"),
                                   psT[qb + u][:, 0:(k1 - k0) * P], ACT.Copy).then_inc(tr_free, 1)

            def o_split(h):
                act.wait_ge(o_done, 2 * h + 2)
                act.activation(hhi[:, h], psM[:, 0:S], ACT.Copy).then_inc(hhi_ready, 1)

            for j in range(2 * HPG + 1):
                if j < 2 * HPG:
                    act.wait_ge(max_ready, j + 1)
                    w = NKEY[j % 2]
                    act.activation(prob[j % 3][:, 0:w], prob[j % 3][:, 0:w], ACT.Exp, bias=nmx[:, j % 2:j % 2 + 1],
                                   scale=SCALE, accum_out=den[:, j % 2:j % 2 + 1]).then_inc(exp_ready, 1)
                if j >= 3 and j % 2 == 1:
                    o_split((j - 3) // 2)
                if j >= 1:
                    prob_out(j - 1)
            o_split(HPG - 1)

            r0 = SLOTS["wo"] // 4
            for c in range(D // N):
                for q in range(4):
                    hi(r0 + c // 2, c % 2 * 2 + q // 2, q % 2)
                    if q == 1 and c >= 2:
                        squares(c - 2, XB["wo"] + c - 1)
                    k = 4 * c + q - 2
                    if 0 <= k < 4:
                        gate_row("gate2", k)
            ahead(SLOTS["up1"] // 4)
            preload(ACT.Sqrt)
            for c in (2, 3):
                squares(c, XB["wo"] + c + 1)
            root()
            ffn_down("down1", 1, ffn_up("up1", 4))

        @block.vector
        def _(dve):
            TT, TS, STT = dve.tensor_tensor, dve.tensor_scalar, dve.scalar_tensor_tensor

            def lo(rnd, r, h):
                dve.wait_ge(hi_ready, rnd * 8 + (2 * r + h + 1))
                q = (2 * r + h) % NP_
                TT(wlo[:, q], raw[:, r, h * PIECE:(h + 1) * PIECE], whi[:, q].bitcast(F32),
                   ALU.subtract).then_inc(lo_ready, 1)

            def mod_mul(m, part):
                for u in part:
                    dve.wait_ge(mod_full[u % NMRAW], m * 32 + 16 * (u // NMRAW + 1))
                    if u == 0 and not (isinstance(m, int) and m == 0):
                        dve.wait_ge(mod_ops, m * (MPC + 1))
                    half = u % 4 // 2
                    w, total = mraw[:, u % NMRAW], u // 4 * 2 + u % 2
                    first = m % 2 * DB + m // 2 * 4 if isinstance(m, int) and m < 2 * STEPS else m * 4
                    STT(w, w, 1.0, cbc[:, half * MSLOT:(half + 1) * MSLOT], ALU.mult, ALU.mult,
                        accum_out=halfsum[:, half, total:total + 1]).then_inc(mod_ops, 1)
                if MPC - 1 in part:
                    dve.wait_ge(mod_ops, m * (MPC + 1) + MPC)
                    TT(modcol[:, bass.ds(first, 4)], halfsum[:, 0], halfsum[:, 1], ALU.add).then_inc(mod_ops, 1)

            def chunk(rnd, work=None, mod=None):
                for q in range(2 * KS):
                    lo(rnd, q // 2, q % 2)
                    if work and q in work:
                        work[q]()
                    if mod is not None and q < 7:
                        mod_mul(mod, (0, 1) if q == 0 else (q + 1,))

            def ahead(rnd, pieces=range(NP_)):
                for q in pieces:
                    lo(rnd, q // 2, q % 2)

            def norm_columns(n, k=0, count=DB):
                gain, g0, sh, sc, chunks_needed = NORMS[n]
                dve.wait_ge(mod_ops, (MPC + 1) * (chunks_needed if n else (k + count) // 2))
                nsc_, nsh_ = nsc[:, k:k + count], nsh[:, k:k + count]
                TT(nsc_, modcol[:, sc + k:sc + k + count], cols("mod_b", sc + k, count), ALU.add)
                TT(nsh_, modcol[:, sh + k:sh + k + count], cols("mod_b", sh + k, count), ALU.add)
                dve.drain()
                STT(nsc_, nsc_, 1.0, cols(gain, g0 + k, count), ALU.add, ALU.mult).then_inc(cols_ready, 1)

            def normalise(n):
                dve.wait_ge(ssq_ready, n)
                dve.reciprocal(rstd, ssq)
                dve.drain()
                for c in range(D // N):
                    for t in range(TB):
                        ins = TS(xn[:, t, c * N:(c + 1) * N], x[:, t, c * N:(c + 1) * N], rstd[:, t:t + 1], None,
                                 ALU.mult)
                    ins.then_inc(xn_ready, 1)

            def low(n, u):
                dve.wait_ge(hhi_ready, HB[n] + u + 1)
                TT(hlo[:, 2 * u:2 * u + 2], h32[:, u % 2], hhi[:, 2 * u:2 * u + 2].bitcast(F32),
                   ALU.subtract).then_inc(hlo_ready, 1)

            def norm_chunk(n, rnd, mod=None, work=None):
                for u in range(8):
                    low(n, u)
                    if 3 <= u < 7:
                        lo(rnd, (u + 1) // 2, (u + 1) % 2)
                    if mod is not None and u >= 1:
                        mod_mul(mod, (u - 1,))
                    if work and u in work:
                        work[u]()
                if mod is not None:
                    mod_mul(mod, (7,))
                dve.drain()

            def diagonal(vec, unit, k):
                if k >= 2:
                    dve.wait_ge(tr_done, UNITS[unit] + k - 1)
                for b in range(4):
                    ins = TS(diag[:, 4 * (k % 2) + b], ident[:], vec[:, 4 * k + b:4 * k + b + 1], None, ALU.mult)
                ins.then_inc(diag_ready, 1)

            def gate_cols(g, chunks_needed):
                dve.wait_ge(mod_ops, (MPC + 1) * chunks_needed)
                TT(nsh[:], modcol[:, g:g + DB], cols("mod_b", g), ALU.add)
                dve.drain()

            def residual(chunks, slots_done):
                dve.wait_ge(used, slots_done * 2)
                tmp = [stage[:, 2 - len(chunks) + k] for k in range(len(chunks))]
                for k, (par, col0) in enumerate(chunks):
                    for t in range(TB):
                        ins = TT(tmp[k][:, t], psG[par][:, t], gate[:, col0:col0 + N], ALU.mult)
                    ins.then_inc(evac, 1)
                dve.drain()
                for k, (_, col0) in enumerate(chunks):
                    xs = x[:, :, col0:col0 + N]
                    TT(xs, xs, tmp[k], ALU.add).then_inc(x_ready, 1)
                dve.drain()

            dve.memset(eps_c, EPS)
            freq = inv_freq()
            for i in range(HR):
                dve.memset(trig[:, 7, :, i:i + 1], float(freq[i]))
            for u in range(UNITS["head_g"]):
                dve.wait_ge(tr_done, u + 1)
                k0, k1 = 4 * u * P, min(4 * u + 4, NRB) * P
                if k0 < NKEPT < k1:
                    dve.tensor_copy(convw[:, 0:k1 - NKEPT], psT[u][:, NKEPT - k0:k1 - k0])
                if k0 < NKEPT:
                    k1 = min(k1, NKEPT)
                    dve.tensor_copy(table[:, k0:k1], psT[u][:, 0:k1 - k0]).then_inc(tr_free, 1)
                else:
                    dve.tensor_copy(convw[:, k0 - NKEPT:k1 - NKEPT], psT[u][:, 0:k1 - k0]).then_inc(tr_free, 1)
            dve.drain()
            dve.wait_ge(const_ready, 3)
            for i in range(2):
                ins = TS(headg[:, i], ident[:], col("head_g", i), None, ALU.mult)
            ins.then_inc(diag_ready, 1)
            dve.wait_ge(tr_done, UNITS["head_g"] + 1)
            dve.tensor_copy(headg[:], psT[0][:, 0:2 * DH].rearrange("p (a b) -> p a b", a=2)).then_inc(tr_free, 1)
            dve.wait_ge(csil_ready, 1)
            for k in range(4):
                diagonal(csil, "c", k)
            k_, r_, a_, b_ = trig[:, 4], trig[:, 1], trig[:, 2], trig[:, 3]
            dve.wait_ge(params_in, 32)
            dve.tensor_copy(posf[:], posi[:])
            dve.drain()
            for t in range(TB):
                TS(a_[:, t], trig[:, 7, t], posf[:, t:t + 1], None, ALU.mult)
            dve.drain()
            TS(b_, a_, 1.0 / (2 * PI), ROUND, ALU.mult, ALU.add)
            dve.drain()
            TS(k_, b_, ROUND, None, ALU.subtract)
            dve.drain()
            STT(b_, k_, -TWO_PI[0], a_, ALU.mult, ALU.add)
            dve.drain()
            STT(a_, k_, -TWO_PI[1], b_, ALU.mult, ALU.add)
            dve.drain()
            STT(b_, k_, -TWO_PI[2], a_, ALU.mult, ALU.add)
            dve.drain()
            TS(r_, b_, PI_BELOW, -PI_BELOW, ALU.min, ALU.max)
            TS(a_, b_, PI / 2, None, ALU.add)
            dve.drain()
            TS(k_, a_, PI, -2 * PI, ALU.is_gt, ALU.mult)
            dve.drain()
            TT(b_, a_, k_, ALU.add)
            dve.drain()
            TS(trig[:, 0], b_, PI_BELOW, -PI_BELOW, ALU.min, ALU.max).then_inc(angle_ready, 1)
            dve.wait_ge(tr_free, UNITS["c"] + 4)

            for j in range(STEPS):
                for u in range(MPC):
                    mod_mul(2 * j, (u,))
                    if j and u in (1, 2):
                        low(0, 2 * j - 3 + u)
                for u in range(MPC):
                    if u < 4:
                        q = 4 * j + u
                        lo(q // 8, q % 8 // 2, q % 2)
                    mod_mul(2 * j + 1, (u,))
                if j == 0:
                    dve.wait_ge(trig_ready, 1)
                    normalise(1)
                norm_columns(0, 4 * j, 4)
            low(0, 6)
            low(0, 7)
            dve.wait_ge(convw_hi, 1)
            TT(cwlo, convw, cwhi.bitcast(F32), ALU.subtract).then_inc(convw_lo, 1)

            r0, u0 = SLOTS["pw1"] // 4, UNITS["pw1"]
            dve.memset(upad[:, :, 0:UPAD], 0.0)
            dve.drain()

            def glu(i):
                dve.wait_ge(tr_free, i * 4 + (u0 + 2))
                for u in range(2):
                    dve.wait_ge(tr_done, i * 4 + (u0 + 2 + u + 1))
                    for b in range(2):
                        k = 2 * u + b
                        ins = STT(upad[:, k, UPAD:UPAD + S], psT[u][:, b * S:(b + 1) * S],
                                  table[:, bass.ds(i * 4 + (ROWS["pw1_b"] + k), 1)], sigb[:, k], ALU.add, ALU.mult)
                    ins.then_inc(tr_free, 1)
                dve.drain()
                dve.sem_inc(u_ready, 1)

            def conv_low(i):
                dve.wait_ge(u_hi, i + 1)
                TT(ulo[:], upad, uhi[:].bitcast(F32), ALU.subtract).then_inc(u_lo, 1)

            def conv(i, taps):
                for j in taps:
                    for b in range(4):
                        y = yln[:, bass.ds(i * 4 + b, 1)]
                        w = convw[:, bass.ds(i * 4 + (j * DB + b), 1)]
                        src = upad[:, b:b + 1, j:j + S]
                        if j == 0:
                            TS(y, src, w, table[:, bass.ds(i * 4 + (ROWS["dw_b"] + b), 1)], ALU.mult, ALU.add)
                        else:
                            STT(y, src, w, y, ALU.mult, ALU.add)
                    dve.drain()

            def conv_join(i):
                dve.wait_ge(taps_used, i * CONV_GROUPS + 2 * CONV_GROUPS)
                for half in range(2):
                    y = yln[:, bass.ds(i * 4 + 2 * half, 2)]
                    ins = TT(y, psC[half][:].rearrange("p (b s) -> p b s", s=S), y, ALU.add)
                ins.then_inc(conv_ready, 1)
                dve.drain()

            def pw1_pair(i, join_at):
                def beside_gate(q):
                    if q == join_at:
                        conv_join(i - 2)
                    if q == 5:
                        glu(i - 1)
                    if q == 7:
                        conv_low(i - 1)
                    if q > 5:
                        conv(i - 1, range(q - 6, q - 5))

                chunk(i * 2 + r0, {q: lambda q=q: beside_gate(q) for q in range(2 * KS)},
                      mod=i * 2 + (MODS["pw1"] - 2))
                chunk(i * 2 + (r0 + 1),
                      {q: lambda q=q: conv(i - 1, range(2 + 2 * q, min(4 + 2 * q, V_TAPS))) for q in range(2 * KS)},
                      mod=i * 2 + (MODS["pw1"] - 1))

            pw1_pair(1, None)
            with dve.Fori(2, PAIRS_PW1) as i:
                pw1_pair(i, 3)
            conv_join(PAIRS_PW1 - 2)
            glu(PAIRS_PW1 - 1)
            conv(PAIRS_PW1 - 1, range(1))
            conv_low(PAIRS_PW1 - 1)
            for k in range(1, V_TAPS):
                conv(PAIRS_PW1 - 1, range(k, k + 1))
                if k <= 12:
                    mod_mul(MODS["conv"] + (k - 1) // MPC, ((k - 1) % MPC,))
            conv_join(PAIRS_PW1 - 1)

            mod_mul(MODS["conv"] + 1, (4, 5))
            dve.wait_ge(tr_done, UNITS["ln"] + 1)
            TS(mu, psT[0][:, 0:S], 1.0 / D, None, ALU.mult).then_inc(tr_free, 1)
            dve.drain()
            mub = mu.rearrange("p (a s) -> p a s", a=1).to_broadcast([P, 4, S])
            for b in range(0, DB, 4):
                TT(yln[:, b:b + 4], yln[:, b:b + 4], mub, ALU.subtract).then_inc(ln_step, 1)
            r0 = SLOTS["pw2"] // 4
            ahead(r0)
            mod_mul(MODS["conv"] + 1, (6, 7))
            dve.wait_ge(tr_done, UNITS["ln"] + 2)
            TS(rs, psT[1][:, 0:S], 1.0 / D, None, ALU.mult).then_inc(tr_free, 1)
            dve.drain()
            dve.sem_inc(ln_step, 1)
            dve.wait_ge(ln_std, 1)
            dve.reciprocal(mu, rs)
            dve.drain()

            def ln_low(u):
                dve.wait_ge(hhi_ready, LNH + u + 1)
                TT(hlo[:, 2 * u:2 * u + 2], ysq[:, 2 * u:2 * u + 2], hhi[:, 2 * u:2 * u + 2].bitcast(F32),
                   ALU.subtract).then_inc(hlo_ready, 1)

            for k in range(4):
                TT(yln[:, 4 * k:4 * k + 4], yln[:, 4 * k:4 * k + 4], mub, ALU.mult).then_inc(ln_step, 1)
                if k:
                    ln_low(k - 1)
            gate_cols(MC0 + 2 * DB, 12)
            for u in range(3, 8):
                ln_low(u)
                if u < 7:
                    lo(r0, (u + 1) // 2, (u + 1) % 2)
                    diagonal(nsh, "gate0", u - 3)
                    mod_mul(MODS["pw2"], (2 * u - 6, 2 * u - 5))
            dve.wait_ge(tr_done, UNITS["gate0"] + 4)
            TT(nsc[:], nsh[:], cols("pw2_b"), ALU.mult)
            dve.drain()

            def add_bias(k):
                dve.wait_ge(tr_free, UNITS["gate0"] + 4)
                dve.wait_ge(tr_done, UNITS["bias0"] + k + 1)
                for t in range(TB):
                    xs = x[:, t, k * N:(k + 1) * N]
                    ins = TT(xs, psT[k % 3][:], xs, ALU.add)
                ins.then_inc(tr_free, 1)

            def bias_step(q):
                if q < 4:
                    diagonal(nsc, "bias0", q)
                if 1 <= q < 5:
                    add_bias(q - 1)
                if q == 5:
                    dve.drain()
                    residual([(0, 0)], (r0 + 1) * 4)

            chunk(r0 + 1, {q: lambda q=q: bias_step(q) for q in range(6)}, mod=MODS["pw2"] + 1)
            for c in range(2, D // N):
                rnd = r0 + c
                chunk(rnd, {3: lambda: residual([((c - 1) % 2, (c - 1) * N)], rnd * 4)}, mod=MODS["pw2"] + c)
            ahead(SLOTS["up0"] // 4, range(3))
            norm_columns(1)
            residual([(1, D - N)], SLOTS["up0"])
            ahead(SLOTS["up0"] // 4, (3,))
            normalise(2)

            def ffn_up(name, layer, n, mods):
                r0, u0 = SLOTS[name] // 4, UNITS[name]
                wrow, brow = ROWS["ffn_w"] + layer * FFN_K * FB, ROWS["ffn_b"] + layer * FB

                def conv3(i, u):
                    dve.wait_ge(tr_done, i * 4 + (u0 + u + 1))
                    for j in reversed(range(FFN_K)):
                        back = FFN_K - 1 - j
                        for b in range(2):
                            k = 2 * u + b
                            g = psT[u][:, b * S:(b + 1) * S - back]
                            w = table[:, bass.ds(i * 4 + (wrow + j * FB + k), 1)]
                            y = convb[:, k, back:S]
                            if back == 0:
                                ins = TS(y, g, w, table[:, bass.ds(i * 4 + (brow + k), 1)], ALU.mult, ALU.add)
                            else:
                                ins = STT(y, g, w, y, ALU.mult, ALU.add)
                        if j:
                            dve.drain()
                    ins.then_inc(tr_free, 1)

                def multiply(i):
                    dve.wait_ge(silu_ready, i + (layer * (PAIRS_UP + 1) + 1))
                    for u in range(2):
                        dve.wait_ge(tr_done, i * 4 + (u0 + 2 + u + 1))
                        ins = TT(hidden[:, bass.ds(i * 4 + 2 * u, 2)], convb[:, 2 * u:2 * u + 2],
                                 psT[(2, 0)[u]][:].rearrange("p (b s) -> p b s", s=S), ALU.mult)
                        ins.then_inc(tr_free, 1)
                    dve.drain()

                def pair(i, first, mod):
                    m = i + MODS[name] if mod else None
                    if first:
                        norm_chunk(n, r0, m)
                    else:
                        chunk(i * 2 + r0, {5: lambda: multiply(i - 1)}, mod=m)
                    chunk(i * 2 + (r0 + 1), {5: lambda: conv3(i, 0), 6: lambda: conv3(i, 1)},
                          mod=m + 1 if mod == 2 else None)

                pair(0, True, mods > 0)
                with dve.Fori(1, min(mods, PAIRS_UP - 1)) as i:
                    pair(i, False, True)
                if mods == PAIRS_UP:
                    pair(PAIRS_UP - 1, False, 2)
                if mods < PAIRS_UP:
                    with dve.Fori(mods, PAIRS_UP) as i:
                        pair(i, False, False)

                def finish():
                    multiply(PAIRS_UP - 1)
                    dve.sem_inc(silu_ready, 1)
                return finish

            def ffn_down(name, layer, m0, up_last):
                def columns(half):
                    parts = [(nt, (2 * half + nt) * N) for nt in range(2)]
                    done = SLOTS[name] + (half + 1) * 2 * DGROUPS
                    if half == 0:
                        residual(parts, done)
                    else:
                        residual(parts[:1], done)
                        residual(parts[1:], done)

                for half in range(2):
                    base = SLOTS[name] + half * 2 * DGROUPS
                    gb = half * DGROUPS

                    def group(i, g, mod=None, part=(), before_last=None, gate=None):
                        s0 = base + 2 * g
                        ring = (gb + g) % 2
                        dve.wait_ge(hid_hi, i * 2 + (layer * 2 * DGROUPS + gb + g + 1))
                        TT(hlo[:, 4 * ring:4 * ring + 4], hidden[:, bass.ds(i * 8 + 4 * g, 4)],
                           hhi[:, 4 * ring:4 * ring + 4].bitcast(F32), ALU.subtract).then_inc(hid_lo, 1)
                        for q in range(4):
                            sl = s0 + q // 2
                            if q == 3 and before_last:
                                before_last()
                            lo(i + sl // 4, sl % 4, q % 2)
                            if gate:
                                diagonal(nsh, gate, q)
                            if mod is not None:
                                mod_mul(mod, (part[q],))

                    def two(i, m, gate=None):
                        group(i, 1, m, (0, 1, 2, 3), gate=gate)
                        group(i, 2, m, (4, 5, 6, 7))

                    m = None if m0 is None else m0 - 1 + 5 * half
                    if half == 0:
                        group(0, 0)
                        up_last()
                        gate_cols((MC0, MC1)[layer] + 5 * DB, (24, 56)[layer])
                        two(0, None, ("gate1", "gate3")[layer])
                    else:
                        group(0, 0, before_last=lambda: columns(0))
                    with dve.Fori(1 - half, 4) as i:
                        two(i, None if m0 is None else i + m)
                    two(4, None if m is None else m + 4)
                if layer == 0:
                    ahead(SLOTS["q"] // 4, range(3))
                    norm_columns(2)
                columns(1)
                if layer == 0:
                    ahead(SLOTS["q"] // 4, (3,))

            ffn_down("down0", 0, MODS["down0"], ffn_up("up0", 0, 1, PAIRS_UP))
            normalise(3)

            heads8 = stage[:, 0].rearrange("p t (h c) -> p (t h) c", c=DH)
            sq8 = stage[:, 1].rearrange("p t (h c) -> p (t h) c", c=DH)
            heads = stage[:, 0].rearrange("p t (h c) -> p t h c", c=DH)
            rtmp = stage[:, 1].rearrange("p t (k h c) -> p k t h c", k=8, c=HR)
            cosb, sinb = (cs[:, n].rearrange("p t (a f) -> p t a f", a=1).to_broadcast([P, TB, 4, HR])
                          for n in range(2))

            def heads_squares(n):
                dve.wait_ge(evac, n)
                dve.tensor_reduce(hss, sq8, AX, ALU.add).then_inc(head_ssq, 1)

            def heads_norm(n, which):
                dve.wait_ge(head_std, n)
                dve.reciprocal(hrs, hsd)
                dve.drain()
                for k in range(8):
                    STT(heads8[:, k], heads8[:, k], hrs[:, k:k + 1], headg[:, which], ALU.mult, ALU.mult)
                dve.drain()
                x1, x2 = heads[:, :, :, 0:HR], heads[:, :, :, HR:ROT]
                TT(rtmp[:, 0], x1, cosb, ALU.mult)
                TT(rtmp[:, 1], x2, sinb, ALU.mult)
                TT(rtmp[:, 2], x2, cosb, ALU.mult)
                TT(rtmp[:, 3], x1, sinb, ALU.mult)
                dve.drain()
                TT(x1, rtmp[:, 0], rtmp[:, 1], ALU.subtract)
                TT(x2, rtmp[:, 2], rtmp[:, 3], ALU.add).then_inc(head_ready, 1)

            def heads_work(name, n):
                base = 0 if name == "q" else QW // N
                return {3: lambda: heads_squares(n + (CHUNKS[name] + 1)),
                        5: lambda: heads_norm(n + (base + 1), name == "q")}

            def heads_stage(name):
                m0 = MODS[name]
                chunk(SLOTS[name] // 4 + 1, heads_work(name, 0), mod=m0)
                with dve.Fori(1, 3) as i:
                    for j in range(2):
                        chunk(i * 2 + (SLOTS[name] // 4 + j), heads_work(name, i * 2 + (j - 1)),
                              mod=i + m0 if j == 1 else None)

            norm_chunk(2, SLOTS["q"] // 4)
            heads_stage("q")
            ahead(SLOTS["k"] // 4)
            norm_columns(3)
            norm_chunk(3, SLOTS["k"] // 4, work=heads_work("q", QW // N - 1))
            heads_stage("k")
            chunk(SLOTS["v"] // 4, heads_work("k", QW // N - 1), mod=MODS["v"])
            chunk(SLOTS["v"] // 4 + 1)

            for n, mk in enumerate((mask1, mask0)):
                v = mk.rearrange("p (g s) -> p g s", g=NG)
                dve.wait_ge(iota_ready, n + 1)
                for g, (_, dil) in enumerate(GROUPS):
                    TS(v[:, g].bitcast(I32), v[:, g].bitcast(I32), dil - 1, None, ALU.bitwise_and)
                dve.drain()
                TS(mk, mk.bitcast(I32), 0, NEG, ALU.is_gt, ALU.mult).then_inc(dil_ready, 1)
            with dve.Fori(1, 3) as i:
                for j in range(2):
                    chunk(i * 2 + (SLOTS["v"] // 4 + j), mod=i * 2 + (MODS["v"] - 1 + j))
            dve.drain()
            dve.wait_ge(mask_ready, 3)

            def softmax_max(j):
                w = NKEY[j % 2]
                dve.wait_ge(score_done, j + 1)
                if j >= 3:
                    dve.wait_ge(tr_done, UNITS["attn"] + ATTN_UNITS[j - 3])
                TT(prob[j % 3][:, 0:w], psG[j % 2][:].rearrange("p t n -> p (t n)")[:, 0:w],
                   masks[1 - j % 2], ALU.add).then_inc(score_read, 1)
                dve.drain()
                dve.reduce_max(mx[:, j % 2:j % 2 + 1], prob[j % 3][:, 0:w], AX)
                dve.drain()
                TS(nmx[:, j % 2:j % 2 + 1], mx[:, j % 2:j % 2 + 1], -SCALE, None, ALU.mult).then_inc(max_ready, 1)

            def softmax_divide(j):
                w = NKEY[j % 2]
                dve.wait_ge(exp_ready, j + 1)
                dve.reciprocal(rden[:, j % 2:j % 2 + 1], den[:, j % 2:j % 2 + 1])
                dve.drain()
                p = prob[j % 3][:, 0:w]
                TS(p, p, rden[:, j % 2:j % 2 + 1], None, ALU.mult).then_inc(prob_ready, 1)

            def o_low(h):
                dve.wait_ge(hhi_ready, HO + h + 1)
                TT(hlo[:, h], psM[:, 0:S], hhi[:, h].bitcast(F32), ALU.subtract).then_inc(o_read, 1)

            for j in range(2 * HPG + 1):
                if j < 2 * HPG:
                    softmax_max(j)
                if j >= 1:
                    softmax_divide(j - 1)
                if j >= 3 and j % 2 == 1:
                    o_low((j - 3) // 2)
            o_low(HPG - 1)
            dve.drain()

            for c in range(D // N):
                rnd, r = SLOTS["wo"] // 4 + c // 2, c % 2 * 2
                if c == 0:
                    gate_cols(MC1 + 2 * DB, 44)
                for q in range(4):
                    lo(rnd, r + q // 2, q % 2)
                    if c == 0:
                        diagonal(nsh, "gate2", q)
                if c == 1:
                    dve.wait_ge(tr_free, UNITS["gate2"] + 4)
                if c:
                    residual([((c - 1) % 2, (c - 1) * N)], rnd * 4 + r)
            ahead(SLOTS["up1"] // 4, range(3))
            norm_columns(4)
            residual([(1, D - N)], SLOTS["up1"])
            ahead(SLOTS["up1"] // 4, (3,))
            normalise(4)
            ffn_down("down1", 1, None, ffn_up("up1", 1, 4, 4))

        @block.tensor
        def _(pe):
            def split_matmul(out_, act_hi, act_lo, q, col0, first, last, done=False):
                w = slice(col0, col0 + N)
                pe.matmul(out_, act_hi, whi[:, q, w], start=first, stop=False)
                pe.matmul(out_, act_hi, wlo[:, q, w], start=False, stop=False)
                ins = pe.matmul(out_, act_lo, whi[:, q, w], start=False, stop=last)
                if done:
                    ins.then_inc(used, 1)

            def chunk(rnd, c, par, work=None, r0=0, slots=KS, units_before=None):
                if not (isinstance(c, int) and c < 2):
                    pe.wait_ge(evac, c - 1)
                for q in range(2 * slots):
                    pe.wait_ge(lo_ready, rnd * 8 + (2 * r0 + q + 1))
                    if units_before is not None:
                        pe.wait_ge(hlo_ready, units_before + q + 1)
                    for kb in range(2):
                        for t in range(TB):
                            b, ts = 2 * q + kb, slice(t * P, (t + 1) * P)
                            split_matmul(psG[par][:, t], hhi[:, b, ts], hlo[:, b, ts], (2 * r0 + q) % NP_, kb * N,
                                         b == 0, b == 4 * slots - 1, kb == 1 and t == TB - 1)
                    if work and q in work:
                        work[q]()

            def transposes(src_of, bank, free):
                pe.wait_ge(tr_free, free)
                for b in range(2):
                    for t in range(TB):
                        ins = pe.transpose(psT[bank][:, b * S + t * P:b * S + (t + 1) * P], src_of(b, t), ident[:])
                ins.then_inc(tr_done, 1)

            def norm_unit(n, u):
                u0 = UNITS[f"norm{n}"]
                pe.wait_ge(xn_ready, STEPS * (ROOT[n] - 1) + u // 2 + 1)
                transposes(lambda b, t: xn[:, t, (2 * u + b) * P:(2 * u + b + 1) * P], u % 3, max(u0, u0 + u - 2))

            def first_stage():
                for j in range(STEPS):
                    norm_unit(0, 2 * j)
                    norm_unit(0, 2 * j + 1)
                    for c in range(2):
                        for h in range(2):
                            piece, unit = 4 * j + 2 * c + h, 2 * j + h
                            pe.wait_ge(lo_ready, piece + 1)
                            pe.wait_ge(hlo_ready, unit + 1)
                            for kb in range(2):
                                for t in range(TB):
                                    b, ts = 2 * unit + kb, slice(t * P, (t + 1) * P)
                                    split_matmul(psG[c][:, t], hhi[:, b, ts], hlo[:, b, ts], piece % NP_, kb * N,
                                                 b == 0, b == DB - 1, kb == 1 and t == TB - 1)

            def norm_chunk(n, rnd, c, late=None):
                for u in range(3):
                    norm_unit(n, u)
                steps = {q: lambda q=q: norm_unit(n, q + 3) for q in range(5)}
                if late:
                    steps[6] = late
                chunk(rnd, c, 0, steps, units_before=HL[n])

            def broadcast(unit, k):
                u0 = UNITS[unit]
                pe.wait_ge(diag_ready, DIAGONALS[unit] + k + 1)
                pe.wait_ge(tr_free, max(u0, u0 + k - 2))
                pe.matmul(psT[k % 3][:], ones[:], diag[:, 4 * (k % 2):4 * (k % 2) + 4].rearrange("p b c -> p (b c)"),
                          start=True, stop=True).then_inc(tr_done, 1)

            pe.wait_ge(const_ready, 3)
            pe.wait_ge(params_in, 32)
            for u in range(UNITS["head_g"]):
                for k in range(4 * u, min(4 * u + 4, NRB)):
                    ins = pe.transpose(psT[u][:, (k - 4 * u) * P:(k - 4 * u + 1) * P], tbl_in[:, k * P:(k + 1) * P],
                                       ident[:])
                ins.then_inc(tr_done, 1)
            pe.wait_ge(diag_ready, 1)
            pe.wait_ge(tr_free, UNITS["head_g"])
            pe.matmul(psT[0][:, 0:2 * DH], ones[:], headg[:].rearrange("p a b -> p (a b)"), start=True,
                      stop=True).then_inc(tr_done, 1)

            for k in range(4):
                broadcast("c", k)

            def pair_transposes(i, u0, value, value_banks):
                n = i * 4 + (u0 + 2 * value)
                for u in range(2):
                    transposes(lambda b, t: stage[:, value, t, (2 * u + b) * P:(2 * u + b + 1) * P],
                               ((0, 1), value_banks)[value][u],
                               n if not value else n - value_banks[0] // 2 - 1 + u)

            def pairs(name, n, count, value_banks=(2, 0), conv=None):
                r0, u0, c0 = SLOTS[name] // 4, UNITS[name], CHUNKS[name]

                def value_transposes(i):
                    pe.wait_ge(evac, i * 2 + (c0 + 2))
                    pair_transposes(i, u0, 1, value_banks)

                def gate_transposes(i):
                    pe.wait_ge(evac, i * 2 + (c0 + 1))
                    pair_transposes(i, u0, 0, value_banks)

                def pair(i, first):
                    if first:
                        norm_chunk(n, r0, c0)
                    else:
                        chunk(i * 2 + r0, i * 2 + c0, 0, {1: lambda: value_transposes(i - 1)})
                    work = {1: lambda: gate_transposes(i)}
                    if conv and not first:
                        def beside(q):
                            def both():
                                if q == 1:
                                    gate_transposes(i)
                                conv(i - 1, (2 * q, 2 * q + 1))
                            return both
                        work = {q: beside(q) for q in range(2 * KS)}
                    chunk(i * 2 + (r0 + 1), i * 2 + (c0 + 1), 1, work)

                if n == 0:
                    first_stage()
                    gate_transposes(0)
                else:
                    pair(0, True)
                with pe.Fori(1, count) as i:
                    pair(i, False)
                return lambda: value_transposes(count - 1)

            def conv_groups(i, groups):
                for g in groups:
                    pe.wait_ge(u_lo, i + 1)
                    pe.wait_ge(taps_ready, i * CONV_GROUPS + g + 1)
                    b, j0 = g // GROUPS_PB, V_TAPS + g % GROUPS_PB * TAPG
                    acc = psC[b // 2][:, b % 2 * S:(b % 2 + 1) * S]
                    for j in range(TAPG):
                        at = slice(j0 + j, j0 + j + S)
                        dhi, dlo = (tapd[:, g % NTAPD, part, j] for part in range(2))
                        pe.matmul(acc, dhi, uhi[:, b, at], start=g % GROUPS_PB == 0 and j == 0, stop=False)
                        pe.matmul(acc, dhi, ulo[:, b, at], start=False, stop=False)
                        ins = pe.matmul(acc, dlo, uhi[:, b, at], start=False,
                                        stop=g % GROUPS_PB == GROUPS_PB - 1 and j == TAPG - 1)
                    ins.then_inc(taps_used, 1)

            pe.sem_inc(taps_used, CONV_GROUPS)
            pairs("pw1", 0, PAIRS_PW1, (0, 1), conv_groups)()
            pe.wait_ge(conv_ready, PAIRS_PW1 - 1)
            pe.wait_ge(tr_free, UNITS["ln"])
            for b in range(DB - 4):
                pe.matmul(psT[0][:, 0:S], ones[:], yln[:, b], start=b == 0, stop=False)
            conv_groups(PAIRS_PW1 - 1, range(CONV_GROUPS))

            pe.wait_ge(conv_ready, PAIRS_PW1)
            for b in range(DB - 4, DB):
                ins = pe.matmul(psT[0][:, 0:S], ones[:], yln[:, b], start=False, stop=b == DB - 1)
            ins.then_inc(tr_done, 1)
            for b in range(DB):
                if b % 4 == 0:
                    pe.wait_ge(ln_sq, b // 4 + 1)
                ins = pe.matmul(psT[1][:, 0:S], ones[:], ysq[:, b], start=b == 0, stop=b == DB - 1)
            ins.then_inc(tr_done, 1)

            for c in range(D // N):
                chunk(SLOTS["pw2"] // 4 + c, CHUNKS["pw2"] + c, c % 2,
                      [{q + 4: lambda q=q: broadcast("gate0", q) for q in range(4)},
                       {q: lambda q=q: broadcast("bias0", q) for q in range(4)}, None, None][c],
                      units_before=LNH if c == 0 else None)

            def ffn_down(name, layer, up_last):
                for half in range(2):
                    base = SLOTS[name] + half * 2 * DGROUPS
                    gb = half * DGROUPS

                    def group(i, g, first=False, last=False, gate=None):
                        ring = (gb + g) % 2
                        pe.wait_ge(hid_lo, i * 2 + (layer * 2 * DGROUPS + gb + g + 1))
                        for q in range(4):
                            n = 2 * (base + 2 * g) + q
                            pe.wait_ge(lo_ready, i * 8 + (n + 1))
                            b = 4 * ring + q
                            for nt in range(2):
                                if first and q == 0:
                                    pe.wait_ge(evac, CHUNKS[name] + 2 * half - 1 + nt)
                                for t in range(TB):
                                    split_matmul(psG[nt][:, t], hhi[:, b, t * P:(t + 1) * P],
                                                 hlo[:, b, t * P:(t + 1) * P], n % NP_, nt * N,
                                                 first and q == 0, last and q == 3, nt == 1 and t == TB - 1)
                            if gate:
                                broadcast(gate, q)

                    group(0, 0, first=True)
                    if half == 0:
                        up_last()
                        group(0, 1, gate=("gate1", "gate3")[layer])
                        group(0, 2)
                    with pe.Fori(1 - half, 4) as i:
                        group(i, 1)
                        group(i, 2)
                    group(4, 1)
                    group(4, 2, last=True)

            ffn_down("down0", 0, pairs("up0", 1, PAIRS_UP))

            def heads_out(name, n):
                pe.wait_ge(head_ready, n + (1 if name == "q" else QW // N + 1))
                for u in range(2):
                    transposes(lambda b, t: stage[:, 0, t, (2 * u + b) * P:(2 * u + b + 1) * P],
                               u, head_units(name, n))

            def heads(name):
                def one(n, par):
                    chunk(n + SLOTS[name] // 4, n + CHUNKS[name], par, {4: lambda: heads_out(name, n - 1)})

                one(1, 1)
                with pe.Fori(1, 3) as i:
                    for j in range(2):
                        one(i * 2 + j, j)

            norm_chunk(2, SLOTS["q"] // 4, CHUNKS["q"])
            heads("q")
            norm_chunk(3, SLOTS["k"] // 4, CHUNKS["k"], lambda: heads_out("q", QW // N - 1))
            heads("k")
            r0, c0 = SLOTS["v"] // 4, CHUNKS["v"]
            chunk(r0, c0, 0, {5: lambda: heads_out("k", QW // N - 1)})
            chunk(r0 + 1, c0 + 1, 1)
            with pe.Fori(1, 3) as i:
                for j in range(2):
                    chunk(i * 2 + (r0 + j), i * 2 + (c0 + j), j)

            def scores(j):
                h, qb = j // 2, j % 2
                nk = P * (1 + qb)
                if j >= 2:
                    pe.wait_ge(score_read, j - 1)
                else:
                    pe.wait_ge(evac, CHUNKS["wo"])
                flat = psG[j % 2][:].rearrange("p t n -> p (t n)")
                for g in range(NG):
                    n = g * HPG + h
                    ins = pe.matmul(flat[:, g * nk:(g + 1) * nk], qT[:, n, qb * P:(qb + 1) * P], kT[:, n, 0:nk],
                                    start=True, stop=True)
                ins.then_inc(score_done, 1)

            def prob_transposes(j):
                h, qb = j // 2, j % 2
                u0 = UNITS["attn"] + 3 * h + qb
                pe.wait_ge(prob_ready, j + 1)
                for u in range(1 + qb):
                    pe.wait_ge(tr_free, max(UNITS["attn"], u0 + u - 2))
                    k0, k1 = (0, 3) if qb == 0 else ((0, 4), (4, 6))[u]
                    for k in range(k0, k1):
                        ins = pe.transpose(psT[qb + u][:, (k - k0) * P:(k - k0 + 1) * P],
                                           prob[j % 3][:, k * P:(k + 1) * P], ident[:])
                    ins.then_inc(tr_done, 1)

            def outputs(j):
                h, qb = j // 2, j % 2
                pe.wait_ge(tr_free, UNITS["attn"] + ATTN_UNITS[j])
                if h >= 1 and qb == 0:
                    pe.wait_ge(o_read, h)
                nb = NG * (1 + qb)
                for k in range(nb):
                    g, kb = k // (1 + qb), k % (1 + qb)
                    n = g * HPG + h
                    ins = pe.matmul(psM[:, qb * P:(qb + 1) * P], vv[:, kb, n * DH:(n + 1) * DH],
                                    probT[j % 2][:, k], start=k == 0, stop=k == nb - 1)
                ins.then_inc(o_done, 1)

            pe.wait_ge(tr_free, UNITS["attn"])
            scores(0)
            scores(1)
            for j in range(2 * HPG):
                if j + 2 < 2 * HPG:
                    scores(j + 2)
                if j >= 1:
                    outputs(j - 1)
                prob_transposes(j)
            outputs(2 * HPG - 1)
            pe.wait_ge(o_read, HPG)
            for c in range(D // N):
                chunk(SLOTS["wo"] // 4 + c // 2, CHUNKS["wo"] + c, c % 2,
                      {q: lambda q=q: broadcast("gate2", q) for q in range(4)} if c == 0 else None,
                      r0=c % 2 * 2, slots=OW // P // 4)
            ffn_down("down1", 1, pairs("up1", 4, PAIRS_UP))


def _slots(w, order=None):
    k, n = w.shape
    t = w.reshape(k // (4 * P), 4, P, n // N, N).transpose(3, 0, 2, 1, 4)
    if order is not None:
        t = t[order]
    return t.reshape(-1, P, SLOT)


def _mod_slots(w):
    return w.reshape(2, MSLOT, w.shape[1] // (2 * P), 2, P).transpose(2, 0, 3, 4, 1).reshape(-1, P, MSLOT)


def _down_slots(w):
    return w.reshape(DFF // (2 * P), 2, P, 2, 2 * N).transpose(3, 0, 2, 1, 4).reshape(-1, P, SLOT)


def _pairs(n):
    return [c for i in range(n) for c in (i, n + i)]


def kernel(x, c, positions, mod_w, mod_b, norm_mix_g, norm_ffn_g, conv_pw1_w, conv_pw1_b, conv_dw_w, conv_dw_b,
           conv_ln_g, conv_ln_b, conv_pw2_w, conv_pw2_b, kv_mod_w, kv_mod_b, kv_norm_g, w_kv, k_norm_g, w_q,
           q_norm_g, w_o, ffn_up_w, ffn_dw_w, ffn_dw_b, ffn_down_w):
    import concourse.bacc as _bacc
    from concourse.bass_utils import run_bass_kernel_spmd as _run

    gate_first = [ch for i in range(PAIRS_PW1) for ch in (PAIRS_PW1 + i, i)]
    pw1 = _slots(conv_pw1_w[0], gate_first)
    side_by_side = [c * KS + k for k in range(KS) for c in range(2)]
    mods = np.concatenate([_mod_slots(mod_w[0]), _mod_slots(kv_mod_w), _mod_slots(mod_w[1])])
    quarters = [(w * STEPS + k) * MPC + u for k in range(STEPS) for w in range(2) for u in range(MPC)]
    wstream = np.concatenate([
        pw1[side_by_side], pw1[2 * KS:], _slots(conv_pw2_w[0]),
        _slots(ffn_up_w[0], _pairs(PAIRS_UP)), _down_slots(ffn_down_w[0]),
        _slots(w_q[0]), _slots(w_kv), _slots(w_o[0]),
        _slots(ffn_up_w[1], _pairs(PAIRS_UP)), _down_slots(ffn_down_w[1])])
    mstream = np.concatenate([mods[quarters], mods[len(quarters):]])
    rows = [c, mod_b[0], kv_mod_b, mod_b[1], norm_mix_g, norm_ffn_g, kv_norm_g, conv_pw1_b, conv_dw_b, conv_ln_g,
            conv_ln_b, conv_pw2_b, k_norm_g, q_norm_g, ffn_dw_w, ffn_dw_b, conv_dw_w]
    rows = np.concatenate([r.reshape(-1, P) for r in rows] + [np.zeros((NRB * P - NROWS, P), np.float32)])
    assert wstream.shape[0] == NSLOTS and mstream.shape[0] == 8 * NMODS

    nc = _bacc.Bacc("TRN2", target_bir_lowering=False, num_devices=1, dynamic_dma_scratch_size=1024)
    arrays = {"wstream": wstream, "mstream": mstream, "x_in": np.ascontiguousarray(x[0]), "rows_in": rows,
              "pos_in": np.ascontiguousarray(positions.reshape(TB, P).T)}
    args = [nc.dram_tensor(n, a.shape, mybir.dt.from_np(a.dtype), kind="ExternalInput").ap()
            for n, a in arrays.items()]
    out = nc.dram_tensor("out", (1, S, D), mybir.dt.float32, kind="ExternalOutput").ap()
    build(nc, *args, out[0])
    r = _run(nc, [arrays], core_ids=[0])
    return r.results[0]["out"]
```
